# Optimizing a Trainium2 kernel written in Bass

```python
import math
import jax, jax.numpy as jnp
from jax import lax
import numpy as np

D_MODEL = 1024
BATCH = 1
SEQ = 2048
DEPTH = 2
DEC_BATCH = 8
DEC_SEQ = 4
PAST_LEN = 16384
PAGE_SIZE = 128

N_EVEN = (DEPTH + 1) // 2
N_ODD = DEPTH // 2

RWKV_HEAD = 64
RWKV_W = D_MODEL // 2
RWKV_HEADS = RWKV_W // RWKV_HEAD
RWKV_W_LORA = 64
RWKV_A_LORA = 64
RWKV_PROJ = 3 * RWKV_W + RWKV_W_LORA + RWKV_A_LORA
RWKV_GN_EPS = 64e-5

GLA_VW = D_MODEL // 2
GLA_KW = GLA_VW // 2
GLA_HEADS = 4
GLA_DK = GLA_KW // GLA_HEADS
GLA_DV = GLA_VW // GLA_HEADS
GLA_LORA = 16
GLA_GATE_NORM = 16.0
GLA_CHUNK = 64
GLA_PROJ = 2 * GLA_KW + GLA_VW + GLA_LORA

EVEN_WIDTH = RWKV_W + GLA_VW
EVEN_PROJ = RWKV_PROJ + GLA_PROJ + EVEN_WIDTH

CONV_C = D_MODEL
CONV_W = 31
ODD_PROJ = 3 * CONV_C

RMS_EPS = 1e-6
LN_EPS = 1e-5

kernel_name = 'hybrid_rwkv7_gla_conformer_conv_step'

def rmsnorm(x, g):
    xf = x.astype(jnp.float32)
    y = xf * lax.rsqrt(jnp.mean(xf * xf, axis=-1, keepdims=True) + RMS_EPS) * g.astype(jnp.float32)
    return y.astype(x.dtype)

def layernorm(x, g, b):
    xf = x.astype(jnp.float32)
    mu = jnp.mean(xf, axis=-1, keepdims=True)
    var = jnp.mean(jnp.square(xf - mu), axis=-1, keepdims=True)
    y = (xf - mu) * lax.rsqrt(var + LN_EPS) * g.astype(jnp.float32) + b.astype(jnp.float32)
    return y.astype(x.dtype)

def _rwkv_step(S, inp):
    r, w, k, v, kk, a = inp
    sa = jnp.einsum('bhvk,bhk->bhv', S, -kk)
    S = S * w[:, :, None, :] + sa[..., None] * (kk * a)[:, :, None, :] + v[..., None] * k[:, :, None, :]
    return S, jnp.einsum('bhvk,bhk->bhv', S, r)

def rwkv7_mix(p, prev_row, s0, mu, w0, w_up, a0, a_up, k_k, k_a, r_k, ln_w, ln_b):
    B, L, _ = p.shape
    H, K = RWKV_HEADS, RWKV_HEAD
    f32 = jnp.float32
    p_prev = jnp.concatenate([prev_row[:, None, :].astype(p.dtype), p[:, :-1]], axis=1)
    xm = p + (p_prev - p) * mu
    o1, o2, o3, o4 = RWKV_W, 2 * RWKV_W, 3 * RWKV_W, 3 * RWKV_W + RWKV_W_LORA
    r, k, v, xw, xa = xm[..., :o1], xm[..., o1:o2], xm[..., o2:o3], xm[..., o3:o4], xm[..., o4:]
    w = -jax.nn.softplus(-(w0 + jnp.tanh(xw) @ w_up).astype(f32)) - 0.5
    decay = jnp.exp(-jnp.exp(w))
    a = jax.nn.sigmoid((a0 + xa @ a_up).astype(f32))
    heads = lambda t: t.astype(f32).reshape(B, L, H, K)
    r, k, v, decay, a = heads(r), heads(k), heads(v), heads(decay), heads(a)
    kk = k * k_k.astype(f32).reshape(H, K)
    kk = kk / jnp.maximum(jnp.sqrt(jnp.sum(kk * kk, axis=-1, keepdims=True)), 1e-12)
    k = k * (1.0 + (a - 1.0) * k_a.astype(f32).reshape(H, K))
    seq = lambda t: jnp.moveaxis(t, 1, 0)
    s_final, y = lax.scan(_rwkv_step, s0.astype(f32),
                          (seq(r), seq(decay), seq(k), seq(v), seq(kk), seq(a)))
    y = jnp.moveaxis(y, 0, 1)
    mean = jnp.mean(y, axis=-1, keepdims=True)
    var = jnp.mean(jnp.square(y - mean), axis=-1, keepdims=True)
    y = ((y - mean) * lax.rsqrt(var + RWKV_GN_EPS)).reshape(B, L, RWKV_W)
    y = y * ln_w.astype(f32) + ln_b.astype(f32)
    bonus = jnp.sum(r * k * r_k.astype(f32), axis=-1, keepdims=True) * v
    out = y + bonus.reshape(B, L, RWKV_W)
    return out.astype(p.dtype), p[:, -1], s_final.astype(s0.dtype)

def _gla_chunk_step(S, inp):
    d, kv = inp
    return d[..., None] * S + kv, S

def gla_mix(p, s0, g_up, g_b, g_norm):
    B, L, _ = p.shape
    H, DK, DV = GLA_HEADS, GLA_DK, GLA_DV
    f32 = jnp.float32
    q = p[..., :GLA_KW]
    k = p[..., GLA_KW:2 * GLA_KW]
    v = p[..., 2 * GLA_KW:2 * GLA_KW + GLA_VW]
    gd = p[..., 2 * GLA_KW + GLA_VW:]
    la = jax.nn.log_sigmoid((gd @ g_up + g_b).astype(f32)) / GLA_GATE_NORM
    C = math.gcd(L, GLA_CHUNK)
    NC = L // C
    chunks = lambda t, d: t.astype(f32).reshape(B, NC, C, H, d).transpose(0, 3, 1, 2, 4)
    q = chunks(q, DK) * (DK ** -0.5)
    k = chunks(k, DK)
    v = chunks(v, DV)
    b = jnp.cumsum(chunks(la, DK), axis=3)
    b_last = b[:, :, :, -1:, :]
    qg = q * jnp.exp(b)
    kg = k * jnp.exp(-b)
    mask = jnp.tril(jnp.ones((C, C), dtype=bool))
    att = jnp.where(mask, jnp.einsum('bhncd,bhnsd->bhncs', qg, kg), 0.0)
    o = jnp.einsum('bhncs,bhnsv->bhncv', att, v)
    kv = jnp.einsum('bhncd,bhncv->bhndv', k * jnp.exp(b_last - b), v)
    dec = jnp.exp(b_last[:, :, :, 0, :])
    s_final, s_before = lax.scan(_gla_chunk_step, s0.astype(f32),
                                 (jnp.moveaxis(dec, 2, 0), jnp.moveaxis(kv, 2, 0)))
    s_before = jnp.moveaxis(s_before, 0, 2)
    o = o + jnp.einsum('bhncd,bhndv->bhncv', qg, s_before)
    o = o * lax.rsqrt(jnp.mean(o * o, axis=-1, keepdims=True) + RMS_EPS) * g_norm.astype(f32)
    o = o.transpose(0, 2, 3, 1, 4).reshape(B, L, GLA_VW)
    return o.astype(p.dtype), s_final.astype(s0.dtype)

def even_layer(x, shift0, s_rwkv0, s_gla0, norm, w_in, mu, w0, w_up, a0, a_up, k_k, k_a, r_k,
               ln_w, ln_b, g_up, g_b, g_norm, w_out):
    h = rmsnorm(x, norm)
    p = h @ w_in
    p_rwkv = p[..., :RWKV_PROJ]
    p_gla = p[..., RWKV_PROJ:RWKV_PROJ + GLA_PROJ]
    gate = p[..., RWKV_PROJ + GLA_PROJ:]
    o_r, shift_new, s_r = rwkv7_mix(p_rwkv, shift0, s_rwkv0, mu, w0, w_up, a0, a_up, k_k, k_a, r_k, ln_w, ln_b)
    o_g, s_g = gla_mix(p_gla, s_gla0, g_up, g_b, g_norm)
    o = jnp.concatenate([o_r, o_g], axis=-1) * jax.nn.silu(gate)
    return x + o @ w_out, shift_new, s_r, s_g

def odd_layer(x, buf, norm, w_in, b_in, conv_w, conv_b, ln_w, ln_b, w_out):
    h = rmsnorm(x, norm)
    p = h @ w_in + b_in
    u = p[..., :CONV_C] * jax.nn.sigmoid(p[..., CONV_C:2 * CONV_C])
    g = p[..., 2 * CONV_C:]
    ext = jnp.concatenate([buf.astype(u.dtype), u], axis=1)
    y = lax.conv_general_dilated(ext, conv_w[:, None, :].astype(u.dtype), (1,), 'VALID',
                                 dimension_numbers=('NWC', 'WIO', 'NWC'),
                                 feature_group_count=CONV_C) + conv_b
    y = jax.nn.silu(layernorm(y, ln_w, ln_b)) * jax.nn.silu(g)
    return x + y @ w_out, ext[:, -(CONV_W - 1):]

def setup_inputs(seed: int = 0) -> dict:
    key = jax.random.key(seed)
    ks = iter(jax.random.split(key, 40))
    nrm = lambda shape, s: s * jax.random.normal(next(ks), shape, jnp.float32)
    E, O = N_EVEN, N_ODD
    return {
        'x_prompt': nrm((BATCH, SEQ, D_MODEL), 1.0),
        'x_sample': nrm((DEC_BATCH, DEC_SEQ, D_MODEL), 1.0),
        'state_rwkv_shift': nrm((E, DEC_BATCH, RWKV_PROJ), 1.0),
        'state_rwkv': nrm((E, DEC_BATCH, RWKV_HEADS, RWKV_HEAD, RWKV_HEAD), 0.3),
        'state_gla': nrm((E, DEC_BATCH, GLA_HEADS, GLA_DK, GLA_DV), 0.3),
        'cache_conv': nrm((O, DEC_BATCH, CONV_W - 1, CONV_C), 0.5),
        'norm_even': 1.0 + nrm((E, D_MODEL), 0.05),
        'w_in_even': nrm((E, D_MODEL, EVEN_PROJ), D_MODEL ** -0.5),
        'rwkv_mu': jax.random.uniform(next(ks), (E, RWKV_PROJ), jnp.float32),
        'rwkv_w0': nrm((E, RWKV_W), 0.5),
        'rwkv_w_up': nrm((E, RWKV_W_LORA, RWKV_W), RWKV_W_LORA ** -0.5),
        'rwkv_a0': nrm((E, RWKV_W), 0.1),
        'rwkv_a_up': nrm((E, RWKV_A_LORA, RWKV_W), RWKV_A_LORA ** -0.5),
        'rwkv_k_k': 0.85 + nrm((E, RWKV_W), 0.05),
        'rwkv_k_a': 1.0 + nrm((E, RWKV_W), 0.05),
        'rwkv_r_k': nrm((E, RWKV_HEADS, RWKV_HEAD), 0.1),
        'rwkv_ln_w': 1.0 + nrm((E, RWKV_W), 0.05),
        'rwkv_ln_b': nrm((E, RWKV_W), 0.02),
        'gla_g_up': nrm((E, GLA_LORA, GLA_KW), GLA_LORA ** -0.5),
        'gla_g_b': nrm((E, GLA_KW), 0.1),
        'gla_norm': 1.0 + nrm((E, GLA_DV), 0.05),
        'w_out_even': nrm((E, EVEN_WIDTH, D_MODEL), EVEN_WIDTH ** -0.5),
        'norm_odd': 1.0 + nrm((O, D_MODEL), 0.05),
        'w_in_odd': nrm((O, D_MODEL, ODD_PROJ), D_MODEL ** -0.5),
        'b_in_odd': nrm((O, ODD_PROJ), 0.02),
        'conv_w': nrm((O, CONV_W, CONV_C), CONV_W ** -0.5),
        'conv_b': nrm((O, CONV_C), 0.02),
        'conv_ln_w': 1.0 + nrm((O, CONV_C), 0.05),
        'conv_ln_b': nrm((O, CONV_C), 0.02),
        'w_out_odd': nrm((O, CONV_C, D_MODEL), CONV_C ** -0.5),
        'final_norm': 1.0 + nrm((D_MODEL,), 0.05),
    }

def reference(x_prompt, x_sample, state_rwkv_shift, state_rwkv, state_gla, cache_conv,
              norm_even, w_in_even, rwkv_mu, rwkv_w0, rwkv_w_up, rwkv_a0, rwkv_a_up, rwkv_k_k,
              rwkv_k_a, rwkv_r_k, rwkv_ln_w, rwkv_ln_b, gla_g_up, gla_g_b, gla_norm, w_out_even,
              norm_odd, w_in_odd, b_in_odd, conv_w, conv_b, conv_ln_w, conv_ln_b, w_out_odd,
              final_norm):
    dt = x_prompt.dtype
    bp = x_prompt.shape[0]
    shift_p0 = jnp.zeros((bp, RWKV_PROJ), dt)
    rwkv_p0 = jnp.zeros((bp, RWKV_HEADS, RWKV_HEAD, RWKV_HEAD), dt)
    gla_p0 = jnp.zeros((bp, GLA_HEADS, GLA_DK, GLA_DV), dt)
    conv_p0 = jnp.zeros((bp, CONV_W - 1, CONV_C), dt)
    xp, xs = x_prompt, x_sample
    sh_p, sh_s, sr_p, sr_s, sg_p, sg_s, cb_p, cb_s = [], [], [], [], [], [], [], []
    for layer in range(DEPTH):
        i = layer // 2
        if layer % 2 == 0:
            ew = (norm_even[i], w_in_even[i], rwkv_mu[i], rwkv_w0[i], rwkv_w_up[i], rwkv_a0[i],
                  rwkv_a_up[i], rwkv_k_k[i], rwkv_k_a[i], rwkv_r_k[i], rwkv_ln_w[i], rwkv_ln_b[i],
                  gla_g_up[i], gla_g_b[i], gla_norm[i], w_out_even[i])
            xp, a1, a2, a3 = even_layer(xp, shift_p0, rwkv_p0, gla_p0, *ew)
            xs, b1, b2, b3 = even_layer(xs, state_rwkv_shift[i], state_rwkv[i], state_gla[i], *ew)
            sh_p.append(a1); sr_p.append(a2); sg_p.append(a3)
            sh_s.append(b1); sr_s.append(b2); sg_s.append(b3)
        else:
            ow = (norm_odd[i], w_in_odd[i], b_in_odd[i], conv_w[i], conv_b[i], conv_ln_w[i],
                  conv_ln_b[i], w_out_odd[i])
            xp, c1 = odd_layer(xp, conv_p0, *ow)
            xs, c2 = odd_layer(xs, cache_conv[i], *ow)
            cb_p.append(c1); cb_s.append(c2)
    y_prompt = rmsnorm(xp, final_norm)
    y_sample = rmsnorm(xs, final_norm)
    return (y_prompt, y_sample,
            jnp.stack(sh_p), jnp.stack(sh_s),
            jnp.stack(sr_p), jnp.stack(sr_s),
            jnp.stack(sg_p), jnp.stack(sg_s),
            jnp.stack(cb_p), jnp.stack(cb_s))


_drawn_inputs = setup_inputs


def setup_inputs(seed=0):
    import zlib

    import numpy as np

    out = dict(_drawn_inputs(seed))
    spreads = {}
    factors = {'rwkv_k_k': 5.23,
     'rwkv_ln_w': 2.949,
     'rwkv_ln_b': 7.581,
     'gla_norm': 2.932,
     'conv_b': 4.74,
     'conv_ln_w': 3.469,
     'conv_ln_b': 8.0}
    for name, (base, spread) in spreads.items():
        noise = np.random.default_rng([zlib.crc32(name.encode()), seed]).standard_normal(out[name].shape)
        drawn = base * np.exp(spread * noise) if base else spread * noise
        out[name] = __import__('jax').numpy.asarray(drawn.astype(out[name].dtype))
    for name, factor in factors.items():
        out[name] = (out[name] * factor).astype(out[name].dtype)
    return out
```

```python
from contextlib import ExitStack
import math

import numpy as np
import concourse.bass as bass
from concourse import mybir

F32 = mybir.dt.float32
ACT = mybir.ActivationFunctionType
ALU = mybir.AluOpType

P = 128
D = 1024
KT = D // P
SEQ = 2048
SB, SL = 8, 4
NS = SB * SL
T = SEQ + NS
BLK = 512
NB = SEQ // BLK
C = 64
NC = BLK // C
RB = 416
NRB = T // RB
HK = 64
RU = 4
GU = 2
CT = KT
CW = 31
HALO = CW - 1
DECAY = math.exp(-0.5)
LN_UP = 30
GN_EPS, RMS_EPS, LN_EPS = 64e-5, 1e-6, 1e-5
RPROJ, GPROJ = 1664, 1040

_COLS = {}
_n = 0
for _name, _w in (("maskA", 128), ("maskAs", 128), ("lvl", 6 * 64), ("lvl1t", 64), ("ident", 128),
                  ("ident2", 64), ("bones", 128), ("ones", 128), ("reset", BLK), ("resets", NS),
                  ("seq", SB), ("maskG", 128), ("maskGs", 128), ("eps", 8)):
    _COLS[_name] = (_n, _n + _w)
    _n += _w
NCONST = _n
R_MUR, R_MUK, R_MUV, R_W0, R_A0, R_KK, R_KA, R_RK, R_LNW, R_LNB = range(10)
G_GB, G_NORM = range(2)
O_BV, O_BG, O_BS, O_CB = range(4)
E_RMS, E_GN, E_LN, E_UP, E_ONE = range(5)


def build(nc, A):
    ctx = ExitStack()
    with ctx:
        def sb(name, *shape):
            return ctx.enter_context(nc.sbuf_tensor(name, list(shape), F32))

        sems = []

        def sem(name):
            s = ctx.enter_context(nc.semaphore(name))
            sems.append(s)
            return s

        ps = [ctx.enter_context(nc.psum_tensor(f"bank{i}", [P, 512], F32)) for i in range(8)]
        PJ, EB, Q = ps[0:2], ps[2:4], ps[4:8]

        def rounds_end():
            nc.gpsimd.sem_clear(range(sems[0].num, sems[-1].num + 1))
            nc.all_engine_barrier()

        K0 = sb("K0", P, NCONST)
        ysum = sb("ysum", P, T)
        hctx = ctx.enter_context(ExitStack())
        H = hctx.enter_context(nc.sbuf_tensor("H", [P, KT, T], F32))

        def cst(name):
            a, b = _COLS[name]
            return K0[:, a:b]

        ident, ident2, bones, ones = cst("ident"), cst("ident2"), cst("bones"), cst("ones")
        eps = cst("eps")

        s_ssum = sem("square_sums_ready")
        s_proj = sem("projection_ready")
        s_lora = sem("lora_ready")
        s_ssq = sem("key_square_sums_ready")
        s_bon = sem("bonus_sums_ready")
        s_A = sem("chunk_products_ready")
        s_tr = sem("transposes_ready")
        s_wv = sem("value_part_ready")
        s_T = sem("inverse_left_ready")
        s_X = sem("inverse_right_ready")
        s_ZS = sem("state_read_ready")
        s_U = sem("removals_ready")
        s_SU = sem("state_change_ready")
        s_Y = sem("outputs_ready")
        s_mean = sem("mean_ready")
        s_var = sem("variance_ready")
        a_sq = sem("squares_done")
        a_ln = sem("log_done")
        a_rs = sem("rstd_done")
        a_ev = sem("projection_evacuated")
        a_halo = sem("halo_moved")
        a_mu = sem("previous_scaled")
        a_sig = sem("sigmoid_done")
        a_exp = sem("decay_exp_done")
        a_kn = sem("key_norm_done")
        a_ka = sem("key_gain_done")
        a_tb = sem("transposes_evacuated")
        a_wv = sem("value_part_evacuated")
        a_y = sem("outputs_evacuated")
        v_h = sem("normalised_done")
        v_mix = sem("mixed")
        v_cs = sem("log_decay_summed")
        v_cl = sem("key_sums_clamped")
        v_kn = sem("key_normalised")
        v_zr = sem("z_and_r_done")
        v_b = sem("b_done")
        v_bp = sem("bonus_product_done")
        v_bv = sem("bonus_done")
        v_M = sem("chunk_products_masked")
        v_x1 = sem("inverse_started")
        v_T = sem("inverse_left_masked")
        v_X = sem("inverse_grown")
        v_W0 = sem("state_read_done")
        v_U = sem("removals_done")
        v_S = sem("state_done")
        v_yc = sem("centred")
        v_o = sem("gated")
        p_set = sem("constants_set")
        p_kp = sem("key_scaled")
        p_ka = sem("key_rate_product_done")
        p_K = sem("k_done")
        p_V = sem("v_placed")
        p_e = sem("chunk_decay_kept")
        p_sh = sem("shift_row_kept")
        a_g = sem("gate_log_steps")
        a_gl = sem("sigmoid_gate_done")
        v_g = sem("gate_input_ready")
        p_u = sem("glu_done")
        p_ys = sem("channel_sum_done")
        v_acc = sem("taps_added")
        d_c = sem("constants_loaded")
        d_x = [sem("x_loaded0"), sem("x_loaded1")]
        d_w = sem("weights_loaded")
        d_p = sem("parameters_loaded")
        d_s = sem("states_loaded")
        d_o = sem("outputs_stored")
        d_o2 = sem("state_stored")
        d_r = sem("residual_loaded")
        d_g = sem("gate_loaded")
        d_sg = [sem("gate_stored0"), sem("gate_stored1")]

        def norm_stage():
            with nc.sbuf_tensor("xin", [P, KT, RB], F32) as xin, \
                    nc.sbuf_tensor("xsq", [P, KT, RB], F32) as xsq, \
                    nc.sbuf_tensor("rst", [P, RB], F32) as rst, \
                    nc.sbuf_tensor("gn", [P, KT], F32) as gn:
                with nc.Block() as block:
                    @block.sync
                    def _(sp):
                        sp.dma_start(K0[:], A["const"]).then_inc(d_c, 16)
                        sp.dma_start(gn[:], A["norm_even"]).then_inc(d_c, 16)
                        sp.wait_ge(d_c, 32)
                rounds_end()
                with nc.Fori(0, NRB) as b:
                    with nc.Block() as block:
                        @block.sync
                        def _(sp):
                            sp.dma_start(xin[:], A["xT"][:, :, bass.ds(b * RB, RB)]).then_inc(d_x[0], 16)

                        @block.scalar
                        def _(act):
                            act.wait_ge(d_x[0], 16)
                            nc.scalar.activation(xsq[:], xin[:], ACT.Square).then_inc(a_sq, 1)
                            act.wait_ge(s_ssum, 1)
                            nc.scalar.activation(rst[:], EB[0][:, 0:RB], ACT.Ln, scale=1.0 / D,
                                                 bias=eps[:, E_RMS:E_RMS + 1]).then_inc(a_ln, 1)
                            act.wait_ge(a_ln, 1)
                            nc.scalar.activation(rst[:], rst[:], ACT.Exp, scale=-0.5).then_inc(a_rs, 1)

                        @block.tensor
                        def _(pe):
                            pe.wait_ge(a_sq, 1)
                            for k in range(KT):
                                mm = nc.tensor.matmul(EB[0][:, 0:RB], ones, xsq[:, k, :],
                                                      start=(k == 0), stop=(k == KT - 1))
                            mm.then_inc(s_ssum, 1)

                        @block.vector
                        def _(dve):
                            dve.wait_ge(d_x[0], 16)
                            dve.wait_ge(a_rs, 1)
                            for k in range(KT):
                                nc.vector.scalar_tensor_tensor(
                                    H[:, k, bass.ds(b * RB, RB)], xin[:, k, :], gn[:, k:k + 1],
                                    rst[:], ALU.mult, ALU.mult)
                    rounds_end()

        def project(bank, w, t, cols, n, m=P):
            for k in range(KT):
                mm = nc.tensor.matmul(bank[0:m, 0:n], w[:, t, k * P:k * P + m], H[:, k, cols:cols + n],
                                      start=(k == 0), stop=(k == KT - 1))
            return mm

        COLS = [(b * BLK, BLK) for b in range(NB)] + [(SEQ, NS)]

        def rwkv_stage():
            c1 = ExitStack()
            with c1:
                def sb(name, *shape):
                    return c1.enter_context(nc.sbuf_tensor(name, list(shape), F32))

                W = sb("W", P, 4, D)
                LT = sb("LT", P, T)
                par = sb("rpar", P, 10)
                omm = sb("romm", P, 4)
                LU = sb("LU", P, P)
                raw = [sb(f"raw{i}", P, 1 + BLK) for i in range(3)]
                raws = [sb(f"raws{i}", P, SB, SL + 1) for i in range(3)]
                shr = sb("shr", P, 3, 1 + SB)
                shi = sb("shi", P, 3, SB)
                ZR = [sb(f"ZR{i}", P, NC, 2, C) for i in range(2)] + [sb("ZRs", P, 1, 2, C)]
                BK, BKs = sb("BK", P, NC, 2, C), sb("BKs", P, 1, 2, C)
                VS, VSs = sb("VS", P, NC, 2, C), sb("VSs", P, 1, 2, C)
                M = sb("M", P, 2, NC, P)
                BT = sb("BT", P, NC, P)
                UV = sb("UV", P, NC, 2, C)
                XX = sb("XX", P, 2, 2, 4, C)
                T1 = sb("T1", P, 2, 4, C)
                WV = sb("WV", P, NC, C)
                W0 = sb("W0t", P, C)
                S, Sd = sb("S", P, C), sb("Sd", P, C)
                Ss = sb("Ss", P, SB, C)
                PS = sb("PSs", P, SB, C)
                r, k, v = sb("r", P, BLK), sb("k", P, BLK), sb("v", P, BLK)
                t0, t1, t2 = sb("t0", P, BLK), sb("t1", P, BLK), sb("t2", P, BLK)
                sg, aa, cs = sb("sg", P, BLK), sb("aa", P, BLK), sb("cs", P, BLK)
                eb, enb, ebm = sb("eb", P, BLK), sb("enb", P, BLK), sb("ebm", P, BLK)
                kkn, kp = sb("kkn", P, BLK), sb("kp", P, BLK)
                bv = [sb(f"bv{i}", P, BLK) for i in range(3)]
                gs = [sb(f"gs{i}", P, BLK) for i in range(3)]
                ebC = [sb(f"ebC{i}", P, SB) for i in range(2)]
                ysb = [sb(f"ysb{i}", P, BLK) for i in range(2)]
                yc, rs = sb("yc", P, BLK), sb("rs", P, BLK)

                with nc.Block() as block:
                    LR = M[:, :, :, :].rearrange("p a b c -> p (a b c)")
                    muL, omL = t0[:, 0:1], t0[:, 1:2]
                    shl, stg = t1[:, 0:1 + SB], t1[:, 16:16 + SB]
                    rawL = raws[0]
                    tmp = [t2, sg]

                    @block.sync
                    def _(sp):
                        sp.dma_start(W[:, 0, :], A["w_even"][0]).then_inc(d_w, 16)
                        sp.dma_start(muL, A["mu_lora"]).then_inc(d_p, 16)
                        sp.dma_start(stg, A["shift_in"][12]).then_inc(d_p, 16)
                        sp.wait_ge(p_sh, 2)
                        sp.dma_start(A["shift_out"][12], shl).then_inc(d_o, 16)
                        sp.wait_ge(d_o, 16)

                    @block.gpsimd
                    def _(pool):
                        for z in [*ZR[2:], BKs, VSs, VS, S, BK]:
                            nc.gpsimd.memset(z[:], 0.0)
                        pool.wait_ge(d_p, 32)
                        nc.gpsimd.tensor_copy(rawL[:, :, 0:1].squeeze(2), stg).then_inc(p_set, 1)
                        pool.wait_ge(a_ev, NB + 1)
                        nc.gpsimd.tensor_copy(shl[:, 0:1], LR[:, SEQ - 1:SEQ]).then_inc(p_sh, 1)
                        pool.wait_ge(d_p, 32)
                        nc.gpsimd.tensor_copy(shl[:, 1:1 + SB], rawL[:, :, SL:SL + 1].squeeze(2)).then_inc(p_sh, 1)

                    @block.tensor
                    def _(pe):
                        pe.wait_ge(d_w, 16)
                        for b, (c0, n) in enumerate(COLS):
                            if b >= 2:
                                pe.wait_ge(a_ev, b - 1)
                            project(PJ[b % 2], W, 0, c0, n).then_inc(s_proj, 1)

                    @block.scalar
                    def _(act):
                        for b, (c0, n) in enumerate(COLS):
                            act.wait_ge(s_proj, b + 1)
                            if b < NB:
                                out, src = LR[:, c0:c0 + n], PJ[b % 2][:, 0:n]
                            else:
                                act.wait_ge(d_p, 32)
                                out = rawL[:, :, 1:1 + SL]
                                src = PJ[b % 2][:, 0:n].rearrange("p (s j) -> p s j", j=SL)
                            nc.scalar.activation(out, src, ACT.Copy).then_inc(a_ev, 1)
                        act.wait_ge(v_mix, 1 + 2 * (NB + 1))
                        nc.scalar.activation(LT[0:64, :], LT[0:64, :], ACT.Tanh)

                    @block.vector
                    def _(dve):
                        dve.wait_ge(d_p, 32)
                        nc.vector.tensor_scalar(omL, muL, -1.0, 1.0, ALU.mult, ALU.add).then_inc(v_mix, 1)
                        dve.wait_ge(v_mix, 1)
                        nc.vector.memset(t2[:, 0:1], 0.0).then_inc(v_x1, 1)
                        for b, (c0, n) in enumerate(COLS):
                            dve.wait_ge(a_ev, b + 1)
                            x = tmp[b % 2]
                            if b == NB:
                                dve.wait_ge(p_set, 1)
                            if b < NB:
                                a = 0 if b else 1
                                cur, prev = LR[:, c0:c0 + n], LR[:, c0 + a - 1:c0 + n - 1]
                                if b == 0:
                                    dve.wait_ge(v_x1, 1)
                                nc.vector.tensor_scalar(x[:, a:n], prev, muL, None, ALU.mult).then_inc(v_mix, 1)
                                out, x = LT[:, c0:c0 + n], x[:, 0:n]
                            else:
                                cur, prev = rawL[:, :, 1:1 + SL], rawL[:, :, 0:SL]
                                x = x[:, 0:n].rearrange("p (s j) -> p s j", j=SL)
                                nc.vector.tensor_scalar(x, prev, muL, None, ALU.mult).then_inc(v_mix, 1)
                                out = LT[:, c0:c0 + n].rearrange("p (s j) -> p s j", j=SL)
                            dve.wait_ge(v_mix, 2 + 2 * b)
                            nc.vector.scalar_tensor_tensor(out, cur, omL, x, ALU.mult, ALU.add).then_inc(v_mix, 1)
                rounds_end()
                with nc.Block() as block:
                    @block.sync
                    def _(sp):
                        sp.dma_start(W[:], A["w_even"][2:6].rearrange("t p n -> p t n")).then_inc(d_w, 16)
                        sp.wait_ge(d_w, 16)
                rounds_end()

                with nc.Fori(0, RU) as u:
                    for step in range(NB + 3):
                        rwkv_step(u, step, W, LT, par, omm, LU, raw, raws, shr, shi, ZR, (BK, BKs), (VS, VSs), M, BT,
                                  UV, XX, T1, WV, W0, S, Sd, Ss, PS, r, k, v, (t0, t1, t2), sg, aa, cs, eb, enb,
                                  ebm, kkn, kp, bv, gs, ebC, ysb, yc, rs)

        def rwkv_step(u, step, W, LT, par, omm, LU, raw, raws, shr, shi, ZRb, BKb, VSb, M, BT, UV, XX, T1, WV, W0, S,
                      Sd, Ss, PS, r, k, v, tmps, sg, aa, cs, eb, enb, ebm, kkn, kp, bv, gs, ebC, ysb, yc, rs):
            e = step if step <= NB else None
            c = step - 1 if 1 <= step <= NB + 1 else None
            g = step - 2 if step >= 2 else None
            t0, t1, t2 = tmps
            sample_e, sample_c = e == NB, c == NB
            if e is not None:
                c0, n = COLS[e]
                we, ne = min(C, n), max(1, n // C)
                ZRe, BKe, VSe = ZRb[2 if sample_e else e % 2], BKb[sample_e], VSb[sample_e]

                def ch(x, lo=0, hi=P):
                    return x[lo:hi, 0:n].rearrange("p (c j) -> p c j", j=we)
            if c is not None:
                ZR, BK, VS = ZRb[2 if sample_c else c % 2], BKb[sample_c], VSb[sample_c]
                nch = 1 if sample_c else NC
                grp = [range(0, 1)] if sample_c else [range(0, 4), range(4, 8)]
                G = len(grp)
                levels = 2 if sample_c else 6
                maskA = cst("maskAs" if sample_c else "maskA")
                nT = 2 if sample_c else 4
            halves = [(0, 64), (64, 128)]

            def evacuate(act, i):
                act.wait_ge(s_proj, i + 1)
                if i == 3:
                    nc.scalar.activation(gs[e % 3][:, 0:n], PJ[1][:, 0:n], ACT.Silu).then_inc(a_ev, 1)
                    return
                bank = PJ[i % 2]
                if sample_e:
                    nc.scalar.activation(raws[i][:, :, 1:1 + SL],
                                         bank[:, 0:n].rearrange("p (s j) -> p s j", j=SL), ACT.Copy).then_inc(a_ev, 1)
                    act.wait_ge(d_x[0], 48)
                    nc.scalar.activation(raws[i][:, :, 0:1].squeeze(2), shi[:, i, :], ACT.Copy).then_inc(a_halo, 1)
                    act.wait_ge(a_halo, i + 1)
                    prev, dst = raws[i][:, :, 0:SL], tmps[i][:, 0:n].rearrange("p (s j) -> p s j", j=SL)
                else:
                    if e:
                        nc.scalar.activation(raw[i][:, 0:1], raw[i][:, BLK:BLK + 1], ACT.Copy).then_inc(a_halo, 1)
                        act.wait_ge(a_halo, i + 1)
                    nc.scalar.activation(raw[i][:, 1:1 + n], bank[:, 0:n], ACT.Copy).then_inc(a_ev, 1)
                    prev, dst = raw[i][:, 0:n], tmps[i][:, 0:n]
                act.wait_ge(a_ev, i + 1)
                if step == 0:
                    act.wait_ge(d_p, 32)
                    act.wait_ge(p_set, 4)
                nc.scalar.activation(dst, prev, ACT.Copy, scale=par[:, i:i + 1]).then_inc(a_mu, 1)

            def mix(dve, i):
                dst = (r, k, v)[i]
                if sample_e:
                    cur = raws[i][:, :, 1:1 + SL]
                    out, x = (y_[:, 0:n].rearrange("p (s j) -> p s j", j=SL) for y_ in (dst, tmps[i]))
                else:
                    cur, out, x = raw[i][:, 1:1 + n], dst[:, 0:n], tmps[i][:, 0:n]
                dve.wait_ge(a_mu, i + 1)
                nc.vector.scalar_tensor_tensor(out, cur, omm[:, i:i + 1], x, ALU.mult, ALU.add).then_inc(v_mix, 1)

            def after_chunk(fn, j):
                if e is not None:
                    fn(j)

            with nc.Block() as block:
                @block.sync
                def _(sp):
                    if step == 0:
                        sp.dma_start(par[:], A["rwkv_par"][bass.ds(u, 1)].rearrange("u p n -> p (u n)")).then_inc(d_p, 16)
                        sp.dma_start(LU[:], A["lora_up"][:, bass.ds(u * P, P)]).then_inc(d_p, 16)
                    if step == NB:
                        sp.dma_start(Ss[:], A["rwkv_in"][bass.ds(u, 1)].rearrange("u p (s v) -> p (u s) v", v=C)).then_inc(d_s, 16)
                    if sample_e:
                        for i in range(3):
                            sp.dma_start(shi[:, i, :], A["shift_in"][bass.ds(u * 3 + i, 1)].rearrange("t p s -> p (t s)")).then_inc(d_x[0], 16)
                        sp.wait_ge(p_sh, 6)
                        for i in range(3):
                            sp.dma_start(A["shift_out"][bass.ds(u * 3 + i, 1)].rearrange("t p s -> p (t s)"),
                                         shr[:, i, :]).then_inc(d_o2, 16)
                        sp.wait_ge(d_s, 16)
                    if step == NB + 1:
                        sp.dma_start(W[:], A["w_even"][bass.ds(u * 4 + 6, 4)].rearrange("t p n -> p t n")).then_inc(d_w, 16)
                        sp.dma_start(A["rwkv_p_out"][bass.ds(u, 1)].rearrange("u p v -> p (u v)"), S[:]).then_inc(d_o2, 16)
                        sp.wait_ge(v_S, 2)
                        sp.dma_start(A["rwkv_s_out"][bass.ds(u, 1)].rearrange("u p (s v) -> p (u s) v", v=C),
                                     Ss[:]).then_inc(d_o2, 16)
                        sp.wait_ge(d_w, 16)
                        sp.wait_ge(d_o2, 32)
                    if g is not None:
                        gc0, gn_ = COLS[g]
                        sp.wait_ge(v_o, 3)
                        sp.dma_start(A["O"][bass.ds(u, 1), :, gc0:gc0 + gn_].rearrange("u p n -> p (u n)"),
                                     rs[:, 0:gn_]).then_inc(d_o, 16)
                        sp.wait_ge(d_o, 16)
                    if sample_e:
                        sp.wait_ge(d_o2, 48)

                @block.tensor
                def _(pe):
                    if g is not None:
                        _, m = COLS[g]
                        nc.tensor.matmul(EB[0][:, 0:m], bones, ysb[g % 2][:, 0:m], start=True, stop=True).then_inc(s_mean, 1)
                    if c is not None:
                        for gi, chunks in enumerate(grp):
                            for h, (lo, hi) in enumerate(halves):
                                for i, q in enumerate(chunks):
                                    mm = nc.tensor.matmul(Q[2 * gi + h][:, i * P:(i + 1) * P], BK[lo:hi, q, :, :],
                                                          ZR[lo:hi, q, :, :], start=True, stop=True)
                                mm.then_inc(s_A, 1)
                    if e is not None:
                        project(PJ[0], W, 0, c0, n).then_inc(s_proj, 1)
                    if c is not None:
                        for t, (src, bank) in enumerate([(BK, Q[0]), (BK, Q[1]), (VS, Q[2]), (VS, Q[3])]
                                                        if not sample_c else [(BK, Q[0]), (VS, Q[2])]):
                            if t == 0:
                                pe.wait_ge(v_M, 2 * G)
                            for i, q in enumerate(grp[t % G]):
                                mm = nc.tensor.transpose(bank[:, i * P:(i + 1) * P], src[:, q, :, :], ident)
                            mm.then_inc(s_tr, 1)
                    if g is not None:
                        pe.wait_ge(a_sq, 1)
                        nc.tensor.matmul(EB[1][:, 0:m], bones, yc[:, 0:m], start=True, stop=True).then_inc(s_var, 1)
                    if e is not None:
                        project(PJ[1], W, 1, c0, n).then_inc(s_proj, 1)
                        pe.wait_ge(a_ev, 1)
                    if c is not None:
                        pe.wait_ge(a_tb, nT)
                        for gi, chunks in enumerate(grp):
                            for i, q in enumerate(chunks):
                                for h, (lo, hi) in enumerate(halves):
                                    mm = nc.tensor.matmul(Q[gi][lo:hi, i * C:(i + 1) * C], M[lo:hi, h, q, 0:C],
                                                          ident2[lo:hi, :], start=True, stop=True)
                            mm.then_inc(s_T, 1)
                        for q in range(nch):
                            for h, (lo, hi) in enumerate(halves):
                                ko, ki = halves[1 - h]
                                mm = nc.tensor.matmul(Q[3][lo:hi, q * C:(q + 1) * C], M[ko:ki, h, q, 0:C],
                                                      UV[ko:ki, q, h, :], start=True, stop=True)
                        mm.then_inc(s_wv, 1)
                    if e is not None:
                        project(PJ[0], W, 2, c0, n).then_inc(s_proj, 1)
                        pe.wait_ge(a_ev, 2)
                    if c is not None:
                        pe.wait_ge(a_wv, 1)
                        for l in range(2, levels + 1):
                            for gi, chunks in enumerate(grp):
                                pe.wait_ge(v_X, G * (l - 2) + gi + 1)
                                for i, q in enumerate(chunks):
                                    for h, (lo, hi) in enumerate(halves):
                                        mm = nc.tensor.matmul(Q[gi][lo:hi, i * C:(i + 1) * C], M[lo:hi, h, q, 0:C],
                                                              XX[lo:hi, gi, 0, i, :], start=True, stop=True)
                                mm.then_inc(s_T, 1)
                            if e is not None and l == 4:
                                project(PJ[1], W, 3, c0, n).then_inc(s_proj, 1)
                            for gi, chunks in enumerate(grp):
                                pe.wait_ge(v_T, G * (l - 2) + gi + 1)
                                for i, q in enumerate(chunks):
                                    for h, (lo, hi) in enumerate(halves):
                                        if l < levels:
                                            nc.tensor.matmul(Q[2 + gi][lo:hi, i * C:(i + 1) * C], XX[lo:hi, gi, 1, i, :],
                                                             T1[lo:hi, gi, i, :], start=True, stop=True)
                                        mm = nc.tensor.matmul(Q[2 + gi][lo:hi, (4 + i) * C:(5 + i) * C], T1[lo:hi, gi, i, :],
                                                              XX[lo:hi, gi, 1, i, :], start=True, stop=True)
                                mm.then_inc(s_X, 1)
                    if e is not None:
                        if c is None:
                            project(PJ[1], W, 3, c0, n).then_inc(s_proj, 1)
                        if step == 0:
                            pe.wait_ge(d_p, 32)
                        if g is not None:
                            pe.wait_ge(v_yc, 1)
                            pe.wait_ge(a_ln, 1)
                        nc.tensor.matmul(EB[0][:, 0:n], LU[0:64, :], LT[0:64, c0:c0 + n], start=True, stop=True).then_inc(s_lora, 1)
                        nc.tensor.matmul(EB[1][:, 0:n], LU[64:128, :], LT[64:128, c0:c0 + n], start=True, stop=True).then_inc(s_lora, 1)

                    def own(j):
                        if j == 0:
                            pe.wait_ge(a_kn, 1)
                            pe.wait_ge(a_sig, 1)
                            nc.tensor.matmul(EB[0][:, 0:n], bones, t0[:, 0:n], start=True, stop=True).then_inc(s_ssq, 1)
                        if j == 6:
                            pe.wait_ge(v_bp, 1)
                            pe.wait_ge(a_sig, 2)
                            nc.tensor.matmul(EB[1][:, 0:n], bones, t2[:, 0:n], start=True, stop=True).then_inc(s_bon, 1)

                    if c is not None and not sample_c:
                        pe.wait_ge(v_X, G * levels)
                        for j in range(NC):
                            if j:
                                pe.wait_ge(v_S, j)
                            for h, (lo, hi) in enumerate(halves):
                                mm = nc.tensor.matmul(Q[0][lo:hi, 0:C], ZR[lo:hi, j, 0, :], S[lo:hi, :], start=True, stop=True)
                            mm.then_inc(s_ZS, 1)
                            pe.wait_ge(v_W0, j + 1)
                            for h, (lo, hi) in enumerate(halves):
                                mm = nc.tensor.matmul(Q[0][lo:hi, C:2 * C], XX[lo:hi, j // 4, 1, j % 4, :], W0[lo:hi, :],
                                                      start=True, stop=True)
                            mm.then_inc(s_U, 1)
                            for h, (lo, hi) in enumerate(halves):
                                nc.tensor.matmul(Q[1][lo:hi, j * C:(j + 1) * C], S[lo:hi, :], ZR[lo:hi, j, 1, :],
                                                 start=True, stop=False)
                            pe.wait_ge(v_U, 2 * (j + 1))
                            for h, (lo, hi) in enumerate(halves):
                                mm = nc.tensor.matmul(Q[0][lo:hi, 2 * C:3 * C], BT[:, j, lo:hi], UV[:, j, h, :],
                                                      start=True, stop=True)
                            mm.then_inc(s_SU, 1)
                            for h, (lo, hi) in enumerate(halves):
                                mm = nc.tensor.matmul(Q[1][lo:hi, j * C:(j + 1) * C], UV[:, j, h, :], M[:, h, j, C:2 * C],
                                                      start=False, stop=True)
                            if j == NC - 1:
                                mm.then_inc(s_Y, 1)
                            after_chunk(own, j)
                    elif sample_c:
                        pe.wait_ge(v_X, G * levels)
                        for h, (lo, hi) in enumerate(halves):
                            mm = nc.tensor.matmul(Q[0][lo:hi, :], ZR[lo:hi, 0, 0, :], Ss[lo:hi, :, :], start=True, stop=True)
                        mm.then_inc(s_ZS, 1)
                        pe.wait_ge(v_W0, 3)
                        for h, (lo, hi) in enumerate(halves):
                            mm = nc.tensor.matmul(Q[0][lo:hi, 0:C], XX[lo:hi, 0, 1, 0, :], W0[lo:hi, :], start=True, stop=True)
                        mm.then_inc(s_U, 1)
                        for q in range(SB):
                            for h, (lo, hi) in enumerate(halves):
                                nc.tensor.matmul(Q[1][lo:hi, q * SL:(q + 1) * SL], Ss[lo:hi, q, :],
                                                 ZR[lo:hi, 0, 1, q * SL:(q + 1) * SL], start=(q == 0), stop=False,
                                                 skip_group_check=True)
                        pe.wait_ge(v_U, 2)
                        for h, (lo, hi) in enumerate(halves):
                            mm = nc.tensor.matmul(Q[1][lo:hi, 0:NS], UV[:, 0, h, :], M[:, h, 0, C:C + NS], start=False,
                                                  stop=True, skip_group_check=True)
                        mm.then_inc(s_Y, 1)
                        pe.wait_ge(v_b, 2)
                        for h, (lo, hi) in enumerate(halves):
                            mm = nc.tensor.matmul(Q[2][lo:hi, :], BT[:, 0, lo:hi], (eb, enb)[h][:, :], start=True, stop=True)
                        mm.then_inc(s_SU, 1)
                    else:
                        for j in range(NC):
                            after_chunk(own, j)

                @block.scalar
                def _(act):
                    if g is not None:
                        _, m = COLS[g]
                    if c is not None:
                        for t in range(nT):
                            bank = Q[t] if not sample_c else Q[2 * t]
                            dst = (BT if t < G else UV)
                            wide = len(grp[0]) * P
                            act.wait_ge(s_tr, t + 1)
                            q0 = grp[t % G][0]
                            if t < G:
                                out = BT[:, q0:q0 + len(grp[0]), :]
                                src = bank[:, 0:wide].rearrange("p (c j) -> p c j", j=P)
                            else:
                                out = UV[:, q0:q0 + len(grp[0]), :, :]
                                src = bank[:, 0:wide].rearrange("p (c h j) -> p c h j", h=2, j=C)
                            nc.scalar.activation(out, src, ACT.Copy).then_inc(a_tb, 1)
                    if e is not None:
                        evacuate(act, 0)
                    if g is not None:
                        act.wait_ge(v_yc, 1)
                        nc.scalar.activation(yc[:, 0:m], ysb[g % 2][:, 0:m], ACT.Square).then_inc(a_sq, 1)
                    if e is not None:
                        evacuate(act, 1)
                    if c is not None:
                        act.wait_ge(s_wv, 1)
                        nc.scalar.activation(WV[:, 0:nch, :], Q[3][:, 0:nch * C].rearrange("p (c j) -> p c j", j=C),
                                             ACT.Copy).then_inc(a_wv, 1)
                    if g is not None:
                        act.wait_ge(s_var, 1)
                        nc.scalar.activation(rs[:, 0:m], EB[1][:, 0:m], ACT.Ln, scale=1.0 / HK,
                                             bias=eps[:, E_GN:E_GN + 1]).then_inc(a_ln, 1)
                        act.wait_ge(a_ln, 1)
                        nc.scalar.activation(rs[:, 0:m], rs[:, 0:m], ACT.Exp, scale=-0.5).then_inc(a_rs, 1)
                    if e is not None:
                        evacuate(act, 2)
                        act.wait_ge(v_mix, 3 + (step == 0))
                        nc.scalar.activation(t0[:, 0:n], k[:, 0:n], ACT.Square, scale=par[:, R_KK:R_KK + 1]).then_inc(a_kn, 1)
                        evacuate(act, 3)
                        for i, (dst, col) in enumerate([(sg, R_W0), (aa, R_A0)]):
                            act.wait_ge(s_lora, i + 1)
                            nc.scalar.activation(dst[:, 0:n], EB[i][:, 0:n], ACT.Sigmoid,
                                                 bias=par[:, col:col + 1]).then_inc(a_sig, 1)
                        act.wait_ge(a_sig, 2)
                        act.wait_ge(v_cl, 1)
                        act.wait_ge(v_mix, 3 + (step == 0))
                        nc.scalar.activation(t0[:, 0:n], aa[:, 0:n], ACT.Identity, scale=par[:, R_KA:R_KA + 1],
                                             bias=omm[:, 3:4]).then_inc(a_ka, 1)
                        act.wait_ge(v_cs, 1)
                        nc.scalar.activation(eb[:, 0:n], cs[:, 0:n], ACT.Exp, scale=-DECAY).then_inc(a_exp, 1)
                        nc.scalar.activation(enb[:, 0:n], cs[:, 0:n], ACT.Exp, scale=DECAY).then_inc(a_exp, 1)
                        act.wait_ge(v_cs, 2)
                        nc.scalar.activation(ebm[:, 0:n], sg[:, 0:n], ACT.Exp, scale=-DECAY).then_inc(a_exp, 1)
                        nc.scalar.activation(t1[:, 0:n], t1[:, 0:n], ACT.Ln, scale=2.0 ** LN_UP).then_inc(a_kn, 1)
                        act.wait_ge(a_kn, 2)
                        nc.scalar.activation(t1[:, 0:n], t1[:, 0:n], ACT.Exp, scale=-0.5,
                                             bias=eps[:, E_UP:E_UP + 1]).then_inc(a_kn, 1)
                    if c is not None:
                        cn = COLS[c][1]
                        act.wait_ge(s_Y, 1)
                        nc.scalar.activation(ysb[c % 2][:, 0:cn], Q[1][:, 0:cn], ACT.Copy).then_inc(a_y, 1)

                @block.vector
                def _(dve):
                    if step == 0:
                        dve.wait_ge(d_p, 32)
                        nc.vector.tensor_scalar(omm[:, 0:3], par[:, 0:3], -1.0, 1.0, ALU.mult, ALU.add)
                        nc.vector.tensor_scalar(omm[:, 3:4], par[:, R_KA:R_KA + 1], -1.0, 1.0, ALU.mult,
                                                ALU.add).then_inc(v_mix, 1)
                        dve.wait_ge(v_mix, 1)
                    if g is not None:
                        _, m = COLS[g]
                        y = ysb[g % 2][:, 0:m]
                        dve.wait_ge(s_mean, 1)
                        nc.vector.scalar_tensor_tensor(y, EB[0][:, 0:m], -1.0 / HK, y, ALU.mult, ALU.add).then_inc(v_yc, 1)
                    if c is not None:
                        for i in range(2 * G):
                            h, chunks = i % 2, grp[i // 2]
                            L = len(chunks)
                            dve.wait_ge(s_A, i + 1)
                            nc.vector.tensor_tensor(M[:, h, chunks[0]:chunks[0] + L, :],
                                                    Q[i][:, 0:L * P].rearrange("p (c j) -> p c j", j=P),
                                                    maskA.unsqueeze(1).to_broadcast([P, L, P]), ALU.mult).then_inc(v_M, 1)
                        dve.wait_ge(v_M, 2 * G)
                        lvl = cst("lvl")
                        for gi, chunks in enumerate(grp):
                            L, q0 = len(chunks), chunks[0]
                            for h, (lo, hi) in enumerate(halves):
                                nc.vector.tensor_tensor(XX[lo:hi, gi, 1, 0:L, :], M[lo:hi, h, q0:q0 + L, 0:C],
                                                        cst("lvl1t")[lo:hi, :].unsqueeze(1).to_broadcast([C, L, C]),
                                                        ALU.mult).then_inc(v_x1, 1)
                            dve.wait_ge(s_T, gi + 1)
                            nc.vector.tensor_tensor(XX[:, gi, 0, 0:L, :], Q[gi][:, 0:L * C].rearrange("p (c j) -> p c j", j=C),
                                                    lvl[:, 0:C].unsqueeze(1).to_broadcast([P, L, C]),
                                                    ALU.mult).then_inc(v_x1, 1)
                            dve.wait_ge(v_x1, 3 * gi + 3)
                            nc.vector.tensor_tensor(XX[:, gi, :, 0:L, :], XX[:, gi, :, 0:L, :],
                                                    ident2.unsqueeze(1).unsqueeze(1).to_broadcast([P, 2, L, C]),
                                                    ALU.add).then_inc(v_X, 1)

                    if c is not None:
                        for l in range(2, levels + 1):
                            for gi, chunks in enumerate(grp):
                                L = len(chunks)
                                dve.wait_ge(s_T, G * (l - 1) + gi + 1)
                                nc.vector.tensor_tensor(T1[:, gi, 0:L, :], Q[gi][:, 0:L * C].rearrange("p (c j) -> p c j", j=C),
                                                        lvl[:, (l - 1) * C:l * C].unsqueeze(1).to_broadcast([P, L, C]),
                                                        ALU.mult).then_inc(v_T, 1)
                            if e is not None and l in (2, 3):
                                mix(dve, l - 2)
                            for gi, chunks in enumerate(grp):
                                L = len(chunks)
                                x0 = 0 if l < levels else 1
                                dve.wait_ge(s_X, G * (l - 2) + gi + 1)
                                pq = Q[2 + gi].rearrange("p (x c j) -> p x c j", x=2, j=C)[:, x0:2, 0:L, :]
                                nc.vector.tensor_tensor(XX[:, gi, x0:2, 0:L, :], pq, XX[:, gi, x0:2, 0:L, :],
                                                        ALU.add).then_inc(v_X, 1)
                    if e is not None:
                        for i in range(0 if c is None else min(2, levels - 1), 3):
                            mix(dve, i)
                    if g is not None:
                        y = ysb[g % 2][:, 0:m]
                        dve.wait_ge(a_rs, 1)
                        nc.vector.tensor_tensor(y, y, rs[:, 0:m], ALU.mult).then_inc(v_o, 1)
                        dve.wait_ge(v_o, 1)
                        nc.vector.scalar_tensor_tensor(y, y, par[:, R_LNW:R_LNW + 1], bv[g % 3][:, 0:m], ALU.mult,
                                                       ALU.add).then_inc(v_o, 1)
                        dve.wait_ge(v_o, 2)
                        nc.vector.scalar_tensor_tensor(rs[:, 0:m], y, par[:, R_LNB:R_LNB + 1], gs[g % 3][:, 0:m], ALU.add,
                                                       ALU.mult).then_inc(v_o, 1)

                    def own(j):
                        if j == 0:
                            dve.wait_ge(a_sig, 1)
                            rm = cst("resets" if sample_e else "reset")
                            nc.vector.tensor_tensor_scan(cs[:, 0:n], rm, sg[:, 0:n], 0.0, ALU.mult, ALU.add).then_inc(v_cs, 1)
                            dve.wait_ge(v_cs, 1)
                            nc.vector.tensor_tensor(sg[:, 0:n], cs[:, 0:n], sg[:, 0:n], ALU.subtract).then_inc(v_cs, 1)
                        if j == 1:
                            dve.wait_ge(s_ssq, 1)
                            nc.vector.tensor_scalar(t1[:, 0:n], EB[0][:, 0:n], 1e-24, None, ALU.max).then_inc(v_cl, 1)
                        if j == 3:
                            dve.wait_ge(a_kn, 3)
                            nc.vector.scalar_tensor_tensor(kkn[:, 0:n], k[:, 0:n], par[:, R_KK:R_KK + 1], t1[:, 0:n],
                                                           ALU.mult, ALU.mult).then_inc(v_kn, 1)
                            dve.wait_ge(v_kn, 1)
                        if j == 4:
                            dve.wait_ge(a_exp, 3)
                            nc.vector.tensor_tensor(ZRe[:, 0:ne, 0, 0:we], ch(kkn), ch(ebm), ALU.mult).then_inc(v_zr, 1)
                            nc.vector.tensor_tensor(ZRe[:, 0:ne, 1, 0:we], ch(r), ch(eb), ALU.mult).then_inc(v_zr, 1)
                        if j == 5:
                            dve.wait_ge(p_kp, 1)
                            dve.wait_ge(v_cl, 1)
                            nc.vector.scalar_tensor_tensor(t2[:, 0:n], r[:, 0:n], par[:, R_RK:R_RK + 1], kp[:, 0:n],
                                                           ALU.mult, ALU.mult).then_inc(v_bp, 1)
                            if c is not None and not sample_e:
                                dve.wait_ge(s_tr, nT)
                            dve.wait_ge(p_ka, 1)
                            for h, (lo, hi) in enumerate(halves):
                                nc.vector.scalar_tensor_tensor(BKe[lo:hi, 0:ne, h, 0:we], ch(aa, lo, hi), -1.0,
                                                               ch(enb, lo, hi), ALU.mult, ALU.mult).then_inc(v_b, 1)
                        if j == 7:
                            dve.wait_ge(s_bon, 1)
                            nc.vector.tensor_tensor(bv[e % 3][:, 0:n], EB[1][:, 0:n], v[:, 0:n], ALU.mult).then_inc(v_bv, 1)

                    if c is not None and not sample_c:
                        dve.wait_ge(a_wv, 1)
                        ec = ebC[c % 2]
                        for j in range(NC):
                            dve.wait_ge(s_ZS, j + 1)
                            nc.vector.tensor_tensor(W0[:], Q[0][:, 0:C], WV[:, j, :], ALU.add).then_inc(v_W0, 1)
                            if j:
                                dve.wait_ge(v_S, j)
                            nc.vector.tensor_scalar(Sd[:], S[:], ec[:, j:j + 1], None, ALU.mult).then_inc(v_x1, 1)
                            dve.wait_ge(s_U, j + 1)
                            for h, (lo, hi) in enumerate(halves):
                                nc.vector.tensor_copy(UV[lo:hi, j, h, :], Q[0][lo:hi, C:2 * C]).then_inc(v_U, 1)
                            dve.wait_ge(s_SU, j + 1)
                            dve.wait_ge(v_x1, 3 * G + j + 1)
                            nc.vector.scalar_tensor_tensor(S[:], Q[0][:, 2 * C:3 * C], ec[:, j:j + 1], Sd[:], ALU.mult,
                                                           ALU.add).then_inc(v_S, 1)
                            after_chunk(own, j)
                    elif sample_c:
                        seq = cst("seq")
                        dve.wait_ge(s_ZS, 1)
                        nc.vector.tensor_tensor(PS[:], Q[0].rearrange("p (s v) -> p s v", v=C),
                                                seq.unsqueeze(2).to_broadcast([P, SB, C]), ALU.mult).then_inc(v_W0, 1)
                        dve.wait_ge(v_W0, 1)
                        nc.vector.tensor_reduce(W0[:], PS[:].rearrange("p s v -> p v s"), mybir.AxisListType.X,
                                                ALU.add).then_inc(v_W0, 1)
                        dve.wait_ge(v_W0, 2)
                        dve.wait_ge(a_wv, 1)
                        nc.vector.tensor_tensor(W0[:], W0[:], WV[:, 0, :], ALU.add).then_inc(v_W0, 1)
                        dve.wait_ge(s_U, 1)
                        for h, (lo, hi) in enumerate(halves):
                            nc.vector.tensor_copy(UV[lo:hi, 0, h, :], Q[0][lo:hi, 0:C]).then_inc(v_U, 1)
                        dve.wait_ge(v_U, 2)
                        for h in range(2):
                            nc.vector.tensor_tensor((eb, enb)[h][:, :].rearrange("p (s v) -> p s v", v=C),
                                                    UV[:, 0, h, :].unsqueeze(1).to_broadcast([P, SB, C]),
                                                    seq.unsqueeze(2).to_broadcast([P, SB, C]), ALU.mult).then_inc(v_b, 1)
                        dve.wait_ge(s_SU, 1)
                        nc.vector.tensor_tensor(Ss[:], Q[2].rearrange("p (s v) -> p s v", v=C), Ss[:], ALU.add).then_inc(v_S, 1)
                        dve.wait_ge(v_S, 1)
                        nc.vector.tensor_tensor(Ss[:], Ss[:], ebC[0][:, :].unsqueeze(2).to_broadcast([P, SB, C]),
                                                ALU.mult).then_inc(v_S, 1)
                    else:
                        for j in range(NC):
                            after_chunk(own, j)

                @block.gpsimd
                def _(pool):
                    if step == 0:
                        for i in range(3):
                            nc.gpsimd.memset(raw[i][:, 0:1], 0.0).then_inc(p_set, 1)
                        nc.gpsimd.memset(S[:], 0.0).then_inc(p_set, 1)
                    if e is None:
                        return
                    pool.wait_ge(v_mix, 3 + (step == 0))
                    if c is not None and not sample_e:
                        pool.wait_ge(s_tr, nT)
                    for h, (lo, hi) in enumerate(halves):
                        nc.gpsimd.tensor_copy(VSe[lo:hi, 0:ne, 1 - h, 0:we], ch(v, lo, hi)).then_inc(p_V, 1)
                        pool.wait_ge(p_V, h + 1)
                    if e == NB - 1 or sample_e:
                        for i in range(3):
                            if not sample_e:
                                nc.gpsimd.tensor_copy(shr[:, i, 0:1], raw[i][:, BLK:BLK + 1]).then_inc(p_sh, 1)
                            else:
                                nc.gpsimd.tensor_copy(shr[:, i, 1:1 + SB], raws[i][:, :, SL:SL + 1].squeeze(2)).then_inc(p_sh, 2)
                    pool.wait_ge(a_exp, 2)
                    last = eb[:, 0:n].rearrange("p (s j) -> p s j", j=SL if sample_e else C)[:, :, -1:].squeeze(2)
                    nc.gpsimd.tensor_copy(ebC[e % 2][:, :], last).then_inc(p_e, 1)
                    pool.wait_ge(a_ka, 1)
                    nc.gpsimd.tensor_tensor(kp[:, 0:n], k[:, 0:n], t0[:, 0:n], ALU.mult).then_inc(p_kp, 1)
                    pool.wait_ge(p_kp, 1)
                    for h, (lo, hi) in enumerate(halves):
                        nc.gpsimd.tensor_tensor(BKe[lo:hi, 0:ne, 1 - h, 0:we], ch(kp, lo, hi), ch(enb, lo, hi),
                                                ALU.mult).then_inc(p_K, 1)
                        pool.wait_ge(p_K, h + 1)
                    pool.wait_ge(v_kn, 1)
                    nc.gpsimd.tensor_tensor(aa[:, 0:n], kkn[:, 0:n], aa[:, 0:n], ALU.mult).then_inc(p_ka, 1)
            rounds_end()

        def gla_stage():
            c1 = ExitStack()
            with c1:
                def sb(name, *shape):
                    return c1.enter_context(nc.sbuf_tensor(name, list(shape), F32))

                B = {
                    "W": sb("gW", P, 6, D), "GD": sb("GD", 16, T), "par": sb("gpar", P, 2), "GL": sb("GL", 16, P),
                    "q": sb("gq", P, BLK), "k": sb("gk", P, BLK),
                    "QG": [sb(f"QG{i}", P, BLK) for i in range(2)] + [sb("QGs", P, P)],
                    "KG": [sb(f"KG{i}", P, BLK) for i in range(2)] + [sb("KGs", P, P)],
                    "V": [[sb(f"V{i}{h}", P, BLK) for h in range(2)] for i in range(2)] + [[sb(f"Vs{h}", P, P) for h in range(2)]],
                    "gs": [[sb(f"gg{i}{h}", P, BLK) for h in range(2)] for i in range(3)],
                    "x": sb("gx", P, BLK), "la": sb("gla", P, BLK), "cs": sb("gcs", P, BLK),
                    "eb": sb("geb", P, BLK), "enb": sb("genb", P, BLK), "ebC": [sb(f"gebC{i}", P, SB) for i in range(2)],
                    "AT": sb("AT", P, 2, 4, P), "KT": sb("KTt", P, 4, P), "VT": [sb(f"VT{h}", P, 4, P) for h in range(2)],
                    "Sh": sb("Sh", P, NC + 1, P), "Sg": sb("Sg", P, SB, P), "VM": sb("VM", 64, 2, SB, P),
                    "o": [sb(f"osb{h}", P, BLK) for h in range(2)], "sq": [sb(f"osq{h}", P, BLK) for h in range(2)],
                    "rs": [sb(f"ors{h}", P, BLK) for h in range(2)],
                }
                W, GD = B["W"], B["GD"]
                with nc.Block() as block:
                    @block.sync
                    def _(sp):
                        sp.dma_start(W[:, 0, :], A["w_even"][1]).then_inc(d_p, 16)
                        sp.wait_ge(s_proj, NB + 1)
                        sp.dma_start(W[:], A["w_even"][18:24].rearrange("t p n -> p t n")).then_inc(d_w, 16)
                        sp.wait_ge(d_w, 16)

                    @block.gpsimd
                    def _(pool):
                        for z in (B["QG"][2], B["KG"][2], *B["V"][2]):
                            nc.gpsimd.memset(z[:], 0.0)

                    @block.tensor
                    def _(pe):
                        pe.wait_ge(d_p, 16)
                        for b, (c0, n) in enumerate(COLS):
                            if b >= 2:
                                pe.wait_ge(a_ev, b - 1)
                            project(PJ[b % 2], W, 0, c0, n, 16).then_inc(s_proj, 1)

                    @block.scalar
                    def _(act):
                        for b, (c0, n) in enumerate(COLS):
                            act.wait_ge(s_proj, b + 1)
                            nc.scalar.activation(GD[:, c0:c0 + n], PJ[b % 2][0:16, 0:n], ACT.Copy).then_inc(a_ev, 1)
                rounds_end()
                with nc.Fori(0, GU) as u:
                    for step in range(NB + 3):
                        gla_step(u, step, B)

        def gla_step(u, step, B):
            W, GD, par, GL, Sh, Sg, AT, KT_, VT, VM = (B[x] for x in ("W", "GD", "par", "GL", "Sh", "Sg", "AT", "KT", "VT", "VM"))
            q, k, x, la, cs, eb, enb, o, sq, rs = (B[y] for y in ("q", "k", "x", "la", "cs", "eb", "enb", "o", "sq", "rs"))
            e = step if step <= NB else None
            c = step - 1 if 1 <= step <= NB + 1 else None
            g = step - 2 if step >= 2 else None
            sample_e, sample_c = e == NB, c == NB
            if e is not None:
                c0, n = COLS[e]
                bi = 2 if sample_e else e % 2
                QGe, KGe, Ve, gse = B["QG"][bi], B["KG"][bi], B["V"][bi], B["gs"][e % 3]
            if c is not None:
                ci = 2 if sample_c else c % 2
                QG, KG, V = B["QG"][ci], B["KG"][ci], B["V"][ci]
                pairs = 1 if sample_c else NC // 2
                wide = pairs * P
                cn = COLS[c][1]
            if g is not None:
                gc0, m = COLS[g]
            halves = [(0, 64), (64, 128)]

            def by_pair(t):
                return t[:, 0:wide].rearrange("p (c j) -> p c j", j=P)

            with nc.Block() as block:
                @block.sync
                def _(sp):
                    if step == 0:
                        sp.dma_start(GL[:], A["gla_up"][:, bass.ds(u * P, P)]).then_inc(d_p, 16)
                        sp.dma_start(par[:], A["gla_par"][bass.ds(u, 1)].rearrange("u p n -> p (u n)")).then_inc(d_p, 16)
                    if step == NB:
                        sp.dma_start(Sg[:], A["gla_in"][bass.ds(u, 1)].rearrange("u p (s v) -> p (u s) v", v=P)).then_inc(d_s, 16)
                        sp.wait_ge(d_s, 16)
                    if step == NB + 1:
                        sp.dma_start(W[:], A["w_even"][24:30].rearrange("t p n -> p t n")).then_inc(d_w, 16)
                        sp.dma_start(A["gla_p_out"][bass.ds(u, 1)].rearrange("u p v -> p (u v)"), Sh[:, NC, :]).then_inc(d_o2, 16)
                        sp.wait_ge(v_S, 2)
                        sp.dma_start(A["gla_s_out"][bass.ds(u, 1)].rearrange("u p (s v) -> p (u s) v", v=P), Sg[:]).then_inc(d_o2, 16)
                        sp.wait_ge(d_w, 16)
                        sp.wait_ge(d_o2, 32)
                    if g is not None:
                        for h in range(2):
                            sp.wait_ge(v_o, 2 * h + 2)
                            sp.dma_start(A["O"][bass.ds(4 + 2 * u + h, 1), :, gc0:gc0 + m].rearrange("u p n -> p (u n)"),
                                         rs[h][:, 0:m]).then_inc(d_o, 16)
                        sp.wait_ge(d_o, 32)

                @block.tensor
                def _(pe):
                    if e is not None:
                        if step == 0:
                            pe.wait_ge(d_p, 32)
                        nc.tensor.matmul(EB[0][:, 0:n], GL[:, :], GD[:, c0:c0 + n], start=True, stop=True).then_inc(s_lora, 1)
                    if c is not None:
                        for h, (lo, hi) in enumerate(halves):
                            for p in range(pairs):
                                mm = nc.tensor.matmul(Q[h][:, p * P:(p + 1) * P], KG[lo:hi, p * P:(p + 1) * P],
                                                      QG[lo:hi, p * P:(p + 1) * P], start=True, stop=True)
                            mm.then_inc(s_A, 1)
                    if e is not None:
                        project(PJ[0], W, 0, c0, n).then_inc(s_proj, 1)
                    if c is not None:
                        for t, (src, bank) in enumerate(((KG, Q[2]), (V[0], Q[3]), (V[1], Q[0]))):
                            if t == 2:
                                pe.wait_ge(v_M, 1)
                            for p in range(pairs):
                                mm = nc.tensor.transpose(bank[:, p * P:(p + 1) * P], src[:, p * P:(p + 1) * P], ident)
                            mm.then_inc(s_tr, 1)
                    if g is not None:
                        pe.wait_ge(a_sq, 2)
                        nc.tensor.matmul(EB[1][:, 0:m], ones, sq[0][:, 0:m], start=True, stop=True).then_inc(s_ssq, 1)
                        if e is not None:
                            pe.wait_ge(v_g, 1)
                        nc.tensor.matmul(EB[0][:, 0:m], ones, sq[1][:, 0:m], start=True, stop=True).then_inc(s_ssq, 1)
                    if e is not None:
                        project(PJ[1], W, 1, c0, n).then_inc(s_proj, 1)
                    if c is not None:
                        pe.wait_ge(a_tb, 3)
                        pe.wait_ge(v_M, 2)
                        if not sample_c:
                            for par_, bank in enumerate((Q[1], Q[2])):
                                rl, rh = halves[par_]
                                for p in range(pairs):
                                    for h, (lo, hi) in enumerate(halves):
                                        mm = nc.tensor.matmul(bank[lo:hi, p * P:(p + 1) * P], KT_[rl:rh, p, lo:hi],
                                                              VT[h][rl:rh, p, :], start=True, stop=True)
                                mm.then_inc(s_SU, 1)
                        else:
                            pe.wait_ge(v_b, 2)
                            for i, bank in enumerate((Q[1], Q[2])):
                                for h, (lo, hi) in enumerate(halves):
                                    mm = nc.tensor.matmul(bank[lo:hi, :], KT_[0:64, 0, lo:hi], VM[:, h, 4 * i:4 * i + 4, :],
                                                          start=True, stop=True)
                                mm.then_inc(s_SU, 1)
                    if e is not None:
                        for t in (2, 3):
                            pe.wait_ge(a_ev, t - 1)
                            project(PJ[t % 2], W, t, c0, n).then_inc(s_proj, 1)
                    if c is not None:
                        if not sample_c:
                            pe.wait_ge(v_S, 1 + 2 * (NC - 1))
                        for h, (lo, hi) in enumerate(halves):
                            bank = (Q[3], Q[0])[h]
                            if sample_c:
                                nc.tensor.matmul(bank[:, 0:NS], VT[h][:, 0, :], AT[:, h, 0, 0:NS], start=True,
                                                 stop=False, skip_group_check=True)
                                for s_ in range(SB):
                                    a = s_ * SL
                                    mm = nc.tensor.matmul(bank[:, a:a + SL], Sg[lo:hi, s_, :], QG[lo:hi, a:a + SL],
                                                          start=False, stop=True, skip_group_check=True)
                            else:
                                for p in range(pairs):
                                    nc.tensor.matmul(bank[:, p * P:(p + 1) * P], VT[h][:, p, :], AT[:, h, p, :],
                                                     start=True, stop=False, skip_group_check=True)
                                    for j in (2 * p, 2 * p + 1):
                                        mm = nc.tensor.matmul(bank[:, j * C:(j + 1) * C], Sh[lo:hi, j, :], QG[lo:hi, j * C:(j + 1) * C],
                                                              start=False, stop=True, skip_group_check=True)
                            mm.then_inc(s_Y, 1)
                    if e is not None:
                        for t in (4, 5):
                            pe.wait_ge(a_ev, t - 1)
                            project(PJ[t % 2], W, t, c0, n).then_inc(s_proj, 1)

                @block.scalar
                def _(act):
                    def evacuate(t, out, func=ACT.Copy, **kw):
                        act.wait_ge(s_proj, t + 1)
                        nc.scalar.activation(out, PJ[t % 2][:, 0:n], func, **kw).then_inc(a_ev, 1)

                    if g is not None:
                        for h in range(2):
                            nc.scalar.activation(sq[h][:, 0:m], o[h][:, 0:m], ACT.Square).then_inc(a_sq, 1)
                    if e is not None:
                        act.wait_ge(v_g, 2)
                        nc.scalar.activation(la[:, 0:n], la[:, 0:n], ACT.Exp, scale=-1.0).then_inc(a_g, 1)
                        act.wait_ge(a_g, 1)
                        nc.scalar.activation(la[:, 0:n], la[:, 0:n], ACT.Ln, bias=eps[:, E_ONE:E_ONE + 1]).then_inc(a_g, 1)
                        evacuate(0, q[:, 0:n], scale=C ** -0.5)
                    if c is not None:
                        for t, (dst, bank) in enumerate(((KT_, Q[2]), (VT[0], Q[3]), (VT[1], Q[0]))):
                            act.wait_ge(s_tr, t + 1)
                            nc.scalar.activation(dst[:, 0:pairs, :], by_pair(bank), ACT.Copy).then_inc(a_tb, 1)
                    if e is not None:
                        evacuate(1, k[:, 0:n])
                    if g is not None:
                        for h in range(2):
                            act.wait_ge(s_ssq, h + 1)
                            nc.scalar.activation(rs[h][:, 0:m], EB[1 - h][:, 0:m], ACT.Ln, scale=1.0 / P,
                                                 bias=eps[:, E_RMS:E_RMS + 1]).then_inc(a_ln, 1)
                        for h in range(2):
                            act.wait_ge(a_ln, h + 1)
                            nc.scalar.activation(rs[h][:, 0:m], rs[h][:, 0:m], ACT.Exp, scale=-0.5).then_inc(a_rs, 1)
                    if e is not None:
                        act.wait_ge(v_cs, 1)
                        nc.scalar.activation(eb[:, 0:n], cs[:, 0:n], ACT.Exp, scale=1.0 / 16).then_inc(a_exp, 1)
                        nc.scalar.activation(enb[:, 0:n], cs[:, 0:n], ACT.Exp, scale=-1.0 / 16).then_inc(a_exp, 1)
                        for h in range(2):
                            evacuate(2 + h, Ve[h][:, 0:n])
                    if c is not None:
                        for h in range(2):
                            act.wait_ge(s_Y, h + 1)
                            if g is not None:
                                act.wait_ge(v_o, 2 * h + 1)
                            nc.scalar.activation(o[h][:, 0:cn], (Q[3], Q[0])[h][:, 0:cn], ACT.Copy).then_inc(a_y, 1)
                    if e is not None:
                        for h in range(2):
                            evacuate(4 + h, gse[h][:, 0:n], ACT.Silu)

                @block.vector
                def _(dve):
                    if e is not None:
                        dve.wait_ge(s_lora, 1)
                        if step == 0:
                            dve.wait_ge(d_p, 32)
                        nc.vector.tensor_scalar(x[:, 0:n], EB[0][:, 0:n], par[:, G_GB:G_GB + 1], None, ALU.add).then_inc(v_g, 1)
                        dve.wait_ge(v_g, 1)
                        nc.vector.scalar_tensor_tensor(la[:, 0:n], x[:, 0:n], -1.0, x[:, 0:n], ALU.mult, ALU.max).then_inc(v_g, 1)
                    if c is not None:
                        mg = cst("maskGs" if sample_c else "maskG")
                        for h in range(2):
                            dve.wait_ge(s_A, h + 1)
                            nc.vector.tensor_tensor(AT[:, h, 0:pairs, :], by_pair(Q[h]),
                                                    mg.unsqueeze(1).to_broadcast([P, pairs, P]), ALU.mult).then_inc(v_M, 1)
                    if e is not None:
                        dve.wait_ge(a_g, 2)
                        nc.vector.scalar_tensor_tensor(x[:, 0:n], x[:, 0:n], 0.0, la[:, 0:n], ALU.min, ALU.subtract).then_inc(v_g, 1)
                        dve.wait_ge(v_g, 3)
                        rm = cst("resets" if sample_e else "reset")
                        nc.vector.tensor_tensor_scan(cs[:, 0:n], rm, x[:, 0:n], 0.0, ALU.mult, ALU.add).then_inc(v_cs, 1)
                    if c is not None and not sample_c:
                        if c == 0:
                            nc.vector.memset(Sh[:, 0, :], 0.0).then_inc(v_S, 1)
                        else:
                            nc.vector.tensor_copy(Sh[:, 0, :], Sh[:, NC, :]).then_inc(v_S, 1)
                        ec = B["ebC"][c % 2]
                        dve.wait_ge(s_SU, 2)
                        for j in range(NC):
                            dve.wait_ge(v_S, 1 + 2 * j)
                            nc.vector.tensor_tensor(Sh[:, j + 1, :], Q[1 + j % 2][:, (j // 2) * P:(j // 2 + 1) * P], Sh[:, j, :],
                                                    ALU.add).then_inc(v_S, 1)
                            dve.wait_ge(v_S, 2 + 2 * j)
                            nc.vector.tensor_scalar(Sh[:, j + 1, :], Sh[:, j + 1, :], ec[:, j:j + 1], None, ALU.mult).then_inc(v_S, 1)
                    if sample_c:
                        dve.wait_ge(a_tb, 3)
                        for h in range(2):
                            nc.vector.tensor_tensor(VM[:, h, :, :], VT[h][0:64, 0, :].unsqueeze(1).to_broadcast([64, SB, P]),
                                                    cst("seq")[0:64, :].unsqueeze(2).to_broadcast([64, SB, P]),
                                                    ALU.mult).then_inc(v_b, 1)
                        dve.wait_ge(s_SU, 2)
                        dve.wait_ge(s_Y, 2)
                        for i in range(2):
                            nc.vector.tensor_tensor(Sg[:, 4 * i:4 * i + 4, :], Q[1 + i].rearrange("p (s v) -> p s v", v=P),
                                                    Sg[:, 4 * i:4 * i + 4, :], ALU.add).then_inc(v_x1, 1)
                        dve.wait_ge(v_x1, 2)
                        nc.vector.tensor_tensor(Sg[:], Sg[:], B["ebC"][0][:, :].unsqueeze(2).to_broadcast([P, SB, P]),
                                                ALU.mult).then_inc(v_S, 2)
                    if g is not None:
                        for h in range(2):
                            dve.wait_ge(a_rs, h + 1)
                            nc.vector.tensor_tensor(rs[h][:, 0:m], o[h][:, 0:m], rs[h][:, 0:m], ALU.mult).then_inc(v_o, 1)
                            dve.wait_ge(v_o, 2 * h + 1)
                            nc.vector.scalar_tensor_tensor(rs[h][:, 0:m], rs[h][:, 0:m], par[:, G_NORM:G_NORM + 1],
                                                           B["gs"][g % 3][h][:, 0:m], ALU.mult, ALU.mult).then_inc(v_o, 1)
                    if e is not None:
                        dve.wait_ge(a_exp, 2)
                        dve.wait_ge(a_ev, 2)
                        nc.vector.tensor_tensor(QGe[:, 0:n], q[:, 0:n], eb[:, 0:n], ALU.mult).then_inc(v_zr, 1)
                        nc.vector.tensor_tensor(KGe[:, 0:n], k[:, 0:n], enb[:, 0:n], ALU.mult).then_inc(v_zr, 1)

                @block.gpsimd
                def _(pool):
                    if e is not None:
                        pool.wait_ge(a_exp, 1)
                        last = eb[:, 0:n].rearrange("p (s j) -> p s j", j=SL if sample_e else C)[:, :, -1:].squeeze(2)
                        nc.gpsimd.tensor_copy(B["ebC"][e % 2][:, :], last).then_inc(p_e, 1)
            rounds_end()

        BANKS = [*Q, *PJ]

        def even_out_stage():
            with nc.sbuf_tensor("WO", [P, KT, D], F32) as WO, nc.sbuf_tensor("ob0", [P, KT, RB], F32) as ob0, \
                    nc.sbuf_tensor("ob1", [P, KT, RB], F32) as ob1, nc.sbuf_tensor("xr0", [P, KT, RB], F32) as xr0, \
                    nc.sbuf_tensor("xr1", [P, KT, RB], F32) as xr1, nc.sbuf_tensor("gno", [P, KT], F32) as gno, \
                    nc.sbuf_tensor("rs2", [P, RB], F32) as rs2:
                ob, xr = (ob0, ob1), (xr0, xr1)

                def load_o(sp, b):
                    sp.dma_start(ob[b % 2][:], A["O"][:, :, b * RB:(b + 1) * RB].rearrange("k p n -> p k n")).then_inc(d_x[0], 16)
                    sp.dma_start(xr[b % 2][:], A["xT"][:, :, b * RB:(b + 1) * RB]).then_inc(d_x[1], 16)

                with nc.Block() as block:
                    @block.sync
                    def _(sp):
                        load_o(sp, 0)
                        sp.dma_start(WO[:], A["w_out_even"]).then_inc(d_w, 16)
                        sp.dma_start(gno[:], A["norm_odd"]).then_inc(d_p, 16)
                        for s_, v_ in ((d_x[0], 16), (d_x[1], 16), (d_w, 16), (d_p, 16)):
                            sp.wait_ge(s_, v_)
                rounds_end()
                for step in range(NRB + 1):
                    e = step if step < NRB else None
                    g = step - 1 if step else None
                    with nc.Block() as block:
                        @block.sync
                        def _(sp):
                            if g is not None:
                                sp.dma_start(A["X2"][:, :, g * RB:(g + 1) * RB], xr[g % 2][:]).then_inc(d_o, 16)
                            if step + 1 < NRB:
                                b = step + 1
                                if g is not None:
                                    sp.wait_ge(d_o, 16)
                                    sp.wait_ge(s_ssum, 1)
                                    sp.wait_ge(v_h, 1)
                                load_o(sp, b)
                                sp.wait_ge(d_x[0], 16)
                                sp.wait_ge(d_x[1], 16)
                            if g is not None:
                                sp.wait_ge(d_o, 16)

                        @block.tensor
                        def _(pe):
                            if e is not None:
                                for t in range(KT):
                                    if t >= len(BANKS):
                                        pe.wait_ge(v_mix, t - len(BANKS) + 1)
                                    for k in range(KT):
                                        mm = nc.tensor.matmul(BANKS[t % len(BANKS)][:, 0:RB], WO[:, k, t * P:(t + 1) * P],
                                                              ob[e % 2][:, k, :], start=(k == 0), stop=(k == KT - 1))
                                    mm.then_inc(s_proj, 1)
                                    if t == 1 and g is not None:
                                        sums(pe)
                            elif g is not None:
                                sums(pe)

                        def sums(pe):
                            pe.wait_ge(a_sq, 1)
                            for k in range(KT):
                                mm = nc.tensor.matmul(EB[0][:, 0:RB], ones, ob[g % 2][:, k, :], start=(k == 0), stop=(k == KT - 1))
                            mm.then_inc(s_ssum, 1)

                        @block.scalar
                        def _(act):
                            if g is not None:
                                nc.scalar.activation(ob[g % 2][:], xr[g % 2][:], ACT.Square).then_inc(a_sq, 1)
                                act.wait_ge(s_ssum, 1)
                                nc.scalar.activation(rs2[:], EB[0][:, 0:RB], ACT.Ln, scale=1.0 / D,
                                                     bias=eps[:, E_RMS:E_RMS + 1]).then_inc(a_ln, 1)
                                act.wait_ge(a_ln, 1)
                                nc.scalar.activation(rs2[:], rs2[:], ACT.Exp, scale=-0.5).then_inc(a_rs, 1)

                        @block.vector
                        def _(dve):
                            def add(t):
                                dve.wait_ge(s_proj, t + 1)
                                nc.vector.tensor_tensor(xr[e % 2][:, t, :], BANKS[t % len(BANKS)][:, 0:RB], xr[e % 2][:, t, :],
                                                        ALU.add).then_inc(v_mix, 1)

                            if e is not None:
                                for t in range(2):
                                    add(t)
                            if g is not None:
                                dve.wait_ge(a_rs, 1)
                                for k in range(KT):
                                    ins = nc.vector.scalar_tensor_tensor(H[:, k, g * RB:(g + 1) * RB], xr[g % 2][:, k, :], gno[:, k:k + 1],
                                                                         rs2[:], ALU.mult, ALU.mult)
                                ins.then_inc(v_h, 1)
                            if e is not None:
                                for t in range(2, KT):
                                    add(t)
                    rounds_end()

        def conv_stage():
            c1 = ExitStack()
            with c1:
                def sb(name, *shape):
                    return c1.enter_context(nc.sbuf_tensor(name, list(shape), F32))

                B = {
                    "W": [sb(f"oW{i}", P, 3, D) for i in range(2)], "par": [sb(f"opar{i}", P, 4) for i in range(2)],
                    "cw": [sb(f"cw{i}", P, CW) for i in range(2)],
                    "U": [sb(f"U{i}", P, HALO + SEQ) for i in range(2)],
                    "Us": [sb(f"Us{i}", P, SB, HALO + SL) for i in range(2)],
                    "acc": sb("acc", P, T), "sg": [sb(f"osg{i}", P, BLK) for i in range(2)],
                    "va": [sb(f"ova{i}", P, BLK) for i in range(2)], "gt": [sb(f"ogt{i}", P, BLK) for i in range(2)],
                }

                def load(sp, t, i, static):
                    one = (lambda a: a[t:t + 1]) if static else (lambda a: a[bass.ds(t, 1)])
                    sp.dma_start(B["W"][i][:], one(A["w_odd"]).rearrange("c j p n -> p (c j) n")).then_inc(d_w, 16)
                    sp.dma_start(B["par"][i][:], one(A["odd_par"]).rearrange("c p n -> p (c n)")).then_inc(d_p, 16)
                    sp.dma_start(B["cw"][i][:], one(A["conv_w"]).rearrange("c p n -> p (c n)")).then_inc(d_p, 16)

                with nc.Block() as block:
                    @block.sync
                    def _(sp):
                        load(sp, 0, 0, True)
                        sp.wait_ge(d_w, 16)
                        sp.wait_ge(d_p, 32)

                    @block.gpsimd
                    def _(pool):
                        nc.gpsimd.memset(ysum[:], 0.0)
                        for i in range(2):
                            nc.gpsimd.memset(B["U"][i][:, 0:HALO], 0.0)
                rounds_end()
                conv_step(B, load, 0, None, 0, True)
                with nc.Fori(0, (CT - 2) // 2) as j:
                    conv_step(B, load, j * 2 + 1, j * 2, 1, False)
                    conv_step(B, load, j * 2 + 2, j * 2 + 1, 0, False)
                conv_step(B, load, CT - 1, CT - 2, 1, True)
                conv_step(B, load, None, CT - 1, 0, True)

        def conv_step(B, load, e, c, i, static):
            W, par, U, Us = B["W"][i], B["par"][i], B["U"][i], B["Us"][i]
            U2, Us2, cw2, par2 = B["U"][1 - i], B["Us"][1 - i], B["cw"][1 - i], B["par"][1 - i]
            acc, sg, va, gt = B["acc"], B["sg"], B["va"], B["gt"]
            one = (lambda a, t: a[t:t + 1]) if static else (lambda a, t: a[bass.ds(t, 1)])
            accs = acc[:, SEQ:T].rearrange("p (s j) -> p s j", j=SL)
            with nc.Block() as block:
                @block.sync
                def _(sp):
                    if e is not None:
                        sp.dma_start(Us[:, :, 0:HALO], one(A["conv_in"], e).rearrange("c p s j -> p (c s) j")).then_inc(d_s, 16)
                    if e is not None and not (static and e == CT - 1):
                        one_ = one(A["w_odd"], e + 1)
                        sp.dma_start(B["W"][1 - i][:], one_.rearrange("c j p n -> p (c j) n")).then_inc(d_w, 16)
                        if c is not None:
                            sp.wait_ge(v_acc, 2 * CW)
                        sp.dma_start(B["par"][1 - i][:], one(A["odd_par"], e + 1).rearrange("c p n -> p (c n)")).then_inc(d_p, 16)
                        sp.dma_start(B["cw"][1 - i][:], one(A["conv_w"], e + 1).rearrange("c p n -> p (c n)")).then_inc(d_p, 16)
                        sp.wait_ge(d_w, 16)
                        sp.wait_ge(d_p, 32)
                    if c is not None:
                        sp.wait_ge(v_acc, 2 * CW)
                        sp.dma_start(one(A["Y"], c).rearrange("c p n -> p (c n)"), acc[:]).then_inc(d_o2, 16)
                        sp.wait_ge(d_o2, 16)
                    if e is not None:
                        sp.wait_ge(p_u, NB + 1)
                        sp.dma_start(one(A["conv_p_out"], e).rearrange("c p n -> p (c n)"), U[:, SEQ:SEQ + HALO]).then_inc(d_x[0], 16)
                        sp.dma_start(one(A["conv_s_out"], e).rearrange("c p s j -> p (c s) j"), Us[:, :, SL:SL + HALO]).then_inc(d_x[0], 16)
                        sp.wait_ge(d_x[0], 32)

                @block.tensor
                def _(pe):
                    if e is None:
                        return
                    for b, (c0, n) in enumerate(COLS):
                        for t in range(3):
                            x = 3 * b + t
                            if x >= 6:
                                pe.wait_ge(a_ev, x - 5)
                            project(BANKS[x % 6], W, t, c0, n).then_inc(s_proj, 1)

                @block.scalar
                def _(act):
                    if e is None:
                        return
                    for b, (c0, n) in enumerate(COLS):
                        for t, (dst, func) in enumerate(((va, ACT.Identity), (sg, ACT.Sigmoid), (gt, ACT.Silu))):
                            x = 3 * b + t
                            act.wait_ge(s_proj, x + 1)
                            if b >= 2:
                                if t < 2:
                                    act.wait_ge(p_u, b - 1)
                                else:
                                    act.wait_ge(d_sg[b % 2], 16 * (b // 2))
                            nc.scalar.activation(dst[b % 2][:, 0:n], BANKS[x % 6][:, 0:n], func, bias=par[:, t:t + 1]).then_inc(a_ev, 1)
                        act.wait_ge(a_ev, 3 * b + 3)
                        act.dma_start(one(A["SG"], e)[:, :, c0:c0 + n].rearrange("c p n -> p (c n)"),
                                      gt[b % 2][:, 0:n]).then_inc(d_sg[b % 2], 16)
                    for i_ in range(2):
                        act.wait_ge(d_sg[i_], 16 * len(range(i_, NB + 1, 2)))

                @block.gpsimd
                def _(pool):
                    if e is not None:
                        for b, (c0, n) in enumerate(COLS):
                            pool.wait_ge(a_ev, 3 * b + 2)
                            if b < NB:
                                nc.gpsimd.tensor_tensor(U[:, HALO + c0:HALO + c0 + n], va[b % 2][:, 0:n], sg[b % 2][:, 0:n],
                                                        ALU.mult).then_inc(p_u, 1)
                            else:
                                pool.wait_ge(d_s, 16)
                                nc.gpsimd.tensor_tensor(Us[:, :, HALO:HALO + SL], va[b % 2][:, 0:n].rearrange("p (s j) -> p s j", j=SL),
                                                        sg[b % 2][:, 0:n].rearrange("p (s j) -> p s j", j=SL), ALU.mult).then_inc(p_u, 1)
                    if c is not None:
                        pool.wait_ge(v_acc, 2 * CW)
                        nc.gpsimd.tensor_tensor(ysum[:], ysum[:], acc[:], ALU.add).then_inc(p_ys, 1)

                @block.vector
                def _(dve):
                    if c is None:
                        return
                    for d in range(CW):
                        w = cw2[:, d:d + 1]
                        for out, src in ((acc[:, 0:SEQ], U2[:, d:d + SEQ]), (accs, Us2[:, :, d:d + SL])):
                            if d == 0:
                                nc.vector.tensor_scalar(out, src, w, par2[:, O_CB:O_CB + 1], ALU.mult, ALU.add).then_inc(v_acc, 1)
                            else:
                                ready = 2 * d - (out is not accs)
                                dve.wait_ge(v_acc, ready)
                                nc.vector.scalar_tensor_tensor(out, src, w, out, ALU.mult, ALU.add).then_inc(v_acc, 1)
            rounds_end()

        def final_stage():
            c1 = ExitStack()
            with c1:
                def sb(name, *shape):
                    return c1.enter_context(nc.sbuf_tensor(name, list(shape), F32))

                WO = sb("WO2", P, KT, D)
                yb = [sb(f"yb{i}", P, KT, RB) for i in range(2)]
                sgb = sb("sgb", P, KT, RB)
                sq = sb("fsq", P, KT, RB)
                xr = [sb(f"fx{i}", P, KT, RB) for i in range(3)]
                rsl, rsf = sb("rsl", P, RB), sb("rsf", P, RB)
                lw, lb, fn = sb("lw", P, KT), sb("lb", P, KT), sb("fn", P, KT)

                def rows(a, b):
                    return a[:, :, b * RB:(b + 1) * RB]

                with nc.Block() as block:
                    @block.sync
                    def _(sp):
                        sp.dma_start(WO[:], A["w_out_odd"]).then_inc(d_w, 16)
                        for dst, name in ((lw, "ln_w"), (lb, "ln_b"), (fn, "final_norm")):
                            sp.dma_start(dst[:], A[name]).then_inc(d_p, 16)
                        sp.wait_ge(d_w, 16)
                        sp.wait_ge(d_p, 48)
                rounds_end()
                for step in range(NRB + 2):
                    a = step if step < NRB else None
                    e = step - 1 if 1 <= step <= NRB else None
                    g = step - 2 if step >= 2 else None
                    with nc.Block() as block:
                        @block.sync
                        def _(sp):
                            if a is not None:
                                sp.dma_start(yb[a % 2][:], A["Y"][:, :, a * RB:(a + 1) * RB].rearrange("k p n -> p k n")).then_inc(d_x[0], 16)
                                sp.dma_start(sgb[:], A["SG"][:, :, a * RB:(a + 1) * RB].rearrange("k p n -> p k n")).then_inc(d_g, 16)
                                sp.dma_start(xr[a % 3][:], rows(A["X2"], a)).then_inc(d_r, 16)
                            if g is not None:
                                sp.wait_ge(v_o, KT)
                                sp.dma_start(rows(A["yT"], g), xr[g % 3][:]).then_inc(d_o, 16)
                                sp.wait_ge(d_o, 16)
                            if a is not None:
                                sp.wait_ge(d_r, 16)

                        @block.tensor
                        def _(pe):
                            if a is not None:
                                nc.tensor.matmul(EB[0][:, 0:RB], ones, ysum[:, a * RB:(a + 1) * RB], start=True, stop=True).then_inc(s_mean, 1)
                            if e is not None:
                                for t in range(KT):
                                    if t >= 5:
                                        pe.wait_ge(v_mix, t - 4)
                                    for k in range(KT):
                                        mm = nc.tensor.matmul(BANKS[t % 5][:, 0:RB], WO[:, k, t * P:(t + 1) * P], yb[e % 2][:, k, :],
                                                              start=(k == 0), stop=(k == KT - 1))
                                    mm.then_inc(s_proj, 1)
                                    if t == 2 and g is not None:
                                        final_sums(pe)
                            elif g is not None:
                                final_sums(pe)
                            if a is not None:
                                pe.wait_ge(a_sq, 1 + (g is not None))
                                for k in range(KT):
                                    mm = nc.tensor.matmul(EB[1][:, 0:RB], ones, sq[:, k, :], start=(k == 0), stop=(k == KT - 1))
                                mm.then_inc(s_var, 1)

                        def final_sums(pe):
                            pe.wait_ge(a_sq, 1)
                            for k in range(KT):
                                mm = nc.tensor.matmul(BANKS[5][:, 0:RB], ones, sq[:, k, :], start=(k == 0), stop=(k == KT - 1))
                            mm.then_inc(s_ssum, 1)

                        @block.scalar
                        def _(act):
                            if g is not None:
                                nc.scalar.activation(sq[:], xr[g % 3][:], ACT.Square).then_inc(a_sq, 1)
                                act.wait_ge(s_ssum, 1)
                                nc.scalar.activation(rsf[:], BANKS[5][:, 0:RB], ACT.Ln, scale=1.0 / D,
                                                     bias=eps[:, E_RMS:E_RMS + 1]).then_inc(a_ln, 1)
                                act.wait_ge(a_ln, 1)
                                nc.scalar.activation(rsf[:], rsf[:], ACT.Exp, scale=-0.5).then_inc(a_rs, 1)
                            if a is not None:
                                n0 = 1 if g is not None else 0
                                act.wait_ge(v_yc, KT)
                                nc.scalar.activation(sq[:], yb[a % 2][:], ACT.Square).then_inc(a_sq, 1)
                                act.wait_ge(s_var, 1)
                                nc.scalar.activation(rsl[:], EB[1][:, 0:RB], ACT.Ln, scale=1.0 / D,
                                                     bias=eps[:, E_LN:E_LN + 1]).then_inc(a_ln, 1)
                                act.wait_ge(a_ln, n0 + 1)
                                nc.scalar.activation(rsl[:], rsl[:], ACT.Exp, scale=-0.5).then_inc(a_rs, 1)
                                for k in range(KT):
                                    act.wait_ge(v_kn, k + 1)
                                    nc.scalar.activation(yb[a % 2][:, k, :], yb[a % 2][:, k, :], ACT.Silu, scale=lw[:, k:k + 1],
                                                         bias=lb[:, k:k + 1]).then_inc(a_gl, 1)

                        @block.gpsimd
                        def _(pool):
                            if a is not None:
                                pool.wait_ge(d_g, 16)
                                for k in range(KT):
                                    pool.wait_ge(a_gl, k + 1)
                                    nc.gpsimd.tensor_tensor(yb[a % 2][:, k, :], yb[a % 2][:, k, :], sgb[:, k, :], ALU.mult).then_inc(p_u, 1)

                        @block.vector
                        def _(dve):
                            n0 = 1 if g is not None else 0
                            if a is not None:
                                dve.wait_ge(d_x[0], 16)
                                dve.wait_ge(s_mean, 1)
                                for k in range(KT):
                                    nc.vector.scalar_tensor_tensor(yb[a % 2][:, k, :], EB[0][:, 0:RB], -1.0 / D, yb[a % 2][:, k, :],
                                                                   ALU.mult, ALU.add).then_inc(v_yc, 1)

                            def add(t):
                                dve.wait_ge(s_proj, t + 1)
                                nc.vector.tensor_tensor(xr[e % 3][:, t, :], BANKS[t % 5][:, 0:RB], xr[e % 3][:, t, :],
                                                        ALU.add).then_inc(v_mix, 1)

                            if e is not None:
                                for t in range(4):
                                    add(t)
                            if g is not None:
                                dve.wait_ge(a_rs, 1)
                                for k in range(KT):
                                    nc.vector.scalar_tensor_tensor(xr[g % 3][:, k, :], xr[g % 3][:, k, :], fn[:, k:k + 1], rsf[:],
                                                                   ALU.mult, ALU.mult).then_inc(v_o, 1)
                            if e is not None:
                                for t in range(4, KT):
                                    add(t)
                            if a is not None:
                                dve.wait_ge(a_rs, n0 + 1)
                                for k in range(KT):
                                    nc.vector.tensor_tensor(yb[a % 2][:, k, :], yb[a % 2][:, k, :], rsl[:], ALU.mult).then_inc(v_kn, 1)
                    rounds_end()

        norm_stage()
        rwkv_stage()
        gla_stage()
        even_out_stage()
        conv_stage()
        hctx.close()
        final_stage()




def constants():
    K = np.zeros((P, NCONST), np.float32)

    def put(name, x):
        a, b = _COLS[name]
        K[:, a:b] = x

    s, t = np.arange(P)[:, None] % C, np.arange(C)[None, :]
    live = (s < NS) & (t < NS) & (s // SL == t // SL)
    put("maskA", np.concatenate([s < t, s <= t], 1))
    put("maskAs", np.concatenate([(s < t) & live, (s <= t) & live], 1))
    lv = [((s >> l) == (t >> l)) & (((s >> (l - 1)) & 1) == 1) & (((t >> (l - 1)) & 1) == 0) for l in range(1, 7)]
    put("lvl", np.concatenate(lv, 1))
    put("lvl1t", ((s >> 1) == (t >> 1)) & (s < t))
    put("ident", np.eye(P))
    put("ident2", s == t)
    r, c = np.arange(P)[:, None], np.arange(P)[None, :]
    put("bones", r // C == c // C)
    put("ones", 1.0)
    put("reset", (np.arange(BLK) % C != 0)[None, :])
    put("resets", (np.arange(NS) % SL != 0)[None, :])
    put("seq", (s < NS) & (s // SL == np.arange(SB)[None, :]))
    put("maskG", (r // C == c // C) & (r <= c))
    put("maskGs", (r < NS) & (c < NS) & (r // SL == c // SL) & (r <= c))
    e = np.zeros((P, 8))
    e[:, E_RMS], e[:, E_GN], e[:, E_LN], e[:, E_UP], e[:, E_ONE] = RMS_EPS, GN_EPS, LN_EPS, 0.5 * LN_UP * math.log(2), 1.0
    put("eps", e)
    return K


def kernel(**inputs):
    import concourse.bacc as bacc
    from concourse.bass_utils import run_bass_kernel_spmd as run

    I = {k: np.asarray(v) for k, v in inputs.items()}

    def tiles(x):
        return x.reshape(KT, P, -1).transpose(1, 0, 2)

    def col(x):
        return x.reshape(-1, P).T

    x = np.concatenate([I["x_prompt"].reshape(SEQ, D), I["x_sample"].reshape(NS, D)], 0)
    w = I["w_in_even"][0]
    G0, S0 = RPROJ, RPROJ + GPROJ
    cols = [(3 * 512, P), (G0 + 1024, 16)]
    for u in range(RU):
        cols += [(u * P, P), (512 + u * P, P), (1024 + u * P, P), (S0 + u * P, P)]
    for g in range(GU):
        cols += [(G0 + g * P, P), (G0 + 256 + g * P, P), (G0 + 512 + 2 * g * P, P), (G0 + 512 + (2 * g + 1) * P, P),
                 (S0 + (4 + 2 * g) * P, P), (S0 + (5 + 2 * g) * P, P)]
    w_even = np.zeros((len(cols), P, KT, P), np.float32)
    for i, (a, n) in enumerate(cols):
        w_even[i, :, :, :n] = tiles(w[:, a:a + n])
    mu = I["rwkv_mu"][0]
    par = [mu[0:512], mu[512:1024], mu[1024:1536], I["rwkv_w0"][0], I["rwkv_a0"][0], I["rwkv_k_k"][0],
           I["rwkv_k_a"][0], I["rwkv_r_k"][0].reshape(-1), I["rwkv_ln_w"][0], I["rwkv_ln_b"][0]]
    shift = I["state_rwkv_shift"][0]
    order = [a + u * P for u in range(RU) for a in (0, 512, 1024)] + [3 * 512]
    wo = I["w_in_odd"][0]
    w_odd = np.stack([np.stack([tiles(wo[:, j * D + c * P:j * D + (c + 1) * P]) for j in range(3)]) for c in range(CT)])
    b3 = I["b_in_odd"][0].reshape(3, CT, P)
    arrays = {
        "const": constants(),
        "xT": x.T.reshape(KT, P, T).transpose(1, 0, 2),
        "norm_even": col(I["norm_even"][0]),
        "w_even": w_even.reshape(len(cols), P, KT * P),
        "mu_lora": mu[1536:1664].reshape(P, 1),
        "rwkv_par": np.stack([p.reshape(RU, P) for p in par], -1),
        "lora_up": np.concatenate([I["rwkv_w_up"][0], I["rwkv_a_up"][0]], 0),
        "shift_in": np.stack([shift[:, a:a + P].T for a in order]),
        "rwkv_in": I["state_rwkv"][0].reshape(SB, RU, 2, C, C).transpose(1, 2, 4, 0, 3).reshape(RU, P, SB * C),
        "gla_in": I["state_gla"][0].reshape(SB, GU, 2, C, P).transpose(1, 2, 3, 0, 4).reshape(GU, P, SB * P),
        "gla_up": I["gla_g_up"][0],
        "gla_par": np.stack([I["gla_g_b"][0].reshape(GU, P), np.broadcast_to(I["gla_norm"][0], (GU, P))], -1),
        "w_out_even": tiles(I["w_out_even"][0]),
        "norm_odd": col(I["norm_odd"][0]),
        "w_odd": w_odd.reshape(CT, 3, P, KT * P),
        "odd_par": np.stack([b3[0], b3[1], b3[2], I["conv_b"][0].reshape(CT, P)], -1),
        "conv_w": I["conv_w"][0].reshape(CW, CT, P).transpose(1, 2, 0),
        "conv_in": I["cache_conv"][0].reshape(SB, HALO, CT, P).transpose(2, 3, 0, 1),
        "ln_w": col(I["conv_ln_w"][0]),
        "ln_b": col(I["conv_ln_b"][0]),
        "w_out_odd": tiles(I["w_out_odd"][0]),
        "final_norm": col(I["final_norm"]),
    }
    outs = {
        "yT": (P, KT, T), "shift_out": (13, P, 1 + SB), "rwkv_p_out": (RU, P, C), "rwkv_s_out": (RU, P, SB * C),
        "gla_p_out": (GU, P, P), "gla_s_out": (GU, P, SB * P), "conv_p_out": (CT, P, HALO),
        "conv_s_out": (CT, P, SB, HALO),
    }
    scratch = {"O": (KT, P, T), "X2": (P, KT, T), "SG": (CT, P, T), "Y": (CT, P, T)}
    nc = bacc.Bacc("TRN2", target_bir_lowering=False, num_devices=1)
    A = {}
    for name, a in arrays.items():
        arrays[name] = a = np.ascontiguousarray(a)
        A[name] = nc.dram_tensor("in_" + name, a.shape, F32, kind="ExternalInput").ap()
    for name, shape in outs.items():
        A[name] = nc.dram_tensor("out_" + name, shape, F32, kind="ExternalOutput").ap()
    for name, shape in scratch.items():
        A[name] = nc.dram_tensor("tmp_" + name, shape, F32, kind="Internal").ap()
    build(nc, A)
    res = run(nc, [{"in_" + k: v for k, v in arrays.items()}], core_ids=[0]).results[0]
    R = {k: np.asarray(res["out_" + k]) for k in outs}
    y = R["yT"].transpose(1, 0, 2).reshape(D, T).T
    sh = np.zeros((1 + SB, RPROJ), np.float32)
    for i, a in enumerate(order):
        sh[:, a:a + P] = R["shift_out"][i].T
    rp = R["rwkv_p_out"].reshape(RU, 2, C, C).transpose(0, 1, 3, 2).reshape(1, 1, 8, C, C)
    rsmp = R["rwkv_s_out"].reshape(RU, 2, C, SB, C).transpose(3, 0, 1, 4, 2).reshape(1, SB, 8, C, C)
    gp = R["gla_p_out"].reshape(1, 1, 4, C, P)
    gsmp = R["gla_s_out"].reshape(GU, 2, C, SB, P).transpose(3, 0, 1, 2, 4).reshape(1, SB, 4, C, P)
    cp = R["conv_p_out"].transpose(2, 0, 1).reshape(1, 1, HALO, D)
    csmp = R["conv_s_out"].transpose(2, 3, 0, 1).reshape(1, SB, HALO, D)
    return (y[:SEQ].reshape(1, SEQ, D).copy(), y[SEQ:].reshape(SB, SL, D).copy(), sh[0:1].reshape(1, 1, RPROJ).copy(),
            sh[1:].reshape(1, SB, RPROJ).copy(), rp.copy(), rsmp.copy(), gp.copy(), gsmp.copy(), cp.copy(), csmp.copy())
```

```python
from contextlib import ExitStack
import math

import numpy as np
import concourse.bass as bass
from concourse import mybir

F32 = mybir.dt.float32
ACT = mybir.ActivationFunctionType
ALU = mybir.AluOpType

P = 128
D = 1024
KT = D // P
SEQ = 2048
SB, SL = 8, 4
NS = SB * SL
T = SEQ + NS
BLK = 512
NB = SEQ // BLK
C = 64
NC = BLK // C
RB = 416
NRB = T // RB
HK = 64
RU = 4
GU = 2
CT = KT
CW = 31
HALO = CW - 1
DECAY = math.exp(-0.5)
LN_UP = 30
GN_EPS, RMS_EPS, LN_EPS = 64e-5, 1e-6, 1e-5
RPROJ, GPROJ = 1664, 1040

_COLS = {}
_n = 0
for _name, _w in (("maskA", 128), ("maskAs", 128), ("lvl", 6 * 64), ("lvl1t", 64), ("ident", 128),
                  ("ident2", 64), ("bones", 128), ("ones", 128), ("reset", BLK), ("resets", NS),
                  ("seq", SB), ("maskG", 128), ("maskGs", 128), ("eps", 8)):
    _COLS[_name] = (_n, _n + _w)
    _n += _w
NCONST = _n
R_MUR, R_MUK, R_MUV, R_W0, R_A0, R_KK, R_KA, R_RK, R_LNW, R_LNB = range(10)
G_GB, G_NORM = range(2)
O_BV, O_BG, O_BS, O_CB = range(4)
E_RMS, E_GN, E_LN, E_UP, E_ONE = range(5)


def build(nc, A):
    ctx = ExitStack()
    with ctx:
        def sb(name, *shape):
            return ctx.enter_context(nc.sbuf_tensor(name, list(shape), F32))

        sems = []

        def sem(name):
            s = ctx.enter_context(nc.semaphore(name))
            sems.append(s)
            return s

        ps = [ctx.enter_context(nc.psum_tensor(f"bank{i}", [P, 512], F32)) for i in range(8)]
        PJ, EB, Q = ps[0:2], ps[2:4], ps[4:8]

        def rounds_end():
            nc.gpsimd.sem_clear(range(sems[0].num, sems[-1].num + 1))
            nc.all_engine_barrier()

        K0 = sb("K0", P, NCONST)
        ysum = sb("ysum", P, T)
        hctx = ctx.enter_context(ExitStack())
        H = hctx.enter_context(nc.sbuf_tensor("H", [P, KT, T], F32))

        def cst(name):
            a, b = _COLS[name]
            return K0[:, a:b]

        ident, ident2, bones, ones = cst("ident"), cst("ident2"), cst("bones"), cst("ones")
        eps = cst("eps")

        s_ssum = sem("square_sums_ready")
        s_proj = sem("projection_ready")
        s_lora = sem("lora_ready")
        s_ssq = sem("key_square_sums_ready")
        s_bon = sem("bonus_sums_ready")
        s_A = sem("chunk_products_ready")
        s_tr = sem("transposes_ready")
        s_wv = sem("value_part_ready")
        s_T = sem("inverse_left_ready")
        s_X = sem("inverse_right_ready")
        s_ZS = sem("state_read_ready")
        s_U = sem("removals_ready")
        s_SU = sem("state_change_ready")
        s_Y = sem("outputs_ready")
        s_mean = sem("mean_ready")
        s_var = sem("variance_ready")
        a_sq = sem("squares_done")
        a_ln = sem("log_done")
        a_rs = sem("rstd_done")
        a_ev = sem("projection_evacuated")
        a_halo = sem("halo_moved")
        a_mu = sem("previous_scaled")
        a_sig = sem("sigmoid_done")
        a_exp = sem("decay_exp_done")
        a_kn = sem("key_norm_done")
        a_ka = sem("key_gain_done")
        a_tb = sem("transposes_evacuated")
        a_wv = sem("value_part_evacuated")
        a_y = sem("outputs_evacuated")
        v_h = sem("normalised_done")
        v_mix = sem("mixed")
        v_cs = sem("log_decay_summed")
        v_cl = sem("key_sums_clamped")
        v_kn = sem("key_normalised")
        v_zr = sem("z_and_r_done")
        v_b = sem("b_done")
        v_bp = sem("bonus_product_done")
        v_bv = sem("bonus_done")
        v_M = sem("chunk_products_masked")
        v_x1 = sem("inverse_started")
        v_T = sem("inverse_left_masked")
        v_X = sem("inverse_grown")
        v_W0 = sem("state_read_done")
        v_U = sem("removals_done")
        v_S = sem("state_done")
        v_yc = sem("centred")
        v_o = sem("gated")
        p_set = sem("constants_set")
        p_kp = sem("key_scaled")
        p_ka = sem("key_rate_product_done")
        p_K = sem("k_done")
        p_V = sem("v_placed")
        p_e = sem("chunk_decay_kept")
        p_sh = sem("shift_row_kept")
        a_g = sem("gate_log_steps")
        a_gl = sem("sigmoid_gate_done")
        v_g = sem("gate_input_ready")
        p_u = sem("glu_done")
        p_ys = sem("channel_sum_done")
        v_acc = sem("taps_added")
        s_tap = sem("tensor_taps_added")
        a_dg = sem("tap_diagonals_done")
        v_pr = sem("sample_products_done")
        v_smp = sem("sample_taps_done")
        v_sum = sem("taps_summed")
        d_c = sem("constants_loaded")
        d_x = [sem("x_loaded0"), sem("x_loaded1")]
        d_w = sem("weights_loaded")
        d_p = sem("parameters_loaded")
        d_s = sem("states_loaded")
        d_o = sem("outputs_stored")
        d_o2 = sem("state_stored")
        d_r = sem("residual_loaded")
        d_g = sem("gate_loaded")
        d_sg = [sem("gate_stored0"), sem("gate_stored1")]

        def norm_stage():
            with nc.sbuf_tensor("xin", [P, KT, RB], F32) as xin, \
                    nc.sbuf_tensor("xsq", [P, KT, RB], F32) as xsq, \
                    nc.sbuf_tensor("rst", [P, RB], F32) as rst, \
                    nc.sbuf_tensor("gn", [P, KT], F32) as gn:
                with nc.Block() as block:
                    @block.sync
                    def _(sp):
                        sp.dma_start(K0[:], A["const"]).then_inc(d_c, 16)
                        sp.dma_start(gn[:], A["norm_even"]).then_inc(d_c, 16)
                        sp.wait_ge(d_c, 32)
                rounds_end()
                with nc.Fori(0, NRB) as b:
                    with nc.Block() as block:
                        @block.sync
                        def _(sp):
                            sp.dma_start(xin[:], A["xT"][:, :, bass.ds(b * RB, RB)]).then_inc(d_x[0], 16)

                        @block.scalar
                        def _(act):
                            act.wait_ge(d_x[0], 16)
                            nc.scalar.activation(xsq[:], xin[:], ACT.Square).then_inc(a_sq, 1)
                            act.wait_ge(s_ssum, 1)
                            nc.scalar.activation(rst[:], EB[0][:, 0:RB], ACT.Ln, scale=1.0 / D,
                                                 bias=eps[:, E_RMS:E_RMS + 1]).then_inc(a_ln, 1)
                            act.wait_ge(a_ln, 1)
                            nc.scalar.activation(rst[:], rst[:], ACT.Exp, scale=-0.5).then_inc(a_rs, 1)

                        @block.tensor
                        def _(pe):
                            pe.wait_ge(v_cl, 1)
                            nc.tensor.matmul(EB[0][:, 0:RB], ones, xsq[:, 0, :], start=True, stop=True).then_inc(s_ssum, 1)

                        @block.vector
                        def _(dve):
                            dve.wait_ge(d_x[0], 16)
                            sum_tiles(dve, xsq, 1, v_pr, v_cl)
                            dve.wait_ge(a_rs, 1)
                            for k in range(KT):
                                nc.vector.scalar_tensor_tensor(
                                    H[:, k, bass.ds(b * RB, RB)], xin[:, k, :], gn[:, k:k + 1],
                                    rst[:], ALU.mult, ALU.mult)
                    rounds_end()

        def project(bank, w, t, cols, n, m=P):
            for k in range(KT):
                mm = nc.tensor.matmul(bank[0:m, 0:n], w[:, t, k * P:k * P + m], H[:, k, cols:cols + n],
                                      start=(k == 0), stop=(k == KT - 1))
            return mm

        def sum_tiles(dve, x, squares, halved, done, before=0):
            dve.wait_ge(a_sq, squares)
            w = KT // 2
            while w > 1:
                nc.vector.tensor_tensor(x[:, 0:w, :], x[:, 0:w, :], x[:, w:2 * w, :], ALU.add).then_inc(halved, 1)
                before += 1
                dve.wait_ge(halved, before)
                w //= 2
            nc.vector.tensor_tensor(x[:, 0, :], x[:, 0, :], x[:, 1, :], ALU.add).then_inc(done, 1)
            return before

        COLS = [(b * BLK, BLK) for b in range(NB)] + [(SEQ, NS)]

        def rwkv_stage():
            c1 = ExitStack()
            with c1:
                def sb(name, *shape):
                    return c1.enter_context(nc.sbuf_tensor(name, list(shape), F32))

                W = sb("W", P, 4, D)
                LT = sb("LT", P, T)
                par = sb("rpar", P, 10)
                omm = sb("romm", P, 4)
                LU = sb("LU", P, P)
                raw = [sb(f"raw{i}", P, 1 + BLK) for i in range(3)]
                raws = [sb(f"raws{i}", P, SB, SL + 1) for i in range(3)]
                shr = sb("shr", P, 3, 1 + SB)
                shi = sb("shi", P, 3, SB)
                ZR = [sb(f"ZR{i}", P, NC, 2, C) for i in range(2)] + [sb("ZRs", P, 1, 2, C)]
                BK, BKs = sb("BK", P, NC, 2, C), sb("BKs", P, 1, 2, C)
                VS, VSs = sb("VS", P, NC, 2, C), sb("VSs", P, 1, 2, C)
                M = sb("M", P, 2, NC, P)
                BT = sb("BT", P, NC, P)
                UV = sb("UV", P, NC, 2, C)
                XX = sb("XX", P, 2, 2, 4, C)
                T1 = sb("T1", P, 2, 4, C)
                WV = sb("WV", P, NC, C)
                W0 = sb("W0t", P, C)
                S, Sd = sb("S", P, C), sb("Sd", P, C)
                Ss = sb("Ss", P, SB, C)
                PS = sb("PSs", P, SB, C)
                r, k, v = sb("r", P, BLK), sb("k", P, BLK), sb("v", P, BLK)
                t0, t1, t2 = sb("t0", P, BLK), sb("t1", P, BLK), sb("t2", P, BLK)
                sg, aa, cs = sb("sg", P, BLK), sb("aa", P, BLK), sb("cs", P, BLK)
                eb, enb, ebm = sb("eb", P, BLK), sb("enb", P, BLK), sb("ebm", P, BLK)
                kkn, kp = sb("kkn", P, BLK), sb("kp", P, BLK)
                bv = [sb(f"bv{i}", P, BLK) for i in range(3)]
                gs = [sb(f"gs{i}", P, BLK) for i in range(3)]
                ebC = [sb(f"ebC{i}", P, SB) for i in range(2)]
                ysb = [sb(f"ysb{i}", P, BLK) for i in range(2)]
                yc, rs = sb("yc", P, BLK), sb("rs", P, BLK)

                with nc.Block() as block:
                    LR = M[:, :, :, :].rearrange("p a b c -> p (a b c)")
                    muL, omL = t0[:, 0:1], t0[:, 1:2]
                    shl, stg = t1[:, 0:1 + SB], t1[:, 16:16 + SB]
                    rawL = raws[0]
                    tmp = [t2, sg]

                    @block.sync
                    def _(sp):
                        sp.dma_start(W[:, 0, :], A["w_even"][0]).then_inc(d_w, 16)
                        sp.dma_start(muL, A["mu_lora"]).then_inc(d_p, 16)
                        sp.dma_start(stg, A["shift_in"][12]).then_inc(d_p, 16)
                        sp.wait_ge(p_sh, 2)
                        sp.dma_start(A["shift_out"][12], shl).then_inc(d_o, 16)
                        sp.wait_ge(d_o, 16)

                    @block.gpsimd
                    def _(pool):
                        for z in [*ZR[2:], BKs, VSs, VS, S, BK]:
                            nc.gpsimd.memset(z[:], 0.0)
                        pool.wait_ge(d_p, 32)
                        nc.gpsimd.tensor_copy(rawL[:, :, 0:1].squeeze(2), stg).then_inc(p_set, 1)
                        pool.wait_ge(a_ev, NB + 1)
                        nc.gpsimd.tensor_copy(shl[:, 0:1], LR[:, SEQ - 1:SEQ]).then_inc(p_sh, 1)
                        pool.wait_ge(d_p, 32)
                        nc.gpsimd.tensor_copy(shl[:, 1:1 + SB], rawL[:, :, SL:SL + 1].squeeze(2)).then_inc(p_sh, 1)

                    @block.tensor
                    def _(pe):
                        pe.wait_ge(d_w, 16)
                        for b, (c0, n) in enumerate(COLS):
                            if b >= 2:
                                pe.wait_ge(a_ev, b - 1)
                            project(PJ[b % 2], W, 0, c0, n).then_inc(s_proj, 1)

                    @block.scalar
                    def _(act):
                        for b, (c0, n) in enumerate(COLS):
                            act.wait_ge(s_proj, b + 1)
                            if b < NB:
                                out, src = LR[:, c0:c0 + n], PJ[b % 2][:, 0:n]
                            else:
                                act.wait_ge(d_p, 32)
                                out = rawL[:, :, 1:1 + SL]
                                src = PJ[b % 2][:, 0:n].rearrange("p (s j) -> p s j", j=SL)
                            nc.scalar.activation(out, src, ACT.Copy).then_inc(a_ev, 1)
                        act.wait_ge(v_mix, 1 + 2 * (NB + 1))
                        nc.scalar.activation(LT[0:64, :], LT[0:64, :], ACT.Tanh)

                    @block.vector
                    def _(dve):
                        dve.wait_ge(d_p, 32)
                        nc.vector.tensor_scalar(omL, muL, -1.0, 1.0, ALU.mult, ALU.add).then_inc(v_mix, 1)
                        dve.wait_ge(v_mix, 1)
                        nc.vector.memset(t2[:, 0:1], 0.0).then_inc(v_x1, 1)
                        for b, (c0, n) in enumerate(COLS):
                            dve.wait_ge(a_ev, b + 1)
                            x = tmp[b % 2]
                            if b == NB:
                                dve.wait_ge(p_set, 1)
                            if b < NB:
                                a = 0 if b else 1
                                cur, prev = LR[:, c0:c0 + n], LR[:, c0 + a - 1:c0 + n - 1]
                                if b == 0:
                                    dve.wait_ge(v_x1, 1)
                                nc.vector.tensor_scalar(x[:, a:n], prev, muL, None, ALU.mult).then_inc(v_mix, 1)
                                out, x = LT[:, c0:c0 + n], x[:, 0:n]
                            else:
                                cur, prev = rawL[:, :, 1:1 + SL], rawL[:, :, 0:SL]
                                x = x[:, 0:n].rearrange("p (s j) -> p s j", j=SL)
                                nc.vector.tensor_scalar(x, prev, muL, None, ALU.mult).then_inc(v_mix, 1)
                                out = LT[:, c0:c0 + n].rearrange("p (s j) -> p s j", j=SL)
                            dve.wait_ge(v_mix, 2 + 2 * b)
                            nc.vector.scalar_tensor_tensor(out, cur, omL, x, ALU.mult, ALU.add).then_inc(v_mix, 1)
                rounds_end()
                with nc.Block() as block:
                    @block.sync
                    def _(sp):
                        sp.dma_start(W[:], A["w_even"][2:6].rearrange("t p n -> p t n")).then_inc(d_w, 16)

                    @block.gpsimd
                    def _(pool):
                        for i in range(3):
                            nc.gpsimd.memset(raw[i][:, 0:1], 0.0)

                    @block.tensor
                    def _(pe):
                        pe.wait_ge(d_w, 16)
                        for i in range(4):
                            if i >= 2:
                                pe.wait_ge(a_ev, i - 1)
                            project(PJ[i % 2], W, i, 0, BLK).then_inc(s_proj, 1)

                    @block.scalar
                    def _(act):
                        for i in range(4):
                            act.wait_ge(s_proj, i + 1)
                            if i < 3:
                                nc.scalar.activation(raw[i][:, 1:1 + BLK], PJ[i % 2][:, :], ACT.Copy).then_inc(a_ev, 1)
                            else:
                                nc.scalar.activation(gs[0][:, :], PJ[1][:, :], ACT.Silu).then_inc(a_ev, 1)
                rounds_end()

                with nc.Fori(0, RU) as u:
                    for step in range(NB + 3):
                        rwkv_step(u, step, W, LT, par, omm, LU, raw, raws, shr, shi, ZR, (BK, BKs), (VS, VSs), M, BT,
                                  UV, XX, T1, WV, W0, S, Sd, Ss, PS, r, k, v, (t0, t1, t2), sg, aa, cs, eb, enb,
                                  ebm, kkn, kp, bv, gs, ebC, ysb, yc, rs)

        def rwkv_step(u, step, W, LT, par, omm, LU, raw, raws, shr, shi, ZRb, BKb, VSb, M, BT, UV, XX, T1, WV, W0, S,
                      Sd, Ss, PS, r, k, v, tmps, sg, aa, cs, eb, enb, ebm, kkn, kp, bv, gs, ebC, ysb, yc, rs):
            f = step + 1 if step < NB else 0 if step == NB + 1 else None
            e = step if step <= NB else None
            c = step - 1 if 1 <= step <= NB + 1 else None
            g = step - 2 if step >= 2 else None
            t0, t1, t2 = tmps
            if f is not None:
                f0, nf = COLS[f]
            sample_e, sample_c = e == NB, c == NB
            if e is not None:
                c0, n = COLS[e]
                we, ne = min(C, n), max(1, n // C)
                ZRe, BKe, VSe = ZRb[2 if sample_e else e % 2], BKb[sample_e], VSb[sample_e]

                def ch(x, lo=0, hi=P):
                    return x[lo:hi, 0:n].rearrange("p (c j) -> p c j", j=we)
            if c is not None:
                ZR, BK, VS = ZRb[2 if sample_c else c % 2], BKb[sample_c], VSb[sample_c]
                nch = 1 if sample_c else NC
                grp = [range(0, 1)] if sample_c else [range(0, 4), range(4, 8)]
                G = len(grp)
                levels = 2 if sample_c else 6
                maskA = cst("maskAs" if sample_c else "maskA")
                nT = 2 if sample_c else 4
            halves = [(0, 64), (64, 128)]

            def evacuate(act, i):
                bank = PJ[i % 2]
                act.wait_ge(s_proj, i + 1)
                if i == 3:
                    if g is not None:
                        act.wait_ge(v_o, 3)
                    nc.scalar.activation(gs[f % 3][:, 0:nf], bank[:, 0:nf], ACT.Silu).then_inc(a_ev, 1)
                elif f == NB:
                    nc.scalar.activation(raws[i][:, :, 1:1 + SL],
                                         bank[:, 0:nf].rearrange("p (s j) -> p s j", j=SL), ACT.Copy).then_inc(a_ev, 1)
                else:
                    if f:
                        act.wait_ge(v_mix, MIXED)
                        nc.scalar.activation(raw[i][:, 0:1], raw[i][:, BLK:BLK + 1], ACT.Copy).then_inc(a_halo, 1)
                        act.wait_ge(a_halo, i + 1)
                    nc.scalar.activation(raw[i][:, 1:1 + nf], bank[:, 0:nf], ACT.Copy).then_inc(a_ev, 1)

            def scale_previous(act, i):
                if sample_e:
                    if i == 0:
                        act.wait_ge(d_x[0], 48)
                        for x in range(3):
                            nc.scalar.activation(raws[x][:, :, 0:1].squeeze(2), shi[:, x, :], ACT.Copy).then_inc(a_halo, 1)
                        act.wait_ge(a_halo, 3)
                    prev, dst = raws[i][:, :, 0:SL], tmps[i][:, 0:n].rearrange("p (s j) -> p s j", j=SL)
                else:
                    prev, dst = raw[i][:, 0:n], tmps[i][:, 0:n]
                if step == 0 and i == 0:
                    act.wait_ge(d_p, 32)
                nc.scalar.activation(dst, prev, ACT.Copy, scale=par[:, i:i + 1]).then_inc(a_mu, 1)

            MIXED = 3 + (step == 0)

            def mix(dve, i):
                dst = (r, k, v)[i]
                if sample_e:
                    cur = raws[i][:, :, 1:1 + SL]
                    out, x = (y_[:, 0:n].rearrange("p (s j) -> p s j", j=SL) for y_ in (dst, tmps[i]))
                else:
                    cur, out, x = raw[i][:, 1:1 + n], dst[:, 0:n], tmps[i][:, 0:n]
                dve.wait_ge(a_mu, i + 1)
                nc.vector.scalar_tensor_tensor(out, cur, omm[:, i:i + 1], x, ALU.mult, ALU.add).then_inc(v_mix, 1)

            with nc.Block() as block:
                @block.sync
                def _(sp):
                    if step == 0:
                        sp.dma_start(par[:], A["rwkv_par"][bass.ds(u, 1)].rearrange("u p n -> p (u n)")).then_inc(d_p, 16)
                        sp.dma_start(LU[:], A["lora_up"][:, bass.ds(u * P, P)]).then_inc(d_p, 16)
                    if step == NB:
                        sp.dma_start(W[:], A["w_even"][bass.ds(u * 4 + 6, 4)].rearrange("t p n -> p t n")).then_inc(d_w, 16)
                        sp.dma_start(Ss[:], A["rwkv_in"][bass.ds(u, 1)].rearrange("u p (s v) -> p (u s) v", v=C)).then_inc(d_s, 16)
                    if sample_e:
                        for i in range(3):
                            sp.dma_start(shi[:, i, :], A["shift_in"][bass.ds(u * 3 + i, 1)].rearrange("t p s -> p (t s)")).then_inc(d_x[0], 16)
                        sp.wait_ge(p_sh, 6)
                        for i in range(3):
                            sp.dma_start(A["shift_out"][bass.ds(u * 3 + i, 1)].rearrange("t p s -> p (t s)"),
                                         shr[:, i, :]).then_inc(d_o2, 16)
                        sp.wait_ge(d_s, 16)
                    if step == NB + 1:
                        sp.dma_start(A["rwkv_p_out"][bass.ds(u, 1)].rearrange("u p v -> p (u v)"), S[:]).then_inc(d_o2, 16)
                        sp.wait_ge(v_S, 2)
                        sp.dma_start(A["rwkv_s_out"][bass.ds(u, 1)].rearrange("u p (s v) -> p (u s) v", v=C),
                                     Ss[:]).then_inc(d_o2, 16)
                        sp.wait_ge(d_o2, 32)
                    if g is not None:
                        gc0, gn_ = COLS[g]
                        sp.wait_ge(v_o, 3)
                        sp.dma_start(A["O"][bass.ds(u, 1), :, gc0:gc0 + gn_].rearrange("u p n -> p (u n)"),
                                     rs[:, 0:gn_]).then_inc(d_o, 16)
                        sp.wait_ge(d_o, 16)
                    if sample_e:
                        sp.wait_ge(d_o2, 48)
                        sp.wait_ge(d_w, 16)

                @block.tensor
                def _(pe):
                    LEVEL = 2

                    def part(lo_, hi_):
                        for x in range(lo_, hi_) if f is not None else ():
                            t, k_ = divmod(x, KT)
                            if k_ == 0 and t < 2 and e is not None:
                                pe.wait_ge(a_sig, t + 1)
                            if k_ == 0 and t >= 2:
                                pe.wait_ge(a_ev, t - 1)
                            mm = nc.tensor.matmul(PJ[t % 2][:, 0:nf], W[:, t, k_ * P:(k_ + 1) * P],
                                                  H[:, k_, f0:f0 + nf], start=(k_ == 0), stop=(k_ == KT - 1))
                            if k_ == KT - 1:
                                mm.then_inc(s_proj, 1)

                    if e is not None:
                        if step == 0:
                            pe.wait_ge(d_p, 32)
                        nc.tensor.matmul(PJ[0][:, 0:n], LU[0:64, :], LT[0:64, c0:c0 + n], start=True, stop=True).then_inc(s_lora, 1)
                        nc.tensor.matmul(PJ[1][:, 0:n], LU[64:128, :], LT[64:128, c0:c0 + n], start=True, stop=True).then_inc(s_lora, 1)
                    if g is not None:
                        _, m = COLS[g]
                        nc.tensor.matmul(EB[0][:, 0:m], bones, ysb[g % 2][:, 0:m], start=True, stop=True).then_inc(s_mean, 1)
                    if c is not None:
                        for gi, chunks in enumerate(grp):
                            for h, (lo, hi) in enumerate(halves):
                                for i, q in enumerate(chunks):
                                    mm = nc.tensor.matmul(Q[2 * gi + h][:, i * P:(i + 1) * P], BK[lo:hi, q, :, :],
                                                          ZR[lo:hi, q, :, :], start=True, stop=True)
                                mm.then_inc(s_A, 1)
                        if sample_c:
                            part(0, KT)
                    if g is not None:
                        pe.wait_ge(a_sq, 1)
                        nc.tensor.matmul(EB[1][:, 0:m], bones, yc[:, 0:m], start=True, stop=True).then_inc(s_var, 1)
                    if e is not None:
                        pe.wait_ge(a_kn, 1)
                        if g is not None:
                            pe.wait_ge(v_yc, 1)
                        nc.tensor.matmul(EB[0][:, 0:n], bones, t0[:, 0:n], start=True, stop=True).then_inc(s_ssq, 1)
                    if c is not None:
                        for t, (src, bank) in enumerate([(BK, Q[0]), (BK, Q[1]), (VS, Q[2]), (VS, Q[3])]
                                                        if not sample_c else [(BK, Q[0]), (VS, Q[2])]):
                            pe.wait_ge(v_M, t + 1 if not sample_c else 2)
                            for i, q in enumerate(grp[t % G]):
                                mm = nc.tensor.transpose(bank[:, i * P:(i + 1) * P], src[:, q, :, :], ident)
                            mm.then_inc(s_tr, 1)
                        if not sample_c:
                            part(0, 2)
                        pe.wait_ge(a_tb, nT)
                        for gi, chunks in enumerate(grp):
                            for i, q in enumerate(chunks):
                                for h, (lo, hi) in enumerate(halves):
                                    mm = nc.tensor.matmul(Q[gi][lo:hi, i * C:(i + 1) * C], M[lo:hi, h, q, 0:C],
                                                          ident2[lo:hi, :], start=True, stop=True)
                            mm.then_inc(s_T, 1)
                        for q in range(nch):
                            for h, (lo, hi) in enumerate(halves):
                                ko, ki = halves[1 - h]
                                mm = nc.tensor.matmul(Q[3][lo:hi, q * C:(q + 1) * C], M[ko:ki, h, q, 0:C],
                                                      UV[ko:ki, q, h, :], start=True, stop=True)
                        mm.then_inc(s_wv, 1)
                        if not sample_c:
                            part(2, 4)
                        pe.wait_ge(a_wv, 1)
                        for l in range(2, levels + 1):
                            for gi, chunks in enumerate(grp):
                                pe.wait_ge(v_X, G * (l - 2) + gi + 1)
                                for i, q in enumerate(chunks):
                                    for h, (lo, hi) in enumerate(halves):
                                        mm = nc.tensor.matmul(Q[gi][lo:hi, i * C:(i + 1) * C], M[lo:hi, h, q, 0:C],
                                                              XX[lo:hi, gi, 0, i, :], start=True, stop=True)
                                mm.then_inc(s_T, 1)
                            if not sample_c:
                                part(LEVEL * (l - 2) + 4, LEVEL * (l - 2) + 5)
                            for gi, chunks in enumerate(grp):
                                pe.wait_ge(v_T, G * (l - 2) + gi + 1)
                                for i, q in enumerate(chunks):
                                    for h, (lo, hi) in enumerate(halves):
                                        if l < levels:
                                            nc.tensor.matmul(Q[2 + gi][lo:hi, i * C:(i + 1) * C], XX[lo:hi, gi, 1, i, :],
                                                             T1[lo:hi, gi, i, :], start=True, stop=True)
                                        mm = nc.tensor.matmul(Q[2 + gi][lo:hi, (4 + i) * C:(5 + i) * C], T1[lo:hi, gi, i, :],
                                                              XX[lo:hi, gi, 1, i, :], start=True, stop=True)
                                mm.then_inc(s_X, 1)
                            if not sample_c:
                                part(LEVEL * (l - 2) + 5, LEVEL * (l - 1) + 4 if l < levels else 4 * KT - 2 * NC)
                    if c is None:
                        part(0, 4 * KT)

                    def bonus():
                        pe.wait_ge(v_bp, 1)
                        if g is not None:
                            pe.wait_ge(a_ln, 1)
                        nc.tensor.matmul(EB[1][:, 0:n], bones, t2[:, 0:n], start=True, stop=True).then_inc(s_bon, 1)

                    FROM = 4 * KT - 2 * NC
                    if c is not None and not sample_c:
                        pe.wait_ge(v_X, G * levels)
                        for j in range(NC):
                            if j:
                                pe.wait_ge(v_S, j)
                            for h, (lo, hi) in enumerate(halves):
                                mm = nc.tensor.matmul(Q[0][lo:hi, 0:C], ZR[lo:hi, j, 0, :], S[lo:hi, :], start=True, stop=True)
                            mm.then_inc(s_ZS, 1)
                            part(FROM + 2 * j, FROM + 2 * j + 1)
                            pe.wait_ge(v_W0, j + 1)
                            for h, (lo, hi) in enumerate(halves):
                                mm = nc.tensor.matmul(Q[0][lo:hi, C:2 * C], XX[lo:hi, j // 4, 1, j % 4, :], W0[lo:hi, :],
                                                      start=True, stop=True)
                            mm.then_inc(s_U, 1)
                            for h, (lo, hi) in enumerate(halves):
                                nc.tensor.matmul(Q[1][lo:hi, j * C:(j + 1) * C], S[lo:hi, :], ZR[lo:hi, j, 1, :],
                                                 start=True, stop=False)
                            pe.wait_ge(v_U, 2 * (j + 1))
                            for h, (lo, hi) in enumerate(halves):
                                mm = nc.tensor.matmul(Q[0][lo:hi, 2 * C:3 * C], BT[:, j, lo:hi], UV[:, j, h, :],
                                                      start=True, stop=True)
                            mm.then_inc(s_SU, 1)
                            for h, (lo, hi) in enumerate(halves):
                                mm = nc.tensor.matmul(Q[1][lo:hi, j * C:(j + 1) * C], UV[:, j, h, :], M[:, h, j, C:2 * C],
                                                      start=False, stop=True)
                            if j == NC - 1:
                                mm.then_inc(s_Y, 1)
                            part(FROM + 2 * j + 1, FROM + 2 * j + 2)
                            if e is not None and j == 6:
                                bonus()
                    elif sample_c:
                        pe.wait_ge(v_X, G * levels)
                        for h, (lo, hi) in enumerate(halves):
                            mm = nc.tensor.matmul(Q[0][lo:hi, :], ZR[lo:hi, 0, 0, :], Ss[lo:hi, :, :], start=True, stop=True)
                        mm.then_inc(s_ZS, 1)
                        part(KT, 2 * KT)
                        pe.wait_ge(v_W0, 3)
                        for h, (lo, hi) in enumerate(halves):
                            mm = nc.tensor.matmul(Q[0][lo:hi, 0:C], XX[lo:hi, 0, 1, 0, :], W0[lo:hi, :], start=True, stop=True)
                        mm.then_inc(s_U, 1)
                        for q in range(SB):
                            for h, (lo, hi) in enumerate(halves):
                                nc.tensor.matmul(Q[1][lo:hi, q * SL:(q + 1) * SL], Ss[lo:hi, q, :],
                                                 ZR[lo:hi, 0, 1, q * SL:(q + 1) * SL], start=(q == 0), stop=False,
                                                 skip_group_check=True)
                        pe.wait_ge(v_U, 2)
                        for h, (lo, hi) in enumerate(halves):
                            mm = nc.tensor.matmul(Q[1][lo:hi, 0:NS], UV[:, 0, h, :], M[:, h, 0, C:C + NS], start=False,
                                                  stop=True, skip_group_check=True)
                        mm.then_inc(s_Y, 1)
                        pe.wait_ge(v_b, 2)
                        for h, (lo, hi) in enumerate(halves):
                            mm = nc.tensor.matmul(Q[2][lo:hi, :], BT[:, 0, lo:hi], (eb, enb)[h][:, :], start=True, stop=True)
                        mm.then_inc(s_SU, 1)
                        part(2 * KT, 4 * KT)
                    elif e is not None:
                        bonus()

                @block.scalar
                def _(act):
                    if g is not None:
                        _, m = COLS[g]
                    if e is not None:
                        for i in range(3):
                            scale_previous(act, i)
                        for i, (dst, col) in enumerate([(sg, R_W0), (aa, R_A0)]):
                            act.wait_ge(s_lora, i + 1)
                            nc.scalar.activation(dst[:, 0:n], PJ[i][:, 0:n], ACT.Sigmoid,
                                                 bias=par[:, col:col + 1]).then_inc(a_sig, 1)
                    if g is not None:
                        act.wait_ge(v_yc, 1)
                        nc.scalar.activation(yc[:, 0:m], ysb[g % 2][:, 0:m], ACT.Square).then_inc(a_sq, 1)
                    if e is not None:
                        act.wait_ge(v_mix, MIXED)
                        nc.scalar.activation(t0[:, 0:n], k[:, 0:n], ACT.Square, scale=par[:, R_KK:R_KK + 1]).then_inc(a_kn, 1)
                    if c is not None:
                        for t in range(nT):
                            bank = Q[t] if not sample_c else Q[2 * t]
                            wide = len(grp[0]) * P
                            act.wait_ge(s_tr, t + 1)
                            q0 = grp[t % G][0]
                            if t < G:
                                out = BT[:, q0:q0 + len(grp[0]), :]
                                src = bank[:, 0:wide].rearrange("p (c j) -> p c j", j=P)
                            else:
                                out = UV[:, q0:q0 + len(grp[0]), :, :]
                                src = bank[:, 0:wide].rearrange("p (c h j) -> p c h j", h=2, j=C)
                            nc.scalar.activation(out, src, ACT.Copy).then_inc(a_tb, 1)
                    if g is not None:
                        act.wait_ge(s_var, 1)
                        nc.scalar.activation(rs[:, 0:m], EB[1][:, 0:m], ACT.Ln, scale=1.0 / HK,
                                             bias=eps[:, E_GN:E_GN + 1]).then_inc(a_ln, 1)
                        act.wait_ge(a_ln, 1)
                        nc.scalar.activation(rs[:, 0:m], rs[:, 0:m], ACT.Exp, scale=-0.5).then_inc(a_rs, 1)
                    if c is not None:
                        act.wait_ge(s_wv, 1)
                        nc.scalar.activation(WV[:, 0:nch, :], Q[3][:, 0:nch * C].rearrange("p (c j) -> p c j", j=C),
                                             ACT.Copy).then_inc(a_wv, 1)
                    if e is not None:
                        act.wait_ge(v_cs, 1)
                        nc.scalar.activation(eb[:, 0:n], cs[:, 0:n], ACT.Exp, scale=-DECAY).then_inc(a_exp, 1)
                        nc.scalar.activation(enb[:, 0:n], cs[:, 0:n], ACT.Exp, scale=DECAY).then_inc(a_exp, 1)
                        act.wait_ge(v_cs, 2)
                        nc.scalar.activation(ebm[:, 0:n], sg[:, 0:n], ACT.Exp, scale=-DECAY).then_inc(a_exp, 1)
                        act.wait_ge(v_cl, 1)
                        act.wait_ge(a_sig, 2)
                        nc.scalar.activation(t1[:, 0:n], t1[:, 0:n], ACT.Ln, scale=2.0 ** LN_UP).then_inc(a_kn, 1)
                        nc.scalar.activation(t0[:, 0:n], aa[:, 0:n], ACT.Identity, scale=par[:, R_KA:R_KA + 1],
                                             bias=omm[:, 3:4]).then_inc(a_ka, 1)
                        act.wait_ge(a_kn, 2)
                        nc.scalar.activation(t1[:, 0:n], t1[:, 0:n], ACT.Exp, scale=-0.5,
                                             bias=eps[:, E_UP:E_UP + 1]).then_inc(a_kn, 1)
                    if f is not None and not sample_c:
                        for i in range(4):
                            evacuate(act, i)
                    if c is not None:
                        cn = COLS[c][1]
                        act.wait_ge(s_Y, 1)
                        nc.scalar.activation(ysb[c % 2][:, 0:cn], Q[1][:, 0:cn], ACT.Copy).then_inc(a_y, 1)
                    if f is not None and sample_c:
                        for i in range(4):
                            evacuate(act, i)

                @block.vector
                def _(dve):
                    def normalise():
                        if g is None:
                            return
                        y = ysb[g % 2][:, 0:m]
                        dve.wait_ge(a_rs, 1)
                        nc.vector.tensor_tensor(y, y, rs[:, 0:m], ALU.mult).then_inc(v_o, 1)
                        dve.wait_ge(v_o, 1)
                        nc.vector.scalar_tensor_tensor(y, y, par[:, R_LNW:R_LNW + 1], bv[g % 3][:, 0:m], ALU.mult,
                                                       ALU.add).then_inc(v_o, 1)
                        dve.wait_ge(v_o, 2)
                        nc.vector.scalar_tensor_tensor(rs[:, 0:m], y, par[:, R_LNB:R_LNB + 1], gs[g % 3][:, 0:m], ALU.add,
                                                       ALU.mult).then_inc(v_o, 1)

                    def own(j):
                        if e is None:
                            return
                        if j == 1:
                            dve.wait_ge(s_ssq, 1)
                            nc.vector.tensor_scalar(t1[:, 0:n], EB[0][:, 0:n], 1e-24, None, ALU.max).then_inc(v_cl, 1)
                        if j == 2:
                            dve.wait_ge(a_kn, 3)
                            nc.vector.scalar_tensor_tensor(kkn[:, 0:n], k[:, 0:n], par[:, R_KK:R_KK + 1], t1[:, 0:n],
                                                           ALU.mult, ALU.mult).then_inc(v_kn, 1)
                        if j == 3:
                            dve.wait_ge(a_exp, 3)
                            dve.wait_ge(v_kn, 1)
                            nc.vector.tensor_tensor(ZRe[:, 0:ne, 0, 0:we], ch(kkn), ch(ebm), ALU.mult).then_inc(v_zr, 1)
                            nc.vector.tensor_tensor(ZRe[:, 0:ne, 1, 0:we], ch(r), ch(eb), ALU.mult).then_inc(v_zr, 1)
                        if j == 4:
                            dve.wait_ge(p_kp, 1)
                            dve.wait_ge(v_cl, 1)
                            nc.vector.scalar_tensor_tensor(t2[:, 0:n], r[:, 0:n], par[:, R_RK:R_RK + 1], kp[:, 0:n],
                                                           ALU.mult, ALU.mult).then_inc(v_bp, 1)
                        if j == 5:
                            if c is not None and not sample_e:
                                dve.wait_ge(s_tr, nT)
                            dve.wait_ge(p_ka, 1)
                            for h, (lo, hi) in enumerate(halves):
                                nc.vector.scalar_tensor_tensor(BKe[lo:hi, 0:ne, h, 0:we], ch(aa, lo, hi), -1.0,
                                                               ch(enb, lo, hi), ALU.mult, ALU.mult).then_inc(v_b, 1)
                        if j == 6:
                            dve.wait_ge(s_bon, 1)
                            nc.vector.tensor_tensor(bv[e % 3][:, 0:n], EB[1][:, 0:n], v[:, 0:n], ALU.mult).then_inc(v_bv, 1)

                    def decays():
                        dve.wait_ge(a_sig, 1)
                        rm = cst("resets" if sample_e else "reset")
                        nc.vector.tensor_tensor_scan(cs[:, 0:n], rm, sg[:, 0:n], 0.0, ALU.mult, ALU.add).then_inc(v_cs, 1)
                        dve.wait_ge(v_cs, 1)
                        nc.vector.tensor_tensor(sg[:, 0:n], cs[:, 0:n], sg[:, 0:n], ALU.subtract).then_inc(v_cs, 1)

                    if step == 0:
                        dve.wait_ge(d_p, 32)
                        nc.vector.tensor_scalar(omm[:, 0:3], par[:, 0:3], -1.0, 1.0, ALU.mult, ALU.add)
                        nc.vector.tensor_scalar(omm[:, 3:4], par[:, R_KA:R_KA + 1], -1.0, 1.0, ALU.mult,
                                                ALU.add).then_inc(v_mix, 1)
                        dve.wait_ge(v_mix, 1)
                    if e is not None:
                        for i in range(3):
                            mix(dve, i)
                    if g is not None:
                        _, m = COLS[g]
                        y = ysb[g % 2][:, 0:m]
                        dve.wait_ge(s_mean, 1)
                        nc.vector.scalar_tensor_tensor(y, EB[0][:, 0:m], -1.0 / HK, y, ALU.mult, ALU.add).then_inc(v_yc, 1)
                    if e is not None:
                        decays()
                    if c is not None:
                        for i in range(2 * G):
                            h, chunks = i % 2, grp[i // 2]
                            L = len(chunks)
                            dve.wait_ge(s_A, i + 1)
                            nc.vector.tensor_tensor(M[:, h, chunks[0]:chunks[0] + L, :],
                                                    Q[i][:, 0:L * P].rearrange("p (c j) -> p c j", j=P),
                                                    maskA.unsqueeze(1).to_broadcast([P, L, P]), ALU.mult).then_inc(v_M, 1)
                        dve.wait_ge(v_M, 2 * G)
                        lvl = cst("lvl")
                        for gi, chunks in enumerate(grp):
                            L, q0 = len(chunks), chunks[0]
                            for h, (lo, hi) in enumerate(halves):
                                nc.vector.tensor_tensor(XX[lo:hi, gi, 1, 0:L, :], M[lo:hi, h, q0:q0 + L, 0:C],
                                                        cst("lvl1t")[lo:hi, :].unsqueeze(1).to_broadcast([C, L, C]),
                                                        ALU.mult).then_inc(v_x1, 1)
                            dve.wait_ge(s_T, gi + 1)
                            nc.vector.tensor_tensor(XX[:, gi, 0, 0:L, :], Q[gi][:, 0:L * C].rearrange("p (c j) -> p c j", j=C),
                                                    lvl[:, 0:C].unsqueeze(1).to_broadcast([P, L, C]),
                                                    ALU.mult).then_inc(v_x1, 1)
                            dve.wait_ge(v_x1, 3 * gi + 3)
                            nc.vector.tensor_tensor(XX[:, gi, :, 0:L, :], XX[:, gi, :, 0:L, :],
                                                    ident2.unsqueeze(1).unsqueeze(1).to_broadcast([P, 2, L, C]),
                                                    ALU.add).then_inc(v_X, 1)

                    if c is not None:
                        for l in range(2, levels + 1):
                            for gi, chunks in enumerate(grp):
                                L = len(chunks)
                                dve.wait_ge(s_T, G * (l - 1) + gi + 1)
                                nc.vector.tensor_tensor(T1[:, gi, 0:L, :], Q[gi][:, 0:L * C].rearrange("p (c j) -> p c j", j=C),
                                                        lvl[:, (l - 1) * C:l * C].unsqueeze(1).to_broadcast([P, L, C]),
                                                        ALU.mult).then_inc(v_T, 1)
                            own(l - 2)
                            for gi, chunks in enumerate(grp):
                                L = len(chunks)
                                x0 = 0 if l < levels else 1
                                dve.wait_ge(s_X, G * (l - 2) + gi + 1)
                                pq = Q[2 + gi].rearrange("p (x c j) -> p x c j", x=2, j=C)[:, x0:2, 0:L, :]
                                nc.vector.tensor_tensor(XX[:, gi, x0:2, 0:L, :], pq, XX[:, gi, x0:2, 0:L, :],
                                                        ALU.add).then_inc(v_X, 1)
                            if l == 2:
                                normalise()
                    else:
                        if g is not None:
                            normalise()

                    if c is not None and not sample_c:
                        dve.wait_ge(a_wv, 1)
                        ec = ebC[c % 2]
                        for j in range(NC):
                            dve.wait_ge(s_ZS, j + 1)
                            nc.vector.tensor_tensor(W0[:], Q[0][:, 0:C], WV[:, j, :], ALU.add).then_inc(v_W0, 1)
                            if j:
                                dve.wait_ge(v_S, j)
                            nc.vector.tensor_scalar(Sd[:], S[:], ec[:, j:j + 1], None, ALU.mult).then_inc(v_x1, 1)
                            dve.wait_ge(s_U, j + 1)
                            for h, (lo, hi) in enumerate(halves):
                                nc.vector.tensor_copy(UV[lo:hi, j, h, :], Q[0][lo:hi, C:2 * C]).then_inc(v_U, 1)
                            dve.wait_ge(s_SU, j + 1)
                            dve.wait_ge(v_x1, 3 * G + j + 1)
                            nc.vector.scalar_tensor_tensor(S[:], Q[0][:, 2 * C:3 * C], ec[:, j:j + 1], Sd[:], ALU.mult,
                                                           ALU.add).then_inc(v_S, 1)
                            if j >= 6:
                                own(j - 1)
                    elif sample_c:
                        seq = cst("seq")
                        dve.wait_ge(s_ZS, 1)
                        nc.vector.tensor_tensor(PS[:], Q[0].rearrange("p (s v) -> p s v", v=C),
                                                seq.unsqueeze(2).to_broadcast([P, SB, C]), ALU.mult).then_inc(v_W0, 1)
                        dve.wait_ge(v_W0, 1)
                        nc.vector.tensor_reduce(W0[:], PS[:].rearrange("p s v -> p v s"), mybir.AxisListType.X,
                                                ALU.add).then_inc(v_W0, 1)
                        dve.wait_ge(v_W0, 2)
                        dve.wait_ge(a_wv, 1)
                        nc.vector.tensor_tensor(W0[:], W0[:], WV[:, 0, :], ALU.add).then_inc(v_W0, 1)
                        dve.wait_ge(s_U, 1)
                        for h, (lo, hi) in enumerate(halves):
                            nc.vector.tensor_copy(UV[lo:hi, 0, h, :], Q[0][lo:hi, 0:C]).then_inc(v_U, 1)
                        dve.wait_ge(v_U, 2)
                        for h in range(2):
                            nc.vector.tensor_tensor((eb, enb)[h][:, :].rearrange("p (s v) -> p s v", v=C),
                                                    UV[:, 0, h, :].unsqueeze(1).to_broadcast([P, SB, C]),
                                                    seq.unsqueeze(2).to_broadcast([P, SB, C]), ALU.mult).then_inc(v_b, 1)
                        dve.wait_ge(s_SU, 1)
                        nc.vector.tensor_tensor(Ss[:], Q[2].rearrange("p (s v) -> p s v", v=C), Ss[:], ALU.add).then_inc(v_S, 1)
                        dve.wait_ge(v_S, 1)
                        nc.vector.tensor_tensor(Ss[:], Ss[:], ebC[0][:, :].unsqueeze(2).to_broadcast([P, SB, C]),
                                                ALU.mult).then_inc(v_S, 1)
                    else:
                        for j in range(7):
                            own(j)

                @block.gpsimd
                def _(pool):
                    if step == 0:
                        nc.gpsimd.memset(S[:], 0.0)
                    if e is None:
                        return
                    if sample_e:
                        for i in range(3):
                            nc.gpsimd.memset(raw[i][:, 0:1], 0.0)
                    pool.wait_ge(v_mix, MIXED)
                    if c is not None and not sample_e:
                        pool.wait_ge(s_tr, nT)
                    for h, (lo, hi) in enumerate(halves):
                        nc.gpsimd.tensor_copy(VSe[lo:hi, 0:ne, 1 - h, 0:we], ch(v, lo, hi)).then_inc(p_V, 1)
                        pool.wait_ge(p_V, h + 1)
                    if e == NB - 1 or sample_e:
                        for i in range(3):
                            if not sample_e:
                                nc.gpsimd.tensor_copy(shr[:, i, 0:1], raw[i][:, BLK:BLK + 1]).then_inc(p_sh, 1)
                            else:
                                nc.gpsimd.tensor_copy(shr[:, i, 1:1 + SB], raws[i][:, :, SL:SL + 1].squeeze(2)).then_inc(p_sh, 2)
                    pool.wait_ge(a_exp, 2)
                    last = eb[:, 0:n].rearrange("p (s j) -> p s j", j=SL if sample_e else C)[:, :, -1:].squeeze(2)
                    nc.gpsimd.tensor_copy(ebC[e % 2][:, :], last).then_inc(p_e, 1)
                    pool.wait_ge(a_ka, 1)
                    nc.gpsimd.tensor_tensor(kp[:, 0:n], k[:, 0:n], t0[:, 0:n], ALU.mult).then_inc(p_kp, 1)
                    pool.wait_ge(p_kp, 1)
                    for h, (lo, hi) in enumerate(halves):
                        nc.gpsimd.tensor_tensor(BKe[lo:hi, 0:ne, 1 - h, 0:we], ch(kp, lo, hi), ch(enb, lo, hi),
                                                ALU.mult).then_inc(p_K, 1)
                        pool.wait_ge(p_K, h + 1)
                    pool.wait_ge(v_kn, 1)
                    nc.gpsimd.tensor_tensor(aa[:, 0:n], kkn[:, 0:n], aa[:, 0:n], ALU.mult).then_inc(p_ka, 1)
            rounds_end()

        def gla_stage():
            c1 = ExitStack()
            with c1:
                def sb(name, *shape):
                    return c1.enter_context(nc.sbuf_tensor(name, list(shape), F32))

                B = {
                    "W": sb("gW", P, 6, D), "GD": sb("GD", 16, T), "par": sb("gpar", P, 2), "GL": sb("GL", 16, P),
                    "q": sb("gq", P, BLK), "k": sb("gk", P, BLK),
                    "QG": [sb(f"QG{i}", P, BLK) for i in range(2)] + [sb("QGs", P, P)],
                    "KG": [sb(f"KG{i}", P, BLK) for i in range(2)] + [sb("KGs", P, P)],
                    "V": [[sb(f"V{i}{h}", P, BLK) for h in range(2)] for i in range(2)] + [[sb(f"Vs{h}", P, P) for h in range(2)]],
                    "gs": [[sb(f"gg{i}{h}", P, BLK) for h in range(2)] for i in range(3)],
                    "x": sb("gx", P, BLK), "la": sb("gla", P, BLK), "cs": sb("gcs", P, BLK),
                    "eb": sb("geb", P, BLK), "enb": sb("genb", P, BLK), "ebC": [sb(f"gebC{i}", P, SB) for i in range(2)],
                    "AT": sb("AT", P, 2, 4, P), "KT": sb("KTt", P, 4, P), "VT": [sb(f"VT{h}", P, 4, P) for h in range(2)],
                    "Sh": sb("Sh", P, NC + 1, P), "Sg": sb("Sg", P, SB, P), "VM": sb("VM", 64, 2, SB, P),
                    "o": [sb(f"osb{h}", P, BLK) for h in range(2)], "sq": [sb(f"osq{h}", P, BLK) for h in range(2)],
                    "rs": [sb(f"ors{h}", P, BLK) for h in range(2)],
                }
                W, GD = B["W"], B["GD"]
                with nc.Block() as block:
                    @block.sync
                    def _(sp):
                        sp.dma_start(W[:, 0, :], A["w_even"][1]).then_inc(d_p, 16)
                        sp.wait_ge(s_proj, NB + 1)
                        sp.dma_start(W[:], A["w_even"][18:24].rearrange("t p n -> p t n")).then_inc(d_w, 16)
                        sp.wait_ge(d_w, 16)

                    @block.gpsimd
                    def _(pool):
                        for z in (B["QG"][2], B["KG"][2], *B["V"][2]):
                            nc.gpsimd.memset(z[:], 0.0)

                    @block.tensor
                    def _(pe):
                        pe.wait_ge(d_p, 16)
                        for b, (c0, n) in enumerate(COLS):
                            if b >= 2:
                                pe.wait_ge(a_ev, b - 1)
                            project(PJ[b % 2], W, 0, c0, n, 16).then_inc(s_proj, 1)

                    @block.scalar
                    def _(act):
                        for b, (c0, n) in enumerate(COLS):
                            act.wait_ge(s_proj, b + 1)
                            nc.scalar.activation(GD[:, c0:c0 + n], PJ[b % 2][0:16, 0:n], ACT.Copy).then_inc(a_ev, 1)
                rounds_end()
                with nc.Fori(0, GU) as u:
                    for step in range(NB + 3):
                        gla_step(u, step, B)

        def gla_step(u, step, B):
            W, GD, par, GL, Sh, Sg, AT, KT_, VT, VM = (B[x] for x in ("W", "GD", "par", "GL", "Sh", "Sg", "AT", "KT", "VT", "VM"))
            q, k, x, la, cs, eb, enb, o, sq, rs = (B[y] for y in ("q", "k", "x", "la", "cs", "eb", "enb", "o", "sq", "rs"))
            e = step if step <= NB else None
            c = step - 1 if 1 <= step <= NB + 1 else None
            g = step - 2 if step >= 2 else None
            sample_e, sample_c = e == NB, c == NB
            if e is not None:
                c0, n = COLS[e]
                bi = 2 if sample_e else e % 2
                QGe, KGe, Ve, gse = B["QG"][bi], B["KG"][bi], B["V"][bi], B["gs"][e % 3]
            if c is not None:
                ci = 2 if sample_c else c % 2
                QG, KG, V = B["QG"][ci], B["KG"][ci], B["V"][ci]
                pairs = 1 if sample_c else NC // 2
                wide = pairs * P
                cn = COLS[c][1]
            if g is not None:
                gc0, m = COLS[g]
            halves = [(0, 64), (64, 128)]

            def by_pair(t):
                return t[:, 0:wide].rearrange("p (c j) -> p c j", j=P)

            with nc.Block() as block:
                @block.sync
                def _(sp):
                    if step == 0:
                        sp.dma_start(GL[:], A["gla_up"][:, bass.ds(u * P, P)]).then_inc(d_p, 16)
                        sp.dma_start(par[:], A["gla_par"][bass.ds(u, 1)].rearrange("u p n -> p (u n)")).then_inc(d_p, 16)
                    if step == NB:
                        sp.dma_start(Sg[:], A["gla_in"][bass.ds(u, 1)].rearrange("u p (s v) -> p (u s) v", v=P)).then_inc(d_s, 16)
                        sp.wait_ge(d_s, 16)
                    if step == NB + 1:
                        sp.dma_start(W[:], A["w_even"][24:30].rearrange("t p n -> p t n")).then_inc(d_w, 16)
                        sp.dma_start(A["gla_p_out"][bass.ds(u, 1)].rearrange("u p v -> p (u v)"), Sh[:, NC, :]).then_inc(d_o2, 16)
                        sp.wait_ge(v_S, 2)
                        sp.dma_start(A["gla_s_out"][bass.ds(u, 1)].rearrange("u p (s v) -> p (u s) v", v=P), Sg[:]).then_inc(d_o2, 16)
                        sp.wait_ge(d_w, 16)
                        sp.wait_ge(d_o2, 32)
                    if g is not None:
                        for h in range(2):
                            sp.wait_ge(v_o, 2 * h + 2)
                            sp.dma_start(A["O"][bass.ds(4 + 2 * u + h, 1), :, gc0:gc0 + m].rearrange("u p n -> p (u n)"),
                                         rs[h][:, 0:m]).then_inc(d_o, 16)
                        sp.wait_ge(d_o, 32)

                @block.tensor
                def _(pe):
                    if e is not None:
                        if step == 0:
                            pe.wait_ge(d_p, 32)
                        nc.tensor.matmul(EB[0][:, 0:n], GL[:, :], GD[:, c0:c0 + n], start=True, stop=True).then_inc(s_lora, 1)
                    if c is not None:
                        for h, (lo, hi) in enumerate(halves):
                            for p in range(pairs):
                                mm = nc.tensor.matmul(Q[h][:, p * P:(p + 1) * P], KG[lo:hi, p * P:(p + 1) * P],
                                                      QG[lo:hi, p * P:(p + 1) * P], start=True, stop=True)
                            mm.then_inc(s_A, 1)
                    if e is not None:
                        project(PJ[0], W, 0, c0, n).then_inc(s_proj, 1)
                    if c is not None:
                        for t, (src, bank) in enumerate(((KG, Q[2]), (V[0], Q[3]), (V[1], Q[0]))):
                            if t == 2:
                                pe.wait_ge(v_M, 1)
                            for p in range(pairs):
                                mm = nc.tensor.transpose(bank[:, p * P:(p + 1) * P], src[:, p * P:(p + 1) * P], ident)
                            mm.then_inc(s_tr, 1)
                    if g is not None:
                        pe.wait_ge(a_sq, 2)
                        nc.tensor.matmul(EB[1][:, 0:m], ones, sq[0][:, 0:m], start=True, stop=True).then_inc(s_ssq, 1)
                        if e is not None:
                            pe.wait_ge(v_g, 1)
                        nc.tensor.matmul(EB[0][:, 0:m], ones, sq[1][:, 0:m], start=True, stop=True).then_inc(s_ssq, 1)
                    if e is not None:
                        project(PJ[1], W, 1, c0, n).then_inc(s_proj, 1)
                    if c is not None:
                        pe.wait_ge(a_tb, 3)
                        pe.wait_ge(v_M, 2)
                        if not sample_c:
                            for par_, bank in enumerate((Q[1], Q[2])):
                                rl, rh = halves[par_]
                                for p in range(pairs):
                                    for h, (lo, hi) in enumerate(halves):
                                        mm = nc.tensor.matmul(bank[lo:hi, p * P:(p + 1) * P], KT_[rl:rh, p, lo:hi],
                                                              VT[h][rl:rh, p, :], start=True, stop=True)
                                mm.then_inc(s_SU, 1)
                        else:
                            pe.wait_ge(v_b, 2)
                            for i, bank in enumerate((Q[1], Q[2])):
                                for h, (lo, hi) in enumerate(halves):
                                    mm = nc.tensor.matmul(bank[lo:hi, :], KT_[0:64, 0, lo:hi], VM[:, h, 4 * i:4 * i + 4, :],
                                                          start=True, stop=True)
                                mm.then_inc(s_SU, 1)
                    if e is not None:
                        for t in (2, 3):
                            pe.wait_ge(a_ev, t - 1)
                            project(PJ[t % 2], W, t, c0, n).then_inc(s_proj, 1)
                    if c is not None:
                        if not sample_c:
                            pe.wait_ge(v_S, 1 + 2 * (NC - 1))
                        for h, (lo, hi) in enumerate(halves):
                            bank = (Q[3], Q[0])[h]
                            if sample_c:
                                nc.tensor.matmul(bank[:, 0:NS], VT[h][:, 0, :], AT[:, h, 0, 0:NS], start=True,
                                                 stop=False, skip_group_check=True)
                                for s_ in range(SB):
                                    a = s_ * SL
                                    mm = nc.tensor.matmul(bank[:, a:a + SL], Sg[lo:hi, s_, :], QG[lo:hi, a:a + SL],
                                                          start=False, stop=True, skip_group_check=True)
                            else:
                                for p in range(pairs):
                                    nc.tensor.matmul(bank[:, p * P:(p + 1) * P], VT[h][:, p, :], AT[:, h, p, :],
                                                     start=True, stop=False, skip_group_check=True)
                                    for j in (2 * p, 2 * p + 1):
                                        mm = nc.tensor.matmul(bank[:, j * C:(j + 1) * C], Sh[lo:hi, j, :], QG[lo:hi, j * C:(j + 1) * C],
                                                              start=False, stop=True, skip_group_check=True)
                            mm.then_inc(s_Y, 1)
                    if e is not None:
                        for t in (4, 5):
                            pe.wait_ge(a_ev, t - 1)
                            project(PJ[t % 2], W, t, c0, n).then_inc(s_proj, 1)

                @block.scalar
                def _(act):
                    def evacuate(t, out, func=ACT.Copy, **kw):
                        act.wait_ge(s_proj, t + 1)
                        nc.scalar.activation(out, PJ[t % 2][:, 0:n], func, **kw).then_inc(a_ev, 1)

                    if g is not None:
                        for h in range(2):
                            nc.scalar.activation(sq[h][:, 0:m], o[h][:, 0:m], ACT.Square).then_inc(a_sq, 1)
                    if e is not None:
                        act.wait_ge(v_g, 2)
                        nc.scalar.activation(la[:, 0:n], la[:, 0:n], ACT.Exp, scale=-1.0).then_inc(a_g, 1)
                        act.wait_ge(a_g, 1)
                        nc.scalar.activation(la[:, 0:n], la[:, 0:n], ACT.Ln, bias=eps[:, E_ONE:E_ONE + 1]).then_inc(a_g, 1)
                        evacuate(0, q[:, 0:n], scale=C ** -0.5)
                    if c is not None:
                        for t, (dst, bank) in enumerate(((KT_, Q[2]), (VT[0], Q[3]), (VT[1], Q[0]))):
                            act.wait_ge(s_tr, t + 1)
                            nc.scalar.activation(dst[:, 0:pairs, :], by_pair(bank), ACT.Copy).then_inc(a_tb, 1)
                    if e is not None:
                        evacuate(1, k[:, 0:n])
                    if g is not None:
                        for h in range(2):
                            act.wait_ge(s_ssq, h + 1)
                            nc.scalar.activation(rs[h][:, 0:m], EB[1 - h][:, 0:m], ACT.Ln, scale=1.0 / P,
                                                 bias=eps[:, E_RMS:E_RMS + 1]).then_inc(a_ln, 1)
                        for h in range(2):
                            act.wait_ge(a_ln, h + 1)
                            nc.scalar.activation(rs[h][:, 0:m], rs[h][:, 0:m], ACT.Exp, scale=-0.5).then_inc(a_rs, 1)
                    if e is not None:
                        act.wait_ge(v_cs, 1)
                        nc.scalar.activation(eb[:, 0:n], cs[:, 0:n], ACT.Exp, scale=1.0 / 16).then_inc(a_exp, 1)
                        nc.scalar.activation(enb[:, 0:n], cs[:, 0:n], ACT.Exp, scale=-1.0 / 16).then_inc(a_exp, 1)
                        for h in range(2):
                            evacuate(2 + h, Ve[h][:, 0:n])
                    if c is not None:
                        for h in range(2):
                            act.wait_ge(s_Y, h + 1)
                            if g is not None:
                                act.wait_ge(v_o, 2 * h + 1)
                            nc.scalar.activation(o[h][:, 0:cn], (Q[3], Q[0])[h][:, 0:cn], ACT.Copy).then_inc(a_y, 1)
                    if e is not None:
                        for h in range(2):
                            evacuate(4 + h, gse[h][:, 0:n], ACT.Silu)

                @block.vector
                def _(dve):
                    if e is not None:
                        dve.wait_ge(s_lora, 1)
                        if step == 0:
                            dve.wait_ge(d_p, 32)
                        nc.vector.tensor_scalar(x[:, 0:n], EB[0][:, 0:n], par[:, G_GB:G_GB + 1], None, ALU.add).then_inc(v_g, 1)
                        dve.wait_ge(v_g, 1)
                        nc.vector.scalar_tensor_tensor(la[:, 0:n], x[:, 0:n], -1.0, x[:, 0:n], ALU.mult, ALU.max).then_inc(v_g, 1)
                    if c is not None:
                        mg = cst("maskGs" if sample_c else "maskG")
                        for h in range(2):
                            dve.wait_ge(s_A, h + 1)
                            nc.vector.tensor_tensor(AT[:, h, 0:pairs, :], by_pair(Q[h]),
                                                    mg.unsqueeze(1).to_broadcast([P, pairs, P]), ALU.mult).then_inc(v_M, 1)
                    if e is not None:
                        dve.wait_ge(a_g, 2)
                        nc.vector.scalar_tensor_tensor(x[:, 0:n], x[:, 0:n], 0.0, la[:, 0:n], ALU.min, ALU.subtract).then_inc(v_g, 1)
                        dve.wait_ge(v_g, 3)
                        rm = cst("resets" if sample_e else "reset")
                        nc.vector.tensor_tensor_scan(cs[:, 0:n], rm, x[:, 0:n], 0.0, ALU.mult, ALU.add).then_inc(v_cs, 1)
                    if c is not None and not sample_c:
                        if c == 0:
                            nc.vector.memset(Sh[:, 0, :], 0.0).then_inc(v_S, 1)
                        else:
                            nc.vector.tensor_copy(Sh[:, 0, :], Sh[:, NC, :]).then_inc(v_S, 1)
                        ec = B["ebC"][c % 2]
                        dve.wait_ge(s_SU, 2)
                        for j in range(NC):
                            dve.wait_ge(v_S, 1 + 2 * j)
                            nc.vector.tensor_tensor(Sh[:, j + 1, :], Q[1 + j % 2][:, (j // 2) * P:(j // 2 + 1) * P], Sh[:, j, :],
                                                    ALU.add).then_inc(v_S, 1)
                            dve.wait_ge(v_S, 2 + 2 * j)
                            nc.vector.tensor_scalar(Sh[:, j + 1, :], Sh[:, j + 1, :], ec[:, j:j + 1], None, ALU.mult).then_inc(v_S, 1)
                    if sample_c:
                        dve.wait_ge(a_tb, 3)
                        for h in range(2):
                            nc.vector.tensor_tensor(VM[:, h, :, :], VT[h][0:64, 0, :].unsqueeze(1).to_broadcast([64, SB, P]),
                                                    cst("seq")[0:64, :].unsqueeze(2).to_broadcast([64, SB, P]),
                                                    ALU.mult).then_inc(v_b, 1)
                        dve.wait_ge(s_SU, 2)
                        dve.wait_ge(s_Y, 2)
                        for i in range(2):
                            nc.vector.tensor_tensor(Sg[:, 4 * i:4 * i + 4, :], Q[1 + i].rearrange("p (s v) -> p s v", v=P),
                                                    Sg[:, 4 * i:4 * i + 4, :], ALU.add).then_inc(v_x1, 1)
                        dve.wait_ge(v_x1, 2)
                        nc.vector.tensor_tensor(Sg[:], Sg[:], B["ebC"][0][:, :].unsqueeze(2).to_broadcast([P, SB, P]),
                                                ALU.mult).then_inc(v_S, 2)
                    if g is not None:
                        for h in range(2):
                            dve.wait_ge(a_rs, h + 1)
                            nc.vector.tensor_tensor(rs[h][:, 0:m], o[h][:, 0:m], rs[h][:, 0:m], ALU.mult).then_inc(v_o, 1)
                            dve.wait_ge(v_o, 2 * h + 1)
                            nc.vector.scalar_tensor_tensor(rs[h][:, 0:m], rs[h][:, 0:m], par[:, G_NORM:G_NORM + 1],
                                                           B["gs"][g % 3][h][:, 0:m], ALU.mult, ALU.mult).then_inc(v_o, 1)
                    if e is not None:
                        dve.wait_ge(a_exp, 2)
                        dve.wait_ge(a_ev, 2)
                        nc.vector.tensor_tensor(QGe[:, 0:n], q[:, 0:n], eb[:, 0:n], ALU.mult).then_inc(v_zr, 1)
                        nc.vector.tensor_tensor(KGe[:, 0:n], k[:, 0:n], enb[:, 0:n], ALU.mult).then_inc(v_zr, 1)

                @block.gpsimd
                def _(pool):
                    if e is not None:
                        pool.wait_ge(a_exp, 1)
                        last = eb[:, 0:n].rearrange("p (s j) -> p s j", j=SL if sample_e else C)[:, :, -1:].squeeze(2)
                        nc.gpsimd.tensor_copy(B["ebC"][e % 2][:, :], last).then_inc(p_e, 1)
            rounds_end()

        BANKS = [*Q, *PJ]

        def even_out_stage():
            c1 = ExitStack()
            with c1:
                def sb(name, *shape):
                    return c1.enter_context(nc.sbuf_tensor(name, list(shape), F32))

                WO = sb("WO", P, KT, D)
                ob = [sb(f"ob{i}", P, KT, RB) for i in range(3)]
                xr = [sb(f"xr{i}", P, KT, RB) for i in range(3)]
                gno, rs2 = sb("gno", P, KT), sb("rs2", P, RB)

                def load_o(sp, b):
                    sp.dma_start(ob[b % 3][:], A["O"][:, :, b * RB:(b + 1) * RB].rearrange("k p n -> p k n")).then_inc(d_x[0], 16)
                    sp.dma_start(xr[b % 3][:], A["xT"][:, :, b * RB:(b + 1) * RB]).then_inc(d_x[1], 16)

                with nc.Block() as block:
                    @block.sync
                    def _(sp):
                        load_o(sp, 0)
                        sp.dma_start(WO[:], A["w_out_even"]).then_inc(d_w, 16)
                        sp.dma_start(gno[:], A["norm_odd"]).then_inc(d_p, 16)
                        for s_, v_ in ((d_x[0], 16), (d_x[1], 16), (d_w, 16), (d_p, 16)):
                            sp.wait_ge(s_, v_)
                rounds_end()
                for step in range(NRB + 1):
                    e = step if step < NRB else None
                    g = step - 1 if step else None
                    with nc.Block() as block:
                        @block.sync
                        def _(sp):
                            if step + 1 < NRB:
                                load_o(sp, step + 1)
                            if g is not None:
                                sp.dma_start(A["X2"][:, :, g * RB:(g + 1) * RB], xr[g % 3][:]).then_inc(d_o, 16)
                            if step + 1 < NRB:
                                sp.wait_ge(d_x[0], 16)
                                sp.wait_ge(d_x[1], 16)
                            if g is not None:
                                sp.wait_ge(d_o, 16)

                        def total(pe):
                            pe.wait_ge(v_cl, 1)
                            nc.tensor.matmul(EB[0][:, 0:RB], ones, ob[g % 3][:, 0, :], start=True, stop=True).then_inc(s_ssum, 1)

                        @block.tensor
                        def _(pe):
                            for t in range(KT if e is not None else 0):
                                if t >= len(BANKS):
                                    pe.wait_ge(v_mix, t - len(BANKS) + 1)
                                for k in range(KT):
                                    mm = nc.tensor.matmul(BANKS[t % len(BANKS)][:, 0:RB], WO[:, k, t * P:(t + 1) * P],
                                                          ob[e % 3][:, k, :], start=(k == 0), stop=(k == KT - 1))
                                mm.then_inc(s_proj, 1)
                                if t == 1 and g is not None:
                                    total(pe)
                            if e is None:
                                total(pe)

                        @block.scalar
                        def _(act):
                            if g is not None:
                                nc.scalar.activation(ob[g % 3][:], xr[g % 3][:], ACT.Square).then_inc(a_sq, 1)
                                act.wait_ge(s_ssum, 1)
                                nc.scalar.activation(rs2[:], EB[0][:, 0:RB], ACT.Ln, scale=1.0 / D,
                                                     bias=eps[:, E_RMS:E_RMS + 1]).then_inc(a_ln, 1)
                                act.wait_ge(a_ln, 1)
                                nc.scalar.activation(rs2[:], rs2[:], ACT.Exp, scale=-0.5).then_inc(a_rs, 1)

                        @block.vector
                        def _(dve):
                            def add(t):
                                dve.wait_ge(s_proj, t + 1)
                                nc.vector.tensor_tensor(xr[e % 3][:, t, :], BANKS[t % len(BANKS)][:, 0:RB], xr[e % 3][:, t, :],
                                                        ALU.add).then_inc(v_mix, 1)

                            if g is not None:
                                sum_tiles(dve, ob[g % 3], 1, v_pr, v_cl)
                            if e is not None:
                                for t in range(2):
                                    add(t)
                            if g is not None:
                                dve.wait_ge(a_rs, 1)
                                for k in range(KT):
                                    nc.vector.scalar_tensor_tensor(H[:, k, g * RB:(g + 1) * RB], xr[g % 3][:, k, :], gno[:, k:k + 1],
                                                                   rs2[:], ALU.mult, ALU.mult)
                            if e is not None:
                                for t in range(2, KT):
                                    add(t)
                    rounds_end()

        LAST_PE_TAPS = 13

        def conv_stage():
            c1 = ExitStack()
            with c1:
                def sb(name, *shape):
                    return c1.enter_context(nc.sbuf_tensor(name, list(shape), F32))

                B = {
                    "W": [sb(f"oW{i}", P, 3, D) for i in range(2)], "par": [sb(f"opar{i}", P, 4) for i in range(2)],
                    "cw": [sb(f"cw{i}", P, CW) for i in range(2)],
                    "U": [sb(f"U{i}", P, HALO + SEQ) for i in range(2)],
                    "Us": [sb(f"Us{i}", P, SB, HALO + SL) for i in range(2)],
                    "acc": [sb(f"acc{i}", P, T) for i in range(2)], "sg": [sb(f"osg{i}", P, RB) for i in range(2)],
                    "va": [sb(f"ova{i}", P, RB) for i in range(2)], "gt": [sb(f"ogt{i}", P, RB) for i in range(2)],
                    "dg": sb("dg", P, LAST_PE_TAPS, P), "pr": sb("prs", P, CW, NS),
                }

                def load(sp, t, i, static):
                    one = (lambda a: a[t:t + 1]) if static else (lambda a: a[bass.ds(t, 1)])
                    sp.dma_start(B["W"][i][:], one(A["w_odd"]).rearrange("c j p n -> p (c j) n")).then_inc(d_w, 16)
                    sp.dma_start(B["par"][i][:], one(A["odd_par"]).rearrange("c p n -> p (c n)")).then_inc(d_p, 16)
                    sp.dma_start(B["cw"][i][:], one(A["conv_w"]).rearrange("c p n -> p (c n)")).then_inc(d_p, 16)

                with nc.Block() as block:
                    @block.sync
                    def _(sp):
                        load(sp, 0, 0, True)
                        sp.wait_ge(d_w, 16)
                        sp.wait_ge(d_p, 32)

                    @block.gpsimd
                    def _(pool):
                        nc.gpsimd.memset(ysum[:], 0.0)
                        for i in range(2):
                            nc.gpsimd.memset(B["U"][i][:, 0:HALO], 0.0)
                rounds_end()
                conv_step(B, 0, None, None, 0, True)
                conv_step(B, 1, 0, None, 1, True)
                with nc.Fori(0, (CT - 2) // 2) as j:
                    conv_step(B, j * 2 + 2, j * 2 + 1, j * 2, 0, False)
                    conv_step(B, j * 2 + 3, j * 2 + 2, j * 2 + 1, 1, False)
                conv_step(B, None, CT - 1, CT - 2, 0, True)
                conv_step(B, None, None, CT - 1, 1, True)

        def conv_step(B, e, c, g, i, static):
            W, par, U, Us = B["W"][i], B["par"][i], B["U"][i], B["Us"][i]
            U2, Us2, cw2, par2 = B["U"][1 - i], B["Us"][1 - i], B["cw"][1 - i], B["par"][1 - i]
            acc, accg, sg, va, gt, dg, pr = B["acc"][1 - i], B["acc"][i], B["sg"], B["va"], B["gt"], B["dg"], B["pr"]
            one = (lambda a, t: a[t:t + 1]) if static else (lambda a, t: a[bass.ds(t, 1)])
            accs = acc[:, SEQ:T]
            RING = [*PJ, *EB]
            BLOCKS = [(b * RB, RB) for b in range(NRB)]
            TAIL = SEQ - (NRB - 1) * RB
            NR = len(RING)
            npe = LAST_PE_TAPS if e is None and c is not None else 0
            nv = CW - npe
            last_e = e is not None and static and e == CT - 1
            with nc.Block() as block:
                @block.sync
                def _(sp):
                    if e is not None:
                        sp.dma_start(Us[:, :, 0:HALO], one(A["conv_in"], e).rearrange("c p s j -> p (c s) j")).then_inc(d_s, 16)
                    if g is not None:
                        sp.dma_start(one(A["Y"], g).rearrange("c p n -> p (c n)"), accg[:]).then_inc(d_o2, 16)
                    if e is not None and not last_e:
                        sp.dma_start(B["W"][1 - i][:], one(A["w_odd"], e + 1).rearrange("c j p n -> p (c j) n")).then_inc(d_w, 16)
                        if c is not None:
                            sp.wait_ge(v_acc, nv)
                            sp.wait_ge(v_smp, 1)
                        sp.dma_start(B["par"][1 - i][:], one(A["odd_par"], e + 1).rearrange("c p n -> p (c n)")).then_inc(d_p, 16)
                        sp.dma_start(B["cw"][1 - i][:], one(A["conv_w"], e + 1).rearrange("c p n -> p (c n)")).then_inc(d_p, 16)
                        sp.wait_ge(d_w, 16)
                        sp.wait_ge(d_p, 32)
                    if g is not None:
                        sp.wait_ge(d_o2, 16)
                    if e is not None:
                        sp.wait_ge(p_u, NRB + 1)
                        sp.dma_start(one(A["conv_p_out"], e).rearrange("c p n -> p (c n)"), U[:, SEQ:SEQ + HALO]).then_inc(d_x[0], 16)
                        sp.dma_start(one(A["conv_s_out"], e).rearrange("c p s j -> p (c s) j"), Us[:, :, SL:SL + HALO]).then_inc(d_x[0], 16)
                        sp.wait_ge(d_x[0], 32)

                @block.tensor
                def _(pe):
                    for b, (c0, n) in enumerate(BLOCKS):
                        if e is not None:
                            for t in range(3):
                                x = 3 * b + t
                                if x >= NR:
                                    pe.wait_ge(a_ev, x - NR + 1)
                                project(RING[x % NR], W, t, c0, n).then_inc(s_proj, 1)
                    for b in range(NB if npe else 0):
                        if b == 0:
                            pe.wait_ge(a_dg, npe)
                        for d in range(npe):
                            mm = nc.tensor.matmul(Q[b][:, :], dg[:, d, :], U2[:, d + b * BLK:d + (b + 1) * BLK],
                                                  start=(d == 0), stop=(d == npe - 1))
                        mm.then_inc(s_tap, 1)

                @block.scalar
                def _(act):
                    if c is not None:
                        for d in range(npe):
                            nc.scalar.activation(dg[:, d, :], ident, ACT.Copy, scale=cw2[:, d:d + 1]).then_inc(a_dg, 1)
                    if e is None:
                        return
                    for b, (c0, n) in enumerate(BLOCKS):
                        for t, (dst, func) in enumerate(((va, ACT.Identity), (sg, ACT.Sigmoid), (gt, ACT.Silu))):
                            x = 3 * b + t
                            act.wait_ge(s_proj, x + 1)
                            if b >= 2:
                                if t < 2:
                                    act.wait_ge(p_u, b - 1)
                                else:
                                    act.wait_ge(d_sg[b % 2], 16 * (b // 2))
                            nc.scalar.activation(dst[b % 2][:, 0:n], RING[x % NR][:, 0:n], func, bias=par[:, t:t + 1]).then_inc(a_ev, 1)
                        act.wait_ge(a_ev, 3 * b + 3)
                        act.dma_start(one(A["SG"], e)[:, :, c0:c0 + n].rearrange("c p n -> p (c n)"),
                                      gt[b % 2][:, 0:n]).then_inc(d_sg[b % 2], 16)
                    for i_ in range(2):
                        act.wait_ge(d_sg[i_], 16 * len(range(i_, NRB, 2)))

                @block.gpsimd
                def _(pool):
                    if e is not None:
                        for b, (c0, n) in enumerate(BLOCKS):
                            pool.wait_ge(a_ev, 3 * b + 2)
                            m = n if b < NRB - 1 else TAIL
                            nc.gpsimd.tensor_tensor(U[:, HALO + c0:HALO + c0 + m], va[b % 2][:, 0:m], sg[b % 2][:, 0:m],
                                                    ALU.mult).then_inc(p_u, 1)
                        pool.wait_ge(d_s, 16)
                        nc.gpsimd.tensor_tensor(Us[:, :, HALO:HALO + SL], va[b % 2][:, m:n].rearrange("p (s j) -> p s j", j=SL),
                                                sg[b % 2][:, m:n].rearrange("p (s j) -> p s j", j=SL), ALU.mult).then_inc(p_u, 1)
                    if g is not None:
                        nc.gpsimd.tensor_tensor(ysum[:], ysum[:], accg[:], ALU.add).then_inc(p_ys, 1)

                @block.vector
                def _(dve):
                    if c is None:
                        return
                    for j in range(SL):
                        nc.vector.tensor_tensor(pr[:, :, j * SB:(j + 1) * SB], Us2[:, :, j:j + CW].rearrange("p s d -> p d s"),
                                                cw2[:, :].unsqueeze(2).to_broadcast([P, CW, SB]), ALU.mult).then_inc(v_pr, 1)
                    dve.wait_ge(v_pr, SL)
                    nc.vector.tensor_reduce(accs.rearrange("p (s j) -> p j s", j=SL),
                                            pr[:, :, :].rearrange("p d (j s) -> p j s d", s=SB), mybir.AxisListType.X,
                                            ALU.add).then_inc(v_pr, 1)
                    dve.wait_ge(v_pr, SL + 1)
                    nc.vector.tensor_scalar(accs, accs, par2[:, O_CB:O_CB + 1], None, ALU.add).then_inc(v_smp, 1)
                    for d in range(npe, CW):
                        out, src, w = acc[:, 0:SEQ], U2[:, d:d + SEQ], cw2[:, d:d + 1]
                        if d == npe:
                            nc.vector.tensor_scalar(out, src, w, par2[:, O_CB:O_CB + 1], ALU.mult, ALU.add).then_inc(v_acc, 1)
                        else:
                            dve.wait_ge(v_acc, d - npe)
                            nc.vector.scalar_tensor_tensor(out, src, w, out, ALU.mult, ALU.add).then_inc(v_acc, 1)
                    dve.wait_ge(v_acc, nv)
                    for b in range(NB if npe else 0):
                        dve.wait_ge(s_tap, b + 1)
                        out = acc[:, b * BLK:(b + 1) * BLK]
                        nc.vector.tensor_tensor(out, out, Q[b][:, :], ALU.add).then_inc(v_sum, 1)
            rounds_end()

        def final_stage():
            c1 = ExitStack()
            with c1:
                def sb(name, *shape):
                    return c1.enter_context(nc.sbuf_tensor(name, list(shape), F32))

                WO = sb("WO2", P, KT, D)
                yb = [sb(f"yb{i}", P, KT, RB) for i in range(3)]
                sgb = [sb(f"sgb{i}", P, KT, RB) for i in range(2)]
                sq = sb("fsq", P, KT, RB)
                xr = [sb(f"fx{i}", P, KT, RB) for i in range(4)]
                rsl, rsf = sb("rsl", P, RB), sb("rsf", P, RB)
                lw, lb, fn = sb("lw", P, KT), sb("lb", P, KT), sb("fn", P, KT)

                def rows(a, b):
                    return a[:, :, b * RB:(b + 1) * RB]

                def load_y(sp, b):
                    sp.dma_start(yb[b % 3][:], A["Y"][:, :, b * RB:(b + 1) * RB].rearrange("k p n -> p k n")).then_inc(d_x[0], 16)
                    sp.dma_start(sgb[b % 2][:], A["SG"][:, :, b * RB:(b + 1) * RB].rearrange("k p n -> p k n")).then_inc(d_g, 16)

                with nc.Block() as block:
                    @block.sync
                    def _(sp):
                        load_y(sp, 0)
                        for dst, name in ((lw, "ln_w"), (lb, "ln_b"), (fn, "final_norm")):
                            sp.dma_start(dst[:], A[name]).then_inc(d_p, 16)
                        for s_, v_ in ((d_x[0], 16), (d_g, 16), (d_p, 48)):
                            sp.wait_ge(s_, v_)
                rounds_end()
                for step in range(NRB + 3):
                    a = step if step < NRB else None
                    e = step - 1 if 1 <= step <= NRB else None
                    g = step - 2 if 2 <= step <= NRB + 1 else None
                    out = step - 3 if step >= 3 else None
                    with nc.Block() as block:
                        @block.sync
                        def _(sp):
                            if step == 0:
                                sp.dma_start(WO[:], A["w_out_odd"]).then_inc(d_w, 16)
                            if a is not None:
                                sp.dma_start(xr[a % 4][:], rows(A["X2"], a)).then_inc(d_r, 16)
                            if step + 1 < NRB:
                                load_y(sp, step + 1)
                            if out is not None:
                                sp.dma_start(rows(A["yT"], out), xr[out % 4][:]).then_inc(d_o, 16)
                            if a is not None:
                                sp.wait_ge(d_r, 16)
                            if step + 1 < NRB:
                                sp.wait_ge(d_x[0], 16)
                                sp.wait_ge(d_g, 16)
                            if out is not None:
                                sp.wait_ge(d_o, 16)
                            if step == 0:
                                sp.wait_ge(d_w, 16)

                        def final_total(pe):
                            pe.wait_ge(v_cl, 1)
                            nc.tensor.matmul(BANKS[5][:, 0:RB], ones, sq[:, 0, :], start=True, stop=True).then_inc(s_ssum, 1)

                        def centred_total(pe):
                            pe.wait_ge(v_cl, 1 + (g is not None))
                            nc.tensor.matmul(EB[1][:, 0:RB], ones, sq[:, 0, :], start=True, stop=True).then_inc(s_var, 1)

                        @block.tensor
                        def _(pe):
                            if a is not None:
                                nc.tensor.matmul(EB[0][:, 0:RB], ones, ysum[:, a * RB:(a + 1) * RB], start=True, stop=True).then_inc(s_mean, 1)
                            for t in range(KT if e is not None else 0):
                                if t >= 5:
                                    pe.wait_ge(v_mix, t - 4)
                                for k in range(KT):
                                    mm = nc.tensor.matmul(BANKS[t % 5][:, 0:RB], WO[:, k, t * P:(t + 1) * P], yb[e % 3][:, k, :],
                                                          start=(k == 0), stop=(k == KT - 1))
                                mm.then_inc(s_proj, 1)
                                if t == 1 and g is not None:
                                    final_total(pe)
                                if t == 3 and a is not None:
                                    centred_total(pe)
                            if e is None and g is not None:
                                final_total(pe)
                            if e is None and a is not None:
                                centred_total(pe)

                        @block.scalar
                        def _(act):
                            if g is not None:
                                nc.scalar.activation(sq[:], xr[g % 4][:], ACT.Square).then_inc(a_sq, 1)
                                act.wait_ge(s_ssum, 1)
                                nc.scalar.activation(rsf[:], BANKS[5][:, 0:RB], ACT.Ln, scale=1.0 / D,
                                                     bias=eps[:, E_RMS:E_RMS + 1]).then_inc(a_ln, 1)
                                act.wait_ge(a_ln, 1)
                                nc.scalar.activation(rsf[:], rsf[:], ACT.Exp, scale=-0.5).then_inc(a_rs, 1)
                            if a is not None:
                                n0 = 1 if g is not None else 0
                                act.wait_ge(v_yc, KT)
                                nc.scalar.activation(sq[:], yb[a % 3][:], ACT.Square).then_inc(a_sq, 1)
                                act.wait_ge(s_var, 1)
                                nc.scalar.activation(rsl[:], EB[1][:, 0:RB], ACT.Ln, scale=1.0 / D,
                                                     bias=eps[:, E_LN:E_LN + 1]).then_inc(a_ln, 1)
                                act.wait_ge(a_ln, n0 + 1)
                                nc.scalar.activation(rsl[:], rsl[:], ACT.Exp, scale=-0.5).then_inc(a_rs, 1)
                                for k in range(KT):
                                    act.wait_ge(v_kn, k + 1)
                                    nc.scalar.activation(yb[a % 3][:, k, :], yb[a % 3][:, k, :], ACT.Silu, scale=lw[:, k:k + 1],
                                                         bias=lb[:, k:k + 1]).then_inc(a_gl, 1)

                        @block.gpsimd
                        def _(pool):
                            if a is not None:
                                for k in range(KT):
                                    pool.wait_ge(a_gl, k + 1)
                                    nc.gpsimd.tensor_tensor(yb[a % 3][:, k, :], yb[a % 3][:, k, :], sgb[a % 2][:, k, :],
                                                            ALU.mult).then_inc(p_u, 1)

                        @block.vector
                        def _(dve):
                            n0 = 1 if g is not None else 0
                            if a is not None:
                                dve.wait_ge(s_mean, 1)
                                for k in range(KT):
                                    nc.vector.scalar_tensor_tensor(yb[a % 3][:, k, :], EB[0][:, 0:RB], -1.0 / D, yb[a % 3][:, k, :],
                                                                   ALU.mult, ALU.add).then_inc(v_yc, 1)

                            def add(t):
                                dve.wait_ge(s_proj, t + 1)
                                nc.vector.tensor_tensor(xr[e % 4][:, t, :], BANKS[t % 5][:, 0:RB], xr[e % 4][:, t, :],
                                                        ALU.add).then_inc(v_mix, 1)

                            steps = 0
                            if g is not None:
                                steps = sum_tiles(dve, sq, 1, v_pr, v_cl)
                            if e is not None:
                                for t in range(2):
                                    add(t)
                            if g is not None:
                                dve.wait_ge(a_rs, 1)
                                for k in range(KT):
                                    nc.vector.scalar_tensor_tensor(xr[g % 4][:, k, :], xr[g % 4][:, k, :], fn[:, k:k + 1], rsf[:],
                                                                   ALU.mult, ALU.mult).then_inc(v_o, 1)
                            if a is not None:
                                sum_tiles(dve, sq, n0 + 1, v_pr, v_cl, steps)
                            if e is not None:
                                for t in range(2, 4):
                                    add(t)
                            if a is not None:
                                dve.wait_ge(a_rs, n0 + 1)
                                for k in range(KT):
                                    nc.vector.tensor_tensor(yb[a % 3][:, k, :], yb[a % 3][:, k, :], rsl[:], ALU.mult).then_inc(v_kn, 1)
                            if e is not None:
                                for t in range(4, KT):
                                    add(t)
                    rounds_end()

        norm_stage()
        rwkv_stage()
        gla_stage()
        even_out_stage()
        conv_stage()
        hctx.close()
        final_stage()




def constants():
    K = np.zeros((P, NCONST), np.float32)

    def put(name, x):
        a, b = _COLS[name]
        K[:, a:b] = x

    s, t = np.arange(P)[:, None] % C, np.arange(C)[None, :]
    live = (s < NS) & (t < NS) & (s // SL == t // SL)
    put("maskA", np.concatenate([s < t, s <= t], 1))
    put("maskAs", np.concatenate([(s < t) & live, (s <= t) & live], 1))
    lv = [((s >> l) == (t >> l)) & (((s >> (l - 1)) & 1) == 1) & (((t >> (l - 1)) & 1) == 0) for l in range(1, 7)]
    put("lvl", np.concatenate(lv, 1))
    put("lvl1t", ((s >> 1) == (t >> 1)) & (s < t))
    put("ident", np.eye(P))
    put("ident2", s == t)
    r, c = np.arange(P)[:, None], np.arange(P)[None, :]
    put("bones", r // C == c // C)
    put("ones", 1.0)
    put("reset", (np.arange(BLK) % C != 0)[None, :])
    put("resets", (np.arange(NS) % SL != 0)[None, :])
    put("seq", (s < NS) & (s // SL == np.arange(SB)[None, :]))
    put("maskG", (r // C == c // C) & (r <= c))
    put("maskGs", (r < NS) & (c < NS) & (r // SL == c // SL) & (r <= c))
    e = np.zeros((P, 8))
    e[:, E_RMS], e[:, E_GN], e[:, E_LN], e[:, E_UP], e[:, E_ONE] = RMS_EPS, GN_EPS, LN_EPS, 0.5 * LN_UP * math.log(2), 1.0
    put("eps", e)
    return K


def kernel(**inputs):
    import concourse.bacc as bacc
    from concourse.bass_utils import run_bass_kernel_spmd as run

    I = {k: np.asarray(v) for k, v in inputs.items()}

    def tiles(x):
        return x.reshape(KT, P, -1).transpose(1, 0, 2)

    def col(x):
        return x.reshape(-1, P).T

    def pad_row(x):
        return np.concatenate([x, np.zeros_like(x[:1])], 0)

    x = np.concatenate([I["x_prompt"].reshape(SEQ, D), I["x_sample"].reshape(NS, D)], 0)
    w = I["w_in_even"][0]
    G0, S0 = RPROJ, RPROJ + GPROJ
    cols = [(3 * 512, P), (G0 + 1024, 16)]
    for u in range(RU):
        cols += [(u * P, P), (512 + u * P, P), (1024 + u * P, P), (S0 + u * P, P)]
    for g in range(GU):
        cols += [(G0 + g * P, P), (G0 + 256 + g * P, P), (G0 + 512 + 2 * g * P, P), (G0 + 512 + (2 * g + 1) * P, P),
                 (S0 + (4 + 2 * g) * P, P), (S0 + (5 + 2 * g) * P, P)]
    w_even = np.zeros((len(cols), P, KT, P), np.float32)
    for i, (a, n) in enumerate(cols):
        w_even[i, :, :, :n] = tiles(w[:, a:a + n])
    mu = I["rwkv_mu"][0]
    par = [mu[0:512], mu[512:1024], mu[1024:1536], I["rwkv_w0"][0], I["rwkv_a0"][0], I["rwkv_k_k"][0],
           I["rwkv_k_a"][0], I["rwkv_r_k"][0].reshape(-1), I["rwkv_ln_w"][0], I["rwkv_ln_b"][0]]
    shift = I["state_rwkv_shift"][0]
    order = [a + u * P for u in range(RU) for a in (0, 512, 1024)] + [3 * 512]
    wo = I["w_in_odd"][0]
    w_odd = np.stack([np.stack([tiles(wo[:, j * D + c * P:j * D + (c + 1) * P]) for j in range(3)]) for c in range(CT)])
    b3 = I["b_in_odd"][0].reshape(3, CT, P)
    arrays = {
        "const": constants(),
        "xT": x.T.reshape(KT, P, T).transpose(1, 0, 2),
        "norm_even": col(I["norm_even"][0]),
        "w_even": w_even.reshape(len(cols), P, KT * P),
        "mu_lora": mu[1536:1664].reshape(P, 1),
        "rwkv_par": np.stack([p.reshape(RU, P) for p in par], -1),
        "lora_up": np.concatenate([I["rwkv_w_up"][0], I["rwkv_a_up"][0]], 0),
        "shift_in": np.stack([shift[:, a:a + P].T for a in order]),
        "rwkv_in": I["state_rwkv"][0].reshape(SB, RU, 2, C, C).transpose(1, 2, 4, 0, 3).reshape(RU, P, SB * C),
        "gla_in": I["state_gla"][0].reshape(SB, GU, 2, C, P).transpose(1, 2, 3, 0, 4).reshape(GU, P, SB * P),
        "gla_up": I["gla_g_up"][0],
        "gla_par": np.stack([I["gla_g_b"][0].reshape(GU, P), np.broadcast_to(I["gla_norm"][0], (GU, P))], -1),
        "w_out_even": tiles(I["w_out_even"][0]),
        "norm_odd": col(I["norm_odd"][0]),
        "w_odd": pad_row(w_odd.reshape(CT, 3, P, KT * P)),
        "odd_par": pad_row(np.stack([b3[0], b3[1], b3[2], I["conv_b"][0].reshape(CT, P)], -1)),
        "conv_w": pad_row(I["conv_w"][0].reshape(CW, CT, P).transpose(1, 2, 0)),
        "conv_in": I["cache_conv"][0].reshape(SB, HALO, CT, P).transpose(2, 3, 0, 1),
        "ln_w": col(I["conv_ln_w"][0]),
        "ln_b": col(I["conv_ln_b"][0]),
        "w_out_odd": tiles(I["w_out_odd"][0]),
        "final_norm": col(I["final_norm"]),
    }
    outs = {
        "yT": (P, KT, T), "shift_out": (13, P, 1 + SB), "rwkv_p_out": (RU, P, C), "rwkv_s_out": (RU, P, SB * C),
        "gla_p_out": (GU, P, P), "gla_s_out": (GU, P, SB * P), "conv_p_out": (CT, P, HALO),
        "conv_s_out": (CT, P, SB, HALO),
    }
    scratch = {"O": (KT, P, T), "X2": (P, KT, T), "SG": (CT, P, T), "Y": (CT, P, T)}
    nc = bacc.Bacc("TRN2", target_bir_lowering=False, num_devices=1)
    A = {}
    for name, a in arrays.items():
        arrays[name] = a = np.ascontiguousarray(a)
        A[name] = nc.dram_tensor("in_" + name, a.shape, F32, kind="ExternalInput").ap()
    for name, shape in outs.items():
        A[name] = nc.dram_tensor("out_" + name, shape, F32, kind="ExternalOutput").ap()
    for name, shape in scratch.items():
        A[name] = nc.dram_tensor("tmp_" + name, shape, F32, kind="Internal").ap()
    build(nc, A)
    res = run(nc, [{"in_" + k: v for k, v in arrays.items()}], core_ids=[0]).results[0]
    R = {k: np.asarray(res["out_" + k]) for k in outs}
    y = R["yT"].transpose(1, 0, 2).reshape(D, T).T
    sh = np.zeros((1 + SB, RPROJ), np.float32)
    for i, a in enumerate(order):
        sh[:, a:a + P] = R["shift_out"][i].T
    rp = R["rwkv_p_out"].reshape(RU, 2, C, C).transpose(0, 1, 3, 2).reshape(1, 1, 8, C, C)
    rsmp = R["rwkv_s_out"].reshape(RU, 2, C, SB, C).transpose(3, 0, 1, 4, 2).reshape(1, SB, 8, C, C)
    gp = R["gla_p_out"].reshape(1, 1, 4, C, P)
    gsmp = R["gla_s_out"].reshape(GU, 2, C, SB, P).transpose(3, 0, 1, 2, 4).reshape(1, SB, 4, C, P)
    cp = R["conv_p_out"].transpose(2, 0, 1).reshape(1, 1, HALO, D)
    csmp = R["conv_s_out"].transpose(2, 3, 0, 1).reshape(1, SB, HALO, D)
    return (y[:SEQ].reshape(1, SEQ, D).copy(), y[SEQ:].reshape(SB, SL, D).copy(), sh[0:1].reshape(1, 1, RPROJ).copy(),
            sh[1:].reshape(1, SB, RPROJ).copy(), rp.copy(), rsmp.copy(), gp.copy(), gsmp.copy(), cp.copy(), csmp.copy())
```

```python
from contextlib import ExitStack
import math

import numpy as np
import concourse.bass as bass
from concourse import mybir

F32 = mybir.dt.float32
ACT = mybir.ActivationFunctionType
ALU = mybir.AluOpType

P = 128
D = 1024
KT = D // P
SEQ = 2048
SB, SL = 8, 4
NS = SB * SL
T = SEQ + NS
BLK = 512
NB = SEQ // BLK
C = 64
NC = BLK // C
RB = 416
NRB = T // RB
HK = 64
RU = 4
GU = 2
CT = KT
CW = 31
HALO = CW - 1
DECAY = math.exp(-0.5)
LN_UP = 30
GN_EPS, RMS_EPS, LN_EPS = 64e-5, 1e-6, 1e-5
RPROJ, GPROJ = 1664, 1040

_COLS = {}
_n = 0
for _name, _w in (("maskA", 128), ("maskAs", 128), ("lvl", 6 * 64), ("lvl1t", 64), ("ident", 128),
                  ("ident2", 64), ("bones", 128), ("ones", 128), ("reset", BLK), ("resets", NS),
                  ("seq", SB), ("maskG", 128), ("maskGs", 128), ("eps", 8)):
    _COLS[_name] = (_n, _n + _w)
    _n += _w
NCONST = _n
R_MUR, R_MUK, R_MUV, R_W0, R_A0, R_KK, R_KA, R_RK, R_LNW, R_LNB = range(10)
G_GB, G_NORM = range(2)
O_BV, O_BG, O_BS, O_CB = range(4)
E_RMS, E_GN, E_LN, E_UP, E_ONE = range(5)


def build(nc, A):
    ctx = ExitStack()
    with ctx:
        def sb(name, *shape):
            return ctx.enter_context(nc.sbuf_tensor(name, list(shape), F32))

        sems = []

        def sem(name):
            s = ctx.enter_context(nc.semaphore(name))
            sems.append(s)
            return s

        ps = [ctx.enter_context(nc.psum_tensor(f"bank{i}", [P, 512], F32)) for i in range(8)]
        PJ, EB, Q = ps[0:2], ps[2:4], ps[4:8]

        def rounds_end():
            nc.gpsimd.sem_clear(range(sems[0].num, sems[-1].num + 1))
            nc.all_engine_barrier()

        K0 = sb("K0", P, NCONST)
        ysum = sb("ysum", P, T)
        H = sb("H", P, KT, T)

        def cst(name):
            a, b = _COLS[name]
            return K0[:, a:b]

        ident, ident2, bones, ones = cst("ident"), cst("ident2"), cst("bones"), cst("ones")
        eps = cst("eps")

        s_ssum = sem("square_sums_ready")
        s_proj = sem("projection_ready")
        s_lora = sem("lora_ready")
        s_ssq = sem("key_square_sums_ready")
        s_bon = sem("bonus_sums_ready")
        s_A = sem("chunk_products_ready")
        s_tr = sem("transposes_ready")
        s_wv = sem("value_part_ready")
        s_T = sem("inverse_left_ready")
        s_X = sem("inverse_right_ready")
        s_ZS = sem("state_read_ready")
        s_U = sem("removals_ready")
        s_SU = sem("state_change_ready")
        s_Y = sem("outputs_ready")
        s_mean = sem("mean_ready")
        s_var = sem("variance_ready")
        a_sq = sem("squares_done")
        a_ln = sem("log_done")
        a_rs = sem("rstd_done")
        a_ev = sem("projection_evacuated")
        a_halo = sem("halo_moved")
        a_mu = sem("previous_scaled")
        a_sig = sem("sigmoid_done")
        a_exp = sem("decay_exp_done")
        a_kn = sem("key_norm_done")
        a_ka = sem("key_gain_done")
        a_tb = sem("transposes_evacuated")
        a_wv = sem("value_part_evacuated")
        a_y = sem("outputs_evacuated")
        v_h = sem("normalised_done")
        v_mix = sem("mixed")
        v_cs = sem("log_decay_summed")
        v_cl = sem("key_sums_clamped")
        v_kn = sem("key_normalised")
        v_zr = sem("z_and_r_done")
        v_b = sem("b_done")
        v_bp = sem("bonus_product_done")
        v_bv = sem("bonus_done")
        v_M = sem("chunk_products_masked")
        v_x1 = sem("inverse_started")
        v_T = sem("inverse_left_masked")
        v_X = sem("inverse_grown")
        v_W0 = sem("state_read_done")
        v_U = sem("removals_done")
        v_S = sem("state_done")
        v_yc = sem("centred")
        v_o = sem("gated")
        p_set = sem("constants_set")
        p_kp = sem("key_scaled")
        p_ka = sem("key_rate_product_done")
        p_K = sem("k_done")
        p_V = sem("v_placed")
        p_e = sem("chunk_decay_kept")
        p_sh = sem("shift_row_kept")
        a_g = sem("gate_log_steps")
        a_gl = sem("sigmoid_gate_done")
        v_g = sem("gate_input_ready")
        p_u = sem("glu_done")
        p_ys = sem("channel_sum_done")
        v_acc = sem("taps_added")
        s_tap = sem("tensor_taps_added")
        a_dg = sem("tap_diagonals_done")
        v_pr = sem("sample_products_done")
        v_smp = sem("sample_taps_done")
        v_sum = sem("taps_summed")
        d_c = sem("constants_loaded")
        d_x = [sem("x_loaded0"), sem("x_loaded1")]
        d_w = sem("weights_loaded")
        d_p = sem("parameters_loaded")
        d_s = sem("states_loaded")
        d_o = sem("outputs_stored")
        d_o2 = sem("state_stored")
        d_r = sem("residual_loaded")
        d_g = sem("gate_loaded")
        d_sg = [sem("gate_stored0"), sem("gate_stored1")]

        def norm_block(first_loads, xsq, rst, gn):
            def rows(b):
                return H[:, :, b * RB:(b + 1) * RB]

            with nc.Block() as block:
                @block.sync
                def _(sp):
                    sp.dma_start(rows(0), A["xT"][:, :, 0:RB]).then_inc(d_x[0], 16)
                    sp.dma_start(K0[:], A["const"]).then_inc(d_c, 16)
                    sp.dma_start(gn, A["norm_even"]).then_inc(d_c, 16)
                    for b in range(1, NRB):
                        if b >= 2:
                            sp.wait_ge(d_x[b % 2], 16 * (b // 2))
                        sp.dma_start(rows(b), A["xT"][:, :, b * RB:(b + 1) * RB]).then_inc(d_x[b % 2], 16)
                    first_loads(sp)

                @block.scalar
                def _(act):
                    def square(b):
                        act.wait_ge(d_x[b % 2], 16 * (b // 2 + 1))
                        if b >= 2:
                            act.wait_ge(s_ssum, b - 1)
                        nc.scalar.activation(xsq[b % 2], rows(b), ACT.Square).then_inc(a_sq, 1)

                    square(0)
                    act.wait_ge(d_c, 32)
                    for b in range(NRB):
                        if b + 1 < NRB:
                            square(b + 1)
                        act.wait_ge(s_ssum, b + 1)
                        if b:
                            act.wait_ge(v_h, b)
                        nc.scalar.activation(rst, EB[b % 2][:, 0:RB], ACT.Ln, scale=1.0 / D,
                                             bias=eps[:, E_RMS:E_RMS + 1]).then_inc(a_ln, 1)
                        act.wait_ge(a_ln, b + 1)
                        nc.scalar.activation(rst, rst, ACT.Exp, scale=-0.5).then_inc(a_rs, 1)

                @block.tensor
                def _(pe):
                    pe.wait_ge(d_c, 32)
                    for b in range(NRB):
                        pe.wait_ge(v_cl, b + 1)
                        if b >= 2:
                            pe.wait_ge(a_ln, b - 1)
                        nc.tensor.matmul(EB[b % 2][:, 0:RB], ones, xsq[b % 2][:, 0, :], start=True, stop=True).then_inc(s_ssum, 1)

                @block.vector
                def _(dve):
                    dve.wait_ge(d_c, 32)
                    steps = sum_tiles(dve, xsq[0], 1, v_pr, v_cl)
                    for b in range(NRB):
                        if b + 1 < NRB:
                            steps = sum_tiles(dve, xsq[(b + 1) % 2], b + 2, v_pr, v_cl, steps)
                        dve.wait_ge(a_rs, b + 1)
                        for k in range(KT):
                            ins = nc.vector.scalar_tensor_tensor(rows(b)[:, k, :], rows(b)[:, k, :], gn[:, k:k + 1],
                                                                 rst, ALU.mult, ALU.mult)
                        ins.then_inc(v_h, 1)
            rounds_end()

        def project(bank, w, t, cols, n, m=P):
            for k in range(KT):
                mm = nc.tensor.matmul(bank[0:m, 0:n], w[:, t, k * P:k * P + m], H[:, k, cols:cols + n],
                                      start=(k == 0), stop=(k == KT - 1))
            return mm

        def sum_tiles(dve, x, squares, halved, done, before=0):
            dve.wait_ge(a_sq, squares)
            w = KT // 2
            while w > 1:
                nc.vector.tensor_tensor(x[:, 0:w, :], x[:, 0:w, :], x[:, w:2 * w, :], ALU.add).then_inc(halved, 1)
                before += 1
                dve.wait_ge(halved, before)
                w //= 2
            nc.vector.tensor_tensor(x[:, 0, :], x[:, 0, :], x[:, 1, :], ALU.add).then_inc(done, 1)
            return before

        COLS = [(b * BLK, BLK) for b in range(NB)] + [(SEQ, NS)]

        def rwkv_stage():
            c1 = ExitStack()
            with c1:
                def sb(name, *shape):
                    return c1.enter_context(nc.sbuf_tensor(name, list(shape), F32))

                W = sb("W", P, 4, D)
                LT = ysum
                par = sb("rpar", P, 10)
                lnp = sb("lnp", P, 2)
                omm = sb("romm", P, 4)
                LU = sb("LU", P, P)
                raw = [sb(f"raw{i}", P, 1 + BLK) for i in range(3)]
                raws = [sb(f"raws{i}", P, SB, SL + 1) for i in range(3)]
                shr = sb("shr", P, 3, 1 + SB)
                shi = sb("shi", P, 3, SB)
                ZR = [sb(f"ZR{i}", P, NC, 2, C) for i in range(2)] + [sb("ZRs", P, 1, 2, C)]
                BK, BKs = sb("BK", P, NC, 2, C), sb("BKs", P, 1, 2, C)
                VSs = sb("VSs", P, 1, 2, C)
                BT = sb("BT", P, NC, P)
                W0 = sb("W0t", P, C)
                S, Sd = sb("S", P, C), sb("Sd", P, C)
                Ss = sb("Ss", P, SB, C)
                PS = sb("PSs", P, SB, C)
                r, k, v = sb("r", P, BLK), sb("k", P, BLK), sb("v", P, BLK)
                t0, t1, t2 = sb("t0", P, BLK), sb("t1", P, BLK), sb("t2", P, BLK)
                sg, aa, cs = sb("sg", P, BLK), sb("aa", P, BLK), sb("cs", P, BLK)
                eb, enb, ebm = sb("eb", P, BLK), sb("enb", P, BLK), sb("ebm", P, BLK)
                kp = sb("kp", P, BLK)
                bv = [sb(f"bv{i}", P, BLK) for i in range(3)]
                gs = [sb(f"gs{i}", P, BLK) for i in range(NB)] + [sb("gss", P, NS)]
                ebC = [sb(f"ebC{i}", P, SB) for i in range(2)]
                ysb = [sb(f"ysb{i}", P, BLK) for i in range(2)]
                yc, rs = sb("yc", P, BLK), sb("rs", P, BLK)
                shared = sb("shared", P, 2 * KT * RB)
                taken = [0]

                def part_of(*shape):
                    a_, n_ = taken[0], math.prod(shape)
                    taken[0] += n_
                    x = shared[:, a_:a_ + n_]
                    if len(shape) == 1:
                        return x
                    names = "abcd"[:len(shape)]
                    return x.rearrange(f"p ({' '.join(names)}) -> p {' '.join(names)}", **dict(zip(names, shape)))

                M = part_of(2, NC, P)
                UV = part_of(NC, 2, C)
                XX = part_of(2, 2, 4, C)
                T1, WV = part_of(2, 4, C), part_of(NC, C)
                VS, kkn = part_of(NC, 2, C), part_of(BLK)

                WL = BT[:, :, :].rearrange("p c n -> p (c n)").unsqueeze(1)
                muL, omL = t0[:, 0:1], t0[:, 1:2]
                shl, stg = t1[:, 0:1 + SB], t1[:, 16:16 + SB]

                def first_loads(sp):
                    sp.dma_start(WL[:, 0, :], A["w_even"][0]).then_inc(d_w, 16)
                    sp.dma_start(muL, A["mu_lora"]).then_inc(d_p, 16)
                    sp.dma_start(stg, A["shift_in"][12]).then_inc(d_p, 16)
                    sp.dma_start(W[:], A["w_even"][2:6].rearrange("t p n -> p t n")).then_inc(d_s, 16)
                    sp.wait_ge(d_w, 16)
                    sp.wait_ge(d_p, 32)
                    sp.wait_ge(d_s, 16)

                squares = shared[:, :].rearrange("p (i k n) -> p i k n", i=2, n=RB)
                norm_block(first_loads, [squares[:, i] for i in range(2)], cs[:, 0:RB], sg[:, 0:KT])
                with nc.Block() as block:
                    LR = M[:, :, :, :].rearrange("p a b c -> p (a b c)")
                    rawL = raws[0]
                    tmp = [t2, sg]

                    @block.sync
                    def _(sp):
                        sp.wait_ge(p_sh, 2)
                        sp.dma_start(A["shift_out"][12], shl).then_inc(d_o, 16)
                        sp.wait_ge(d_o, 16)

                    @block.gpsimd
                    def _(pool):
                        for z in [*ZR[2:], BKs, VSs, VS, S, BK, Ss, lnp, gs[NB], ysb[NB % 2][:, 0:NS], bv[NB % 3][:, 0:NS]]:
                            nc.gpsimd.memset(z[:], 0.0)
                        for i in range(3):
                            nc.gpsimd.memset(raw[i][:, 0:1], 0.0)
                        nc.gpsimd.tensor_copy(rawL[:, :, 0:1].squeeze(2), stg).then_inc(p_set, 1)
                        pool.wait_ge(a_ev, NB + 1)
                        nc.gpsimd.tensor_copy(shl[:, 0:1], LR[:, SEQ - 1:SEQ]).then_inc(p_sh, 1)
                        nc.gpsimd.tensor_copy(shl[:, 1:1 + SB], rawL[:, :, SL:SL + 1].squeeze(2)).then_inc(p_sh, 1)

                    @block.tensor
                    def _(pe):
                        for b, (c0, n) in enumerate(COLS):
                            if b >= 2:
                                pe.wait_ge(a_ev, b - 1)
                            project(PJ[b % 2], WL, 0, c0, n).then_inc(s_proj, 1)
                        for i in range(3):
                            x = len(COLS) + i
                            pe.wait_ge(a_ev, x - 1)
                            project(PJ[x % 2], W, i, 0, BLK).then_inc(s_proj, 1)

                    @block.scalar
                    def _(act):
                        for b, (c0, n) in enumerate(COLS):
                            act.wait_ge(s_proj, b + 1)
                            if b < NB:
                                out, src = LR[:, c0:c0 + n], PJ[b % 2][:, 0:n]
                            else:
                                out = rawL[:, :, 1:1 + SL]
                                src = PJ[b % 2][:, 0:n].rearrange("p (s j) -> p s j", j=SL)
                            nc.scalar.activation(out, src, ACT.Copy).then_inc(a_ev, 1)
                        for i in range(3):
                            x = len(COLS) + i
                            act.wait_ge(s_proj, x + 1)
                            nc.scalar.activation(raw[i][:, 1:1 + BLK], PJ[x % 2][:, :], ACT.Copy).then_inc(a_ev, 1)
                        act.wait_ge(v_mix, 1 + 2 * (NB + 1))
                        nc.scalar.activation(LT[0:64, :], LT[0:64, :], ACT.Tanh)

                    @block.vector
                    def _(dve):
                        nc.vector.tensor_scalar(omL, muL, -1.0, 1.0, ALU.mult, ALU.add).then_inc(v_mix, 1)
                        dve.wait_ge(v_mix, 1)
                        nc.vector.memset(t2[:, 0:1], 0.0).then_inc(v_x1, 1)
                        for b, (c0, n) in enumerate(COLS):
                            dve.wait_ge(a_ev, b + 1)
                            x = tmp[b % 2]
                            if b == NB:
                                dve.wait_ge(p_set, 1)
                            if b < NB:
                                a = 0 if b else 1
                                cur, prev = LR[:, c0:c0 + n], LR[:, c0 + a - 1:c0 + n - 1]
                                if b == 0:
                                    dve.wait_ge(v_x1, 1)
                                nc.vector.tensor_scalar(x[:, a:n], prev, muL, None, ALU.mult).then_inc(v_mix, 1)
                                out, x = LT[:, c0:c0 + n], x[:, 0:n]
                            else:
                                cur, prev = rawL[:, :, 1:1 + SL], rawL[:, :, 0:SL]
                                x = x[:, 0:n].rearrange("p (s j) -> p s j", j=SL)
                                nc.vector.tensor_scalar(x, prev, muL, None, ALU.mult).then_inc(v_mix, 1)
                                out = LT[:, c0:c0 + n].rearrange("p (s j) -> p s j", j=SL)
                            dve.wait_ge(v_mix, 2 + 2 * b)
                            nc.vector.scalar_tensor_tensor(out, cur, omL, x, ALU.mult, ALU.add).then_inc(v_mix, 1)
                rounds_end()
                def step_of(u, step):
                    return rwkv_step(u, step, W, LT, (par, lnp), omm, LU, raw, raws, shr, shi, ZR, (BK, BKs), (VS, VSs), M, BT,
                                     UV, XX, T1, WV, W0, S, Sd, Ss, PS, r, k, v, (t0, t1, t2), sg, aa, cs, eb, enb,
                                     ebm, kkn, kp, bv, gs, ebC, ysb, yc, rs)

                with nc.Fori(0, RU) as u:
                    for step in range(NB + 2):
                        step_of(u, step)
                step_of(RU, NB + 2)

        def rwkv_step(u, step, W, LT, pars, omm, LU, raw, raws, shr, shi, ZRb, BKb, VSb, M, BT, UV, XX, T1, WV, W0, S,
                      Sd, Ss, PS, r, k, v, tmps, sg, aa, cs, eb, enb, ebm, kkn, kp, bv, gs, ebC, ysb, yc, rs):
            par, lnp = pars
            f = step + 1 if step < NB - 1 else 0 if step == NB else None
            e = step if step <= NB else None
            c = step - 1 if 1 <= step <= NB + 1 else None
            g = step - 2 if step >= 2 else NB if step == 0 else None
            gn_w, gn_b = (lnp[:, 0:1], lnp[:, 1:2]) if g == NB else (par[:, R_LNW:R_LNW + 1], par[:, R_LNB:R_LNB + 1])
            g_row = u if g == NB else u + 1
            t0, t1, t2 = tmps
            JOBS = [(i, f) for i in range(3)] if f is not None else []
            if step == 0:
                JOBS += [(i, NB) for i in range(4)]
            elif step == NB - 1:
                JOBS += [(3, NB - 2), (3, NB - 1)]
            elif step < NB:
                JOBS += [(3, step - 1)]
            ALL = KT * len(JOBS)
            sample_e, sample_c = e == NB, c == NB
            if e is not None:
                c0, n = COLS[e]
                we, ne = min(C, n), max(1, n // C)
                ZRe, BKe, VSe = ZRb[2 if sample_e else e % 2], BKb[sample_e], VSb[sample_e]

                def ch(x, lo=0, hi=P):
                    return x[lo:hi, 0:n].rearrange("p (c j) -> p c j", j=we)
            if c is not None:
                ZR, BK, VS = ZRb[2 if sample_c else c % 2], BKb[sample_c], VSb[sample_c]
                nch = 1 if sample_c else NC
                grp = [range(0, 1)] if sample_c else [range(0, 4), range(4, 8)]
                G = len(grp)
                levels = 2 if sample_c else 6
                maskA = cst("maskAs" if sample_c else "maskA")
                nT = 2 if sample_c else 4
            halves = [(0, 64), (64, 128)]

            def evacuate(act, j):
                i, item = JOBS[j]
                bank, nf = PJ[j % 2], COLS[item][1]
                act.wait_ge(s_proj, j + 1)
                if i == 3:
                    if item == NB:
                        act.wait_ge(v_o, 3)
                    nc.scalar.activation(gs[item][:, 0:nf], bank[:, 0:nf], ACT.Silu).then_inc(a_ev, 1)
                elif item == NB:
                    nc.scalar.activation(raws[i][:, :, 1:1 + SL],
                                         bank[:, 0:nf].rearrange("p (s j) -> p s j", j=SL), ACT.Copy).then_inc(a_ev, 1)
                else:
                    if item:
                        act.wait_ge(v_mix, MIXED)
                        nc.scalar.activation(raw[i][:, 0:1], raw[i][:, BLK:BLK + 1], ACT.Copy).then_inc(a_halo, 1)
                        act.wait_ge(a_halo, i + 1)
                    nc.scalar.activation(raw[i][:, 1:1 + nf], bank[:, 0:nf], ACT.Copy).then_inc(a_ev, 1)

            def scale_previous(act, i):
                if sample_e:
                    if i == 0:
                        act.wait_ge(d_x[0], 48)
                        for x in range(3):
                            nc.scalar.activation(raws[x][:, :, 0:1].squeeze(2), shi[:, x, :], ACT.Copy).then_inc(a_halo, 1)
                        act.wait_ge(a_halo, 3)
                    prev, dst = raws[i][:, :, 0:SL], tmps[i][:, 0:n].rearrange("p (s j) -> p s j", j=SL)
                else:
                    prev, dst = raw[i][:, 0:n], tmps[i][:, 0:n]
                if step == 0 and i == 0:
                    act.wait_ge(d_p, 32)
                nc.scalar.activation(dst, prev, ACT.Copy, scale=par[:, i:i + 1]).then_inc(a_mu, 1)

            MIXED = 3 + (step == 0)

            def mix(dve, i):
                dst = (r, k, v)[i]
                if sample_e:
                    cur = raws[i][:, :, 1:1 + SL]
                    out, x = (y_[:, 0:n].rearrange("p (s j) -> p s j", j=SL) for y_ in (dst, tmps[i]))
                else:
                    cur, out, x = raw[i][:, 1:1 + n], dst[:, 0:n], tmps[i][:, 0:n]
                dve.wait_ge(a_mu, i + 1)
                nc.vector.scalar_tensor_tensor(out, cur, omm[:, i:i + 1], x, ALU.mult, ALU.add).then_inc(v_mix, 1)

            with nc.Block() as block:
                @block.sync
                def _(sp):
                    if step == 0:
                        sp.dma_start(par[:], A["rwkv_par"][bass.ds(u, 1)].rearrange("u p n -> p (u n)")).then_inc(d_p, 16)
                        sp.dma_start(LU[:], A["lora_up"][:, bass.ds(u * P, P)]).then_inc(d_p, 16)
                    if step == NB - 1:
                        sp.dma_start(W[:, 0:3, :], A["w_even"][bass.ds(u * 4 + 6, 3)].rearrange("t p n -> p t n")).then_inc(d_w, 16)
                    if step == NB:
                        sp.dma_start(W[:, 3:4, :], A["w_even"][bass.ds(u * 4 + 9, 1)].rearrange("t p n -> p t n")).then_inc(d_w, 16)
                        sp.dma_start(Ss[:], A["rwkv_in"][bass.ds(u, 1)].rearrange("u p (s v) -> p (u s) v", v=C)).then_inc(d_s, 16)
                    if sample_e:
                        for i in range(3):
                            sp.dma_start(shi[:, i, :], A["shift_in"][bass.ds(u * 3 + i, 1)].rearrange("t p s -> p (t s)")).then_inc(d_x[0], 16)
                        sp.wait_ge(p_sh, 6)
                        for i in range(3):
                            sp.dma_start(A["shift_out"][bass.ds(u * 3 + i, 1)].rearrange("t p s -> p (t s)"),
                                         shr[:, i, :]).then_inc(d_o2, 16)
                        sp.wait_ge(d_s, 16)
                    if step == NB + 1:
                        sp.dma_start(A["rwkv_p_out"][bass.ds(u, 1)].rearrange("u p v -> p (u v)"), S[:]).then_inc(d_o2, 16)
                        sp.wait_ge(d_o2, 16)
                    if g == NB:
                        sp.dma_start(A["rwkv_s_out"][bass.ds(u, 1)].rearrange("u p (s v) -> p (u s) v", v=C),
                                     Ss[:]).then_inc(d_o2, 16)
                        sp.wait_ge(d_o2, 16)
                    if g is not None:
                        gc0, gn_ = COLS[g]
                        sp.wait_ge(v_o, 3)
                        sp.dma_start(A["O"][bass.ds(g_row, 1), :, gc0:gc0 + gn_].rearrange("u p n -> p (u n)"),
                                     rs[:, 0:gn_]).then_inc(d_o, 16)
                        sp.wait_ge(d_o, 16)
                    if sample_e:
                        sp.wait_ge(d_o2, 48)
                    if step in (NB - 1, NB):
                        sp.wait_ge(d_w, 16)

                @block.tensor
                def _(pe):
                    issued = [0]

                    def upto(n_):
                        for x in range(issued[0], min(n_, ALL)):
                            j, k_ = divmod(x, KT)
                            t, item = JOBS[j]
                            f0, nf = COLS[item]
                            if k_ == 0 and j < 2:
                                pe.wait_ge(a_sig, j + 1)
                            if k_ == 0 and j >= 2:
                                pe.wait_ge(a_ev, j - 1)
                            mm = nc.tensor.matmul(PJ[j % 2][:, 0:nf], W[:, t, k_ * P:(k_ + 1) * P],
                                                  H[:, k_, f0:f0 + nf], start=(k_ == 0), stop=(k_ == KT - 1))
                            if k_ == KT - 1:
                                mm.then_inc(s_proj, 1)
                            issued[0] = x + 1

                    if e is not None:
                        if step == 0:
                            pe.wait_ge(d_p, 32)
                        nc.tensor.matmul(PJ[0][:, 0:n], LU[0:64, :], LT[0:64, c0:c0 + n], start=True, stop=True).then_inc(s_lora, 1)
                        nc.tensor.matmul(PJ[1][:, 0:n], LU[64:128, :], LT[64:128, c0:c0 + n], start=True, stop=True).then_inc(s_lora, 1)
                    if g is not None:
                        _, m = COLS[g]
                        nc.tensor.matmul(EB[0][:, 0:m], bones, ysb[g % 2][:, 0:m], start=True, stop=True).then_inc(s_mean, 1)
                    if c is not None:
                        for gi, chunks in enumerate(grp):
                            for h, (lo, hi) in enumerate(halves):
                                for i, q in enumerate(chunks):
                                    mm = nc.tensor.matmul(Q[2 * gi + h][:, i * P:(i + 1) * P], BK[lo:hi, q, :, :],
                                                          ZR[lo:hi, q, :, :], start=True, stop=True)
                                mm.then_inc(s_A, 1)
                    if g is not None:
                        pe.wait_ge(a_sq, 1)
                        nc.tensor.matmul(EB[1][:, 0:m], bones, yc[:, 0:m], start=True, stop=True).then_inc(s_var, 1)
                    if e is not None:
                        pe.wait_ge(a_kn, 1)
                        if g is not None:
                            pe.wait_ge(v_yc, 1)
                        nc.tensor.matmul(EB[0][:, 0:n], bones, t0[:, 0:n], start=True, stop=True).then_inc(s_ssq, 1)
                    if c is not None:
                        for t, (src, bank) in enumerate([(BK, Q[0]), (BK, Q[1]), (VS, Q[2]), (VS, Q[3])]
                                                        if not sample_c else [(BK, Q[0]), (VS, Q[2])]):
                            pe.wait_ge(v_M, t + 1 if not sample_c else 2)
                            for i, q in enumerate(grp[t % G]):
                                mm = nc.tensor.transpose(bank[:, i * P:(i + 1) * P], src[:, q, :, :], ident)
                            mm.then_inc(s_tr, 1)
                        upto(3)
                        pe.wait_ge(a_tb, nT)
                        for gi, chunks in enumerate(grp):
                            for i, q in enumerate(chunks):
                                for h, (lo, hi) in enumerate(halves):
                                    mm = nc.tensor.matmul(Q[gi][lo:hi, i * C:(i + 1) * C], M[lo:hi, h, q, 0:C],
                                                          ident2[lo:hi, :], start=True, stop=True)
                            mm.then_inc(s_T, 1)
                        for q in range(nch):
                            for h, (lo, hi) in enumerate(halves):
                                ko, ki = halves[1 - h]
                                mm = nc.tensor.matmul(Q[3][lo:hi, q * C:(q + 1) * C], M[ko:ki, h, q, 0:C],
                                                      UV[ko:ki, q, h, :], start=True, stop=True)
                        mm.then_inc(s_wv, 1)
                        upto(5)
                        pe.wait_ge(a_wv, 1)
                        for l in range(2, levels + 1):
                            for gi, chunks in enumerate(grp):
                                pe.wait_ge(v_X, G * (l - 2) + gi + 1)
                                for i, q in enumerate(chunks):
                                    for h, (lo, hi) in enumerate(halves):
                                        mm = nc.tensor.matmul(Q[gi][lo:hi, i * C:(i + 1) * C], M[lo:hi, h, q, 0:C],
                                                              XX[lo:hi, gi, 0, i, :], start=True, stop=True)
                                mm.then_inc(s_T, 1)
                            upto(issued[0] + 1)
                            for gi, chunks in enumerate(grp):
                                pe.wait_ge(v_T, G * (l - 2) + gi + 1)
                                for i, q in enumerate(chunks):
                                    for h, (lo, hi) in enumerate(halves):
                                        if l < levels:
                                            nc.tensor.matmul(Q[2 + gi][lo:hi, i * C:(i + 1) * C], XX[lo:hi, gi, 1, i, :],
                                                             T1[lo:hi, gi, i, :], start=True, stop=True)
                                        mm = nc.tensor.matmul(Q[2 + gi][lo:hi, (4 + i) * C:(5 + i) * C], T1[lo:hi, gi, i, :],
                                                              XX[lo:hi, gi, 1, i, :], start=True, stop=True)
                                mm.then_inc(s_X, 1)
                            upto(issued[0] + 1)
                    if c is None:
                        upto(ALL)
                    upto(ALL - 2 * NC)

                    def bonus():
                        pe.wait_ge(v_bp, 1)
                        if g is not None:
                            pe.wait_ge(a_ln, 1)
                        nc.tensor.matmul(EB[1][:, 0:n], bones, t2[:, 0:n], start=True, stop=True).then_inc(s_bon, 1)

                    if c is not None and not sample_c:
                        pe.wait_ge(v_X, G * levels)
                        for j in range(NC):
                            if j:
                                pe.wait_ge(v_S, j)
                            for h, (lo, hi) in enumerate(halves):
                                mm = nc.tensor.matmul(Q[0][lo:hi, 0:C], ZR[lo:hi, j, 0, :], S[lo:hi, :], start=True, stop=True)
                            mm.then_inc(s_ZS, 1)
                            upto(issued[0] + 1)
                            pe.wait_ge(v_W0, j + 1)
                            for h, (lo, hi) in enumerate(halves):
                                mm = nc.tensor.matmul(Q[0][lo:hi, C:2 * C], XX[lo:hi, j // 4, 1, j % 4, :], W0[lo:hi, :],
                                                      start=True, stop=True)
                            mm.then_inc(s_U, 1)
                            for h, (lo, hi) in enumerate(halves):
                                nc.tensor.matmul(Q[1][lo:hi, j * C:(j + 1) * C], S[lo:hi, :], ZR[lo:hi, j, 1, :],
                                                 start=True, stop=False)
                            pe.wait_ge(v_U, 2 * (j + 1))
                            for h, (lo, hi) in enumerate(halves):
                                mm = nc.tensor.matmul(Q[0][lo:hi, 2 * C:3 * C], BT[:, j, lo:hi], UV[:, j, h, :],
                                                      start=True, stop=True)
                            mm.then_inc(s_SU, 1)
                            for h, (lo, hi) in enumerate(halves):
                                mm = nc.tensor.matmul(Q[1][lo:hi, j * C:(j + 1) * C], UV[:, j, h, :], M[:, h, j, C:2 * C],
                                                      start=False, stop=True)
                            if j == NC - 1:
                                mm.then_inc(s_Y, 1)
                            upto(issued[0] + 1)
                            if e is not None and j == 6:
                                bonus()
                    elif sample_c:
                        pe.wait_ge(v_X, G * levels)
                        for h, (lo, hi) in enumerate(halves):
                            mm = nc.tensor.matmul(Q[0][lo:hi, :], ZR[lo:hi, 0, 0, :], Ss[lo:hi, :, :], start=True, stop=True)
                        mm.then_inc(s_ZS, 1)
                        pe.wait_ge(v_W0, 3)
                        for h, (lo, hi) in enumerate(halves):
                            mm = nc.tensor.matmul(Q[0][lo:hi, 0:C], XX[lo:hi, 0, 1, 0, :], W0[lo:hi, :], start=True, stop=True)
                        mm.then_inc(s_U, 1)
                        for q in range(SB):
                            for h, (lo, hi) in enumerate(halves):
                                nc.tensor.matmul(Q[1][lo:hi, q * SL:(q + 1) * SL], Ss[lo:hi, q, :],
                                                 ZR[lo:hi, 0, 1, q * SL:(q + 1) * SL], start=(q == 0), stop=False,
                                                 skip_group_check=True)
                        pe.wait_ge(v_U, 2)
                        for h, (lo, hi) in enumerate(halves):
                            mm = nc.tensor.matmul(Q[1][lo:hi, 0:NS], UV[:, 0, h, :], M[:, h, 0, C:C + NS], start=False,
                                                  stop=True, skip_group_check=True)
                        mm.then_inc(s_Y, 1)
                        pe.wait_ge(v_b, 2)
                        for h, (lo, hi) in enumerate(halves):
                            mm = nc.tensor.matmul(Q[2][lo:hi, :], BT[:, 0, lo:hi], (eb, enb)[h][:, :], start=True, stop=True)
                        mm.then_inc(s_SU, 1)
                    elif e is not None:
                        bonus()

                @block.scalar
                def _(act):
                    if g is not None:
                        _, m = COLS[g]
                    if e is not None:
                        for i in range(3):
                            scale_previous(act, i)
                        for i, (dst, col) in enumerate([(sg, R_W0), (aa, R_A0)]):
                            act.wait_ge(s_lora, i + 1)
                            nc.scalar.activation(dst[:, 0:n], PJ[i][:, 0:n], ACT.Sigmoid,
                                                 bias=par[:, col:col + 1]).then_inc(a_sig, 1)
                    if g is not None:
                        act.wait_ge(v_yc, 1)
                        nc.scalar.activation(yc[:, 0:m], ysb[g % 2][:, 0:m], ACT.Square).then_inc(a_sq, 1)
                    if e is not None:
                        act.wait_ge(v_mix, MIXED)
                        nc.scalar.activation(t0[:, 0:n], k[:, 0:n], ACT.Square, scale=par[:, R_KK:R_KK + 1]).then_inc(a_kn, 1)
                    if c is not None:
                        for t in range(nT):
                            bank = Q[t] if not sample_c else Q[2 * t]
                            wide = len(grp[0]) * P
                            act.wait_ge(s_tr, t + 1)
                            q0 = grp[t % G][0]
                            if t < G:
                                out = BT[:, q0:q0 + len(grp[0]), :]
                                src = bank[:, 0:wide].rearrange("p (c j) -> p c j", j=P)
                            else:
                                out = UV[:, q0:q0 + len(grp[0]), :, :]
                                src = bank[:, 0:wide].rearrange("p (c h j) -> p c h j", h=2, j=C)
                            nc.scalar.activation(out, src, ACT.Copy).then_inc(a_tb, 1)
                    if g is not None:
                        act.wait_ge(s_var, 1)
                        nc.scalar.activation(rs[:, 0:m], EB[1][:, 0:m], ACT.Ln, scale=1.0 / HK,
                                             bias=eps[:, E_GN:E_GN + 1]).then_inc(a_ln, 1)
                        act.wait_ge(a_ln, 1)
                        nc.scalar.activation(rs[:, 0:m], rs[:, 0:m], ACT.Exp, scale=-0.5).then_inc(a_rs, 1)
                    if c is not None:
                        act.wait_ge(s_wv, 1)
                        nc.scalar.activation(WV[:, 0:nch, :], Q[3][:, 0:nch * C].rearrange("p (c j) -> p c j", j=C),
                                             ACT.Copy).then_inc(a_wv, 1)
                    if e is not None:
                        act.wait_ge(v_cs, 1)
                        nc.scalar.activation(eb[:, 0:n], cs[:, 0:n], ACT.Exp, scale=-DECAY).then_inc(a_exp, 1)
                        nc.scalar.activation(enb[:, 0:n], cs[:, 0:n], ACT.Exp, scale=DECAY).then_inc(a_exp, 1)
                        act.wait_ge(v_cs, 2)
                        nc.scalar.activation(ebm[:, 0:n], sg[:, 0:n], ACT.Exp, scale=-DECAY).then_inc(a_exp, 1)
                        act.wait_ge(v_cl, 1)
                        act.wait_ge(a_sig, 2)
                        nc.scalar.activation(t1[:, 0:n], t1[:, 0:n], ACT.Ln, scale=2.0 ** LN_UP).then_inc(a_kn, 1)
                        nc.scalar.activation(t0[:, 0:n], aa[:, 0:n], ACT.Identity, scale=par[:, R_KA:R_KA + 1],
                                             bias=omm[:, 3:4]).then_inc(a_ka, 1)
                        act.wait_ge(a_kn, 2)
                        nc.scalar.activation(t1[:, 0:n], t1[:, 0:n], ACT.Exp, scale=-0.5,
                                             bias=eps[:, E_UP:E_UP + 1]).then_inc(a_kn, 1)
                    for j in range(len(JOBS)):
                        evacuate(act, j)
                    if step == NB + 1:
                        nc.scalar.activation(lnp[:], par[:, R_LNW:R_LNB + 1], ACT.Copy)
                    if c is not None:
                        cn = COLS[c][1]
                        act.wait_ge(s_Y, 1)
                        nc.scalar.activation(ysb[c % 2][:, 0:cn], Q[1][:, 0:cn], ACT.Copy).then_inc(a_y, 1)

                @block.vector
                def _(dve):
                    def normalise():
                        if g is None:
                            return
                        y = ysb[g % 2][:, 0:m]
                        dve.wait_ge(a_rs, 1)
                        nc.vector.tensor_tensor(y, y, rs[:, 0:m], ALU.mult).then_inc(v_o, 1)
                        dve.wait_ge(v_o, 1)
                        nc.vector.scalar_tensor_tensor(y, y, gn_w, bv[g % 3][:, 0:m], ALU.mult,
                                                       ALU.add).then_inc(v_o, 1)
                        dve.wait_ge(v_o, 2)
                        nc.vector.scalar_tensor_tensor(rs[:, 0:m], y, gn_b, gs[g][:, 0:m], ALU.add,
                                                       ALU.mult).then_inc(v_o, 1)

                    def own(j):
                        if e is None:
                            return
                        if j == 1:
                            dve.wait_ge(s_ssq, 1)
                            nc.vector.tensor_scalar(t1[:, 0:n], EB[0][:, 0:n], 1e-24, None, ALU.max).then_inc(v_cl, 1)
                        if j == 2:
                            dve.wait_ge(a_kn, 3)
                            nc.vector.scalar_tensor_tensor(kkn[:, 0:n], k[:, 0:n], par[:, R_KK:R_KK + 1], t1[:, 0:n],
                                                           ALU.mult, ALU.mult).then_inc(v_kn, 1)
                        if j == 3:
                            dve.wait_ge(a_exp, 3)
                            dve.wait_ge(v_kn, 1)
                            nc.vector.tensor_tensor(ZRe[:, 0:ne, 0, 0:we], ch(kkn), ch(ebm), ALU.mult).then_inc(v_zr, 1)
                            nc.vector.tensor_tensor(ZRe[:, 0:ne, 1, 0:we], ch(r), ch(eb), ALU.mult).then_inc(v_zr, 1)
                        if j == 4:
                            dve.wait_ge(p_kp, 1)
                            dve.wait_ge(v_cl, 1)
                            nc.vector.scalar_tensor_tensor(t2[:, 0:n], r[:, 0:n], par[:, R_RK:R_RK + 1], kp[:, 0:n],
                                                           ALU.mult, ALU.mult).then_inc(v_bp, 1)
                        if j == 5:
                            if c is not None and not sample_e:
                                dve.wait_ge(s_tr, nT)
                            dve.wait_ge(p_ka, 1)
                            for h, (lo, hi) in enumerate(halves):
                                nc.vector.scalar_tensor_tensor(BKe[lo:hi, 0:ne, h, 0:we], ch(aa, lo, hi), -1.0,
                                                               ch(enb, lo, hi), ALU.mult, ALU.mult).then_inc(v_b, 1)
                        if j == 6:
                            dve.wait_ge(s_bon, 1)
                            nc.vector.tensor_tensor(bv[e % 3][:, 0:n], EB[1][:, 0:n], v[:, 0:n], ALU.mult).then_inc(v_bv, 1)

                    def decays():
                        dve.wait_ge(a_sig, 1)
                        rm = cst("resets" if sample_e else "reset")
                        nc.vector.tensor_tensor_scan(cs[:, 0:n], rm, sg[:, 0:n], 0.0, ALU.mult, ALU.add).then_inc(v_cs, 1)
                        dve.wait_ge(v_cs, 1)
                        nc.vector.tensor_tensor(sg[:, 0:n], cs[:, 0:n], sg[:, 0:n], ALU.subtract).then_inc(v_cs, 1)

                    if step == 0:
                        dve.wait_ge(d_p, 32)
                        nc.vector.tensor_scalar(omm[:, 0:3], par[:, 0:3], -1.0, 1.0, ALU.mult, ALU.add)
                        nc.vector.tensor_scalar(omm[:, 3:4], par[:, R_KA:R_KA + 1], -1.0, 1.0, ALU.mult,
                                                ALU.add).then_inc(v_mix, 1)
                        dve.wait_ge(v_mix, 1)
                    if e is not None:
                        for i in range(3):
                            mix(dve, i)
                    if g is not None:
                        _, m = COLS[g]
                        y = ysb[g % 2][:, 0:m]
                        dve.wait_ge(s_mean, 1)
                        nc.vector.scalar_tensor_tensor(y, EB[0][:, 0:m], -1.0 / HK, y, ALU.mult, ALU.add).then_inc(v_yc, 1)
                    if e is not None:
                        decays()
                    if c is not None:
                        for i in range(2 * G):
                            h, chunks = i % 2, grp[i // 2]
                            L = len(chunks)
                            dve.wait_ge(s_A, i + 1)
                            nc.vector.tensor_tensor(M[:, h, chunks[0]:chunks[0] + L, :],
                                                    Q[i][:, 0:L * P].rearrange("p (c j) -> p c j", j=P),
                                                    maskA.unsqueeze(1).to_broadcast([P, L, P]), ALU.mult).then_inc(v_M, 1)
                        dve.wait_ge(v_M, 2 * G)
                        lvl = cst("lvl")
                        for gi, chunks in enumerate(grp):
                            L, q0 = len(chunks), chunks[0]
                            for h, (lo, hi) in enumerate(halves):
                                nc.vector.tensor_tensor(XX[lo:hi, gi, 1, 0:L, :], M[lo:hi, h, q0:q0 + L, 0:C],
                                                        cst("lvl1t")[lo:hi, :].unsqueeze(1).to_broadcast([C, L, C]),
                                                        ALU.mult).then_inc(v_x1, 1)
                            dve.wait_ge(s_T, gi + 1)
                            nc.vector.tensor_tensor(XX[:, gi, 0, 0:L, :], Q[gi][:, 0:L * C].rearrange("p (c j) -> p c j", j=C),
                                                    lvl[:, 0:C].unsqueeze(1).to_broadcast([P, L, C]),
                                                    ALU.mult).then_inc(v_x1, 1)
                            dve.wait_ge(v_x1, 3 * gi + 3)
                            nc.vector.tensor_tensor(XX[:, gi, :, 0:L, :], XX[:, gi, :, 0:L, :],
                                                    ident2.unsqueeze(1).unsqueeze(1).to_broadcast([P, 2, L, C]),
                                                    ALU.add).then_inc(v_X, 1)

                    if c is not None:
                        for l in range(2, levels + 1):
                            for gi, chunks in enumerate(grp):
                                L = len(chunks)
                                dve.wait_ge(s_T, G * (l - 1) + gi + 1)
                                nc.vector.tensor_tensor(T1[:, gi, 0:L, :], Q[gi][:, 0:L * C].rearrange("p (c j) -> p c j", j=C),
                                                        lvl[:, (l - 1) * C:l * C].unsqueeze(1).to_broadcast([P, L, C]),
                                                        ALU.mult).then_inc(v_T, 1)
                            own(l - 2)
                            for gi, chunks in enumerate(grp):
                                L = len(chunks)
                                x0 = 0 if l < levels else 1
                                dve.wait_ge(s_X, G * (l - 2) + gi + 1)
                                pq = Q[2 + gi].rearrange("p (x c j) -> p x c j", x=2, j=C)[:, x0:2, 0:L, :]
                                nc.vector.tensor_tensor(XX[:, gi, x0:2, 0:L, :], pq, XX[:, gi, x0:2, 0:L, :],
                                                        ALU.add).then_inc(v_X, 1)
                            if l == 2:
                                normalise()
                    else:
                        if g is not None:
                            normalise()

                    if c is not None and not sample_c:
                        dve.wait_ge(a_wv, 1)
                        ec = ebC[c % 2]
                        for j in range(NC):
                            dve.wait_ge(s_ZS, j + 1)
                            nc.vector.tensor_tensor(W0[:], Q[0][:, 0:C], WV[:, j, :], ALU.add).then_inc(v_W0, 1)
                            if j:
                                dve.wait_ge(v_S, j)
                            nc.vector.tensor_scalar(Sd[:], S[:], ec[:, j:j + 1], None, ALU.mult).then_inc(v_x1, 1)
                            dve.wait_ge(s_U, j + 1)
                            for h, (lo, hi) in enumerate(halves):
                                nc.vector.tensor_copy(UV[lo:hi, j, h, :], Q[0][lo:hi, C:2 * C]).then_inc(v_U, 1)
                            dve.wait_ge(s_SU, j + 1)
                            dve.wait_ge(v_x1, 3 * G + j + 1)
                            nc.vector.scalar_tensor_tensor(S[:], Q[0][:, 2 * C:3 * C], ec[:, j:j + 1], Sd[:], ALU.mult,
                                                           ALU.add).then_inc(v_S, 1)
                            if j >= 6:
                                own(j - 1)
                    elif sample_c:
                        seq = cst("seq")
                        dve.wait_ge(s_ZS, 1)
                        nc.vector.tensor_tensor(PS[:], Q[0].rearrange("p (s v) -> p s v", v=C),
                                                seq.unsqueeze(2).to_broadcast([P, SB, C]), ALU.mult).then_inc(v_W0, 1)
                        dve.wait_ge(v_W0, 1)
                        nc.vector.tensor_reduce(W0[:], PS[:].rearrange("p s v -> p v s"), mybir.AxisListType.X,
                                                ALU.add).then_inc(v_W0, 1)
                        dve.wait_ge(v_W0, 2)
                        dve.wait_ge(a_wv, 1)
                        nc.vector.tensor_tensor(W0[:], W0[:], WV[:, 0, :], ALU.add).then_inc(v_W0, 1)
                        dve.wait_ge(s_U, 1)
                        for h, (lo, hi) in enumerate(halves):
                            nc.vector.tensor_copy(UV[lo:hi, 0, h, :], Q[0][lo:hi, 0:C]).then_inc(v_U, 1)
                        dve.wait_ge(v_U, 2)
                        for h in range(2):
                            nc.vector.tensor_tensor((eb, enb)[h][:, :].rearrange("p (s v) -> p s v", v=C),
                                                    UV[:, 0, h, :].unsqueeze(1).to_broadcast([P, SB, C]),
                                                    seq.unsqueeze(2).to_broadcast([P, SB, C]), ALU.mult).then_inc(v_b, 1)
                        dve.wait_ge(s_SU, 1)
                        nc.vector.tensor_tensor(Ss[:], Q[2].rearrange("p (s v) -> p s v", v=C), Ss[:], ALU.add).then_inc(v_S, 1)
                        dve.wait_ge(v_S, 1)
                        nc.vector.tensor_tensor(Ss[:], Ss[:], ebC[0][:, :].unsqueeze(2).to_broadcast([P, SB, C]),
                                                ALU.mult).then_inc(v_S, 1)
                    else:
                        for j in range(7):
                            own(j)

                @block.gpsimd
                def _(pool):
                    if step == 0:
                        nc.gpsimd.memset(S[:], 0.0)
                    if e is None:
                        return
                    if sample_e:
                        for i in range(3):
                            nc.gpsimd.memset(raw[i][:, 0:1], 0.0)
                    pool.wait_ge(v_mix, MIXED)
                    if c is not None and not sample_e:
                        pool.wait_ge(s_tr, nT)
                    for h, (lo, hi) in enumerate(halves):
                        nc.gpsimd.tensor_copy(VSe[lo:hi, 0:ne, 1 - h, 0:we], ch(v, lo, hi)).then_inc(p_V, 1)
                        pool.wait_ge(p_V, h + 1)
                    if e == NB - 1 or sample_e:
                        for i in range(3):
                            if not sample_e:
                                nc.gpsimd.tensor_copy(shr[:, i, 0:1], raw[i][:, BLK:BLK + 1]).then_inc(p_sh, 1)
                            else:
                                nc.gpsimd.tensor_copy(shr[:, i, 1:1 + SB], raws[i][:, :, SL:SL + 1].squeeze(2)).then_inc(p_sh, 2)
                    pool.wait_ge(a_exp, 2)
                    last = eb[:, 0:n].rearrange("p (s j) -> p s j", j=SL if sample_e else C)[:, :, -1:].squeeze(2)
                    nc.gpsimd.tensor_copy(ebC[e % 2][:, :], last).then_inc(p_e, 1)
                    pool.wait_ge(a_ka, 1)
                    nc.gpsimd.tensor_tensor(kp[:, 0:n], k[:, 0:n], t0[:, 0:n], ALU.mult).then_inc(p_kp, 1)
                    pool.wait_ge(p_kp, 1)
                    for h, (lo, hi) in enumerate(halves):
                        nc.gpsimd.tensor_tensor(BKe[lo:hi, 0:ne, 1 - h, 0:we], ch(kp, lo, hi), ch(enb, lo, hi),
                                                ALU.mult).then_inc(p_K, 1)
                        pool.wait_ge(p_K, h + 1)
                    pool.wait_ge(v_kn, 1)
                    nc.gpsimd.tensor_tensor(aa[:, 0:n], kkn[:, 0:n], aa[:, 0:n], ALU.mult).then_inc(p_ka, 1)
            rounds_end()

        def gla_stage():
            c1 = ExitStack()
            with c1:
                def sb(name, *shape):
                    return c1.enter_context(nc.sbuf_tensor(name, list(shape), F32))

                B = {
                    "W": sb("gW", P, 6, D), "GD": ysum[0:16, :], "par": sb("gpar", P, 2), "gnp": sb("gnp", P, 1), "GL": sb("GL", 16, P),
                    "q": sb("gq", P, BLK), "k": sb("gk", P, BLK),
                    "QG": [sb(f"QG{i}", P, BLK) for i in range(2)] + [sb("QGs", P, P)],
                    "KG": [sb(f"KG{i}", P, BLK) for i in range(2)] + [sb("KGs", P, P)],
                    "V": [[sb(f"V{i}{h}", P, BLK) for h in range(2)] for i in range(2)] + [[sb(f"Vs{h}", P, P) for h in range(2)]],
                    "gs": [[sb(f"gg{i}{h}", P, BLK) for h in range(2)] for i in range(3)],
                    "x": sb("gx", P, BLK), "la": sb("gla", P, BLK), "cs": sb("gcs", P, BLK),
                    "eb": sb("geb", P, BLK), "enb": sb("genb", P, BLK), "ebC": [sb(f"gebC{i}", P, SB) for i in range(2)],
                    "AT": sb("AT", P, 2, 4, P), "KT": sb("KTt", P, 4, P), "VT": [sb(f"VT{h}", P, 4, P) for h in range(2)],
                    "Sh": sb("Sh", P, NC + 1, P), "Sg": sb("Sg", P, SB, P), "VM": sb("VM", 64, 2, SB, P),
                    "o": [sb(f"osb{h}", P, BLK) for h in range(2)], "sq": [sb(f"osq{h}", P, BLK) for h in range(2)],
                    "rs": [sb(f"ors{h}", P, BLK) for h in range(2)],
                }
                W, GD = B["W"], B["GD"]
                WG = B["AT"][:, :, :, :].rearrange("p h c n -> p (h c n)").unsqueeze(1)
                with nc.Block() as block:
                    @block.sync
                    def _(sp):
                        sp.dma_start(WG[:, 0, :], A["w_even"][1]).then_inc(d_p, 16)
                        sp.dma_start(W[:], A["w_even"][18:24].rearrange("t p n -> p t n")).then_inc(d_w, 16)
                        sp.dma_start(WO0[:], A["w_out_even"][:, 0:KT // 2, :]).then_inc(d_s, 16)
                        sp.dma_start(gno[:], A["norm_odd"]).then_inc(d_o, 16)
                        sp.wait_ge(d_w, 16)
                        sp.wait_ge(d_s, 16)
                        sp.wait_ge(d_o, 16)

                    @block.gpsimd
                    def _(pool):
                        for z in (B["QG"][2], B["KG"][2], *B["V"][2], B["Sg"], B["gnp"], *(x[:, 0:NS] for x in (*B["o"], *B["gs"][NB % 3]))):
                            nc.gpsimd.memset(z[:], 0.0)

                    @block.tensor
                    def _(pe):
                        pe.wait_ge(d_p, 16)
                        for b, (c0, n) in enumerate(COLS):
                            if b >= 2:
                                pe.wait_ge(a_ev, b - 1)
                            project(PJ[b % 2], WG, 0, c0, n, 16).then_inc(s_proj, 1)

                    @block.scalar
                    def _(act):
                        for b, (c0, n) in enumerate(COLS):
                            act.wait_ge(s_proj, b + 1)
                            nc.scalar.activation(GD[:, c0:c0 + n], PJ[b % 2][0:16, 0:n], ACT.Copy).then_inc(a_ev, 1)
                rounds_end()
                with nc.Fori(0, GU) as u:
                    for step in range(NB + 2):
                        gla_step(u, step, B)
                gla_step(GU, NB + 2, B)

        def gla_step(u, step, B):
            W, GD, par, GL, Sh, Sg, AT, KT_, VT, VM = (B[x] for x in ("W", "GD", "par", "GL", "Sh", "Sg", "AT", "KT", "VT", "VM"))
            q, k, x, la, cs, eb, enb, o, sq, rs = (B[y] for y in ("q", "k", "x", "la", "cs", "eb", "enb", "o", "sq", "rs"))
            e = step if step <= NB else None
            c = step - 1 if 1 <= step <= NB + 1 else None
            g = step - 2 if step >= 2 else NB if step == 0 else None
            g_gain = B["gnp"][:, 0:1] if g == NB else par[:, G_NORM:G_NORM + 1]
            g_row = RU + 3 + 2 * u - 2 * (g == NB)
            sample_e, sample_c = e == NB, c == NB
            if e is not None:
                c0, n = COLS[e]
                bi = 2 if sample_e else e % 2
                QGe, KGe, Ve, gse = B["QG"][bi], B["KG"][bi], B["V"][bi], B["gs"][e % 3]
            if c is not None:
                ci = 2 if sample_c else c % 2
                QG, KG, V = B["QG"][ci], B["KG"][ci], B["V"][ci]
                pairs = 1 if sample_c else NC // 2
                wide = pairs * P
                cn = COLS[c][1]
            if g is not None:
                gc0, m = COLS[g]
            halves = [(0, 64), (64, 128)]

            def by_pair(t):
                return t[:, 0:wide].rearrange("p (c j) -> p c j", j=P)

            with nc.Block() as block:
                @block.sync
                def _(sp):
                    if step == 0:
                        sp.dma_start(GL[:], A["gla_up"][:, bass.ds(u * P, P)]).then_inc(d_p, 16)
                        sp.dma_start(par[:], A["gla_par"][bass.ds(u, 1)].rearrange("u p n -> p (u n)")).then_inc(d_p, 16)
                    if step == NB:
                        sp.dma_start(Sg[:], A["gla_in"][bass.ds(u, 1)].rearrange("u p (s v) -> p (u s) v", v=P)).then_inc(d_s, 16)
                        sp.wait_ge(d_s, 16)
                        sp.wait_ge(s_proj, 6)
                        sp.dma_start(W[:], A["w_even"][24:30].rearrange("t p n -> p t n")).then_inc(d_w, 16)
                    if step == NB + 1:
                        sp.dma_start(A["gla_p_out"][bass.ds(u, 1)].rearrange("u p v -> p (u v)"), Sh[:, NC, :]).then_inc(d_o2, 16)
                        sp.wait_ge(d_o2, 16)
                    if g == NB:
                        sp.dma_start(A["gla_s_out"][bass.ds(u, 1)].rearrange("u p (s v) -> p (u s) v", v=P), Sg[:]).then_inc(d_o2, 16)
                        sp.wait_ge(d_o2, 16)
                    if g is not None:
                        for h in range(2):
                            sp.wait_ge(v_o, 2 * h + 2)
                            sp.dma_start(A["O"][bass.ds(g_row + h, 1), :, gc0:gc0 + m].rearrange("u p n -> p (u n)"),
                                         rs[h][:, 0:m]).then_inc(d_o, 16)
                        sp.wait_ge(d_o, 32)
                    if step == NB:
                        sp.wait_ge(d_w, 16)

                @block.tensor
                def _(pe):
                    if e is not None:
                        if step == 0:
                            pe.wait_ge(d_p, 32)
                        nc.tensor.matmul(EB[0][:, 0:n], GL[:, :], GD[:, c0:c0 + n], start=True, stop=True).then_inc(s_lora, 1)
                    if c is not None:
                        for h, (lo, hi) in enumerate(halves):
                            for p in range(pairs):
                                mm = nc.tensor.matmul(Q[h][:, p * P:(p + 1) * P], KG[lo:hi, p * P:(p + 1) * P],
                                                      QG[lo:hi, p * P:(p + 1) * P], start=True, stop=True)
                            mm.then_inc(s_A, 1)
                    if e is not None:
                        project(PJ[0], W, 0, c0, n).then_inc(s_proj, 1)
                    if c is not None:
                        for t, (src, bank) in enumerate(((KG, Q[2]), (V[0], Q[3]), (V[1], Q[0]))):
                            if t == 2:
                                pe.wait_ge(v_M, 1)
                            for p in range(pairs):
                                mm = nc.tensor.transpose(bank[:, p * P:(p + 1) * P], src[:, p * P:(p + 1) * P], ident)
                            mm.then_inc(s_tr, 1)
                    if g is not None:
                        pe.wait_ge(a_sq, 2)
                        nc.tensor.matmul(EB[1][:, 0:m], ones, sq[0][:, 0:m], start=True, stop=True).then_inc(s_ssq, 1)
                        if e is not None:
                            pe.wait_ge(v_g, 1)
                        nc.tensor.matmul(EB[0][:, 0:m], ones, sq[1][:, 0:m], start=True, stop=True).then_inc(s_ssq, 1)
                    if e is not None:
                        project(PJ[1], W, 1, c0, n).then_inc(s_proj, 1)
                    if c is not None:
                        pe.wait_ge(a_tb, 3)
                        pe.wait_ge(v_M, 2)
                        if not sample_c:
                            for par_, bank in enumerate((Q[1], Q[2])):
                                rl, rh = halves[par_]
                                for p in range(pairs):
                                    for h, (lo, hi) in enumerate(halves):
                                        mm = nc.tensor.matmul(bank[lo:hi, p * P:(p + 1) * P], KT_[rl:rh, p, lo:hi],
                                                              VT[h][rl:rh, p, :], start=True, stop=True)
                                mm.then_inc(s_SU, 1)
                        else:
                            pe.wait_ge(v_b, 2)
                            for i, bank in enumerate((Q[1], Q[2])):
                                for h, (lo, hi) in enumerate(halves):
                                    mm = nc.tensor.matmul(bank[lo:hi, :], KT_[0:64, 0, lo:hi], VM[:, h, 4 * i:4 * i + 4, :],
                                                          start=True, stop=True)
                                mm.then_inc(s_SU, 1)
                    if e is not None:
                        for t in (2, 3, 4, 5) if sample_e else (2, 3):
                            pe.wait_ge(a_ev, t - 1)
                            project(PJ[t % 2], W, t, c0, n).then_inc(s_proj, 1)
                    if c is not None:
                        if not sample_c:
                            pe.wait_ge(v_S, 1 + 2 * (NC - 1))
                        for h, (lo, hi) in enumerate(halves):
                            bank = (Q[3], Q[0])[h]
                            if sample_c:
                                nc.tensor.matmul(bank[:, 0:NS], VT[h][:, 0, :], AT[:, h, 0, 0:NS], start=True,
                                                 stop=False, skip_group_check=True)
                                for s_ in range(SB):
                                    a = s_ * SL
                                    mm = nc.tensor.matmul(bank[:, a:a + SL], Sg[lo:hi, s_, :], QG[lo:hi, a:a + SL],
                                                          start=False, stop=True, skip_group_check=True)
                            else:
                                for p in range(pairs):
                                    nc.tensor.matmul(bank[:, p * P:(p + 1) * P], VT[h][:, p, :], AT[:, h, p, :],
                                                     start=True, stop=False, skip_group_check=True)
                                    for j in (2 * p, 2 * p + 1):
                                        mm = nc.tensor.matmul(bank[:, j * C:(j + 1) * C], Sh[lo:hi, j, :], QG[lo:hi, j * C:(j + 1) * C],
                                                              start=False, stop=True, skip_group_check=True)
                            mm.then_inc(s_Y, 1)
                    if e is not None and not sample_e:
                        for t in (4, 5):
                            pe.wait_ge(a_ev, t - 1)
                            project(PJ[t % 2], W, t, c0, n).then_inc(s_proj, 1)

                @block.scalar
                def _(act):
                    def evacuate(t, out, func=ACT.Copy, **kw):
                        act.wait_ge(s_proj, t + 1)
                        nc.scalar.activation(out, PJ[t % 2][:, 0:n], func, **kw).then_inc(a_ev, 1)

                    if g is not None:
                        for h in range(2):
                            nc.scalar.activation(sq[h][:, 0:m], o[h][:, 0:m], ACT.Square).then_inc(a_sq, 1)
                    if e is not None:
                        act.wait_ge(v_g, 2)
                        nc.scalar.activation(la[:, 0:n], la[:, 0:n], ACT.Exp, scale=-1.0).then_inc(a_g, 1)
                        act.wait_ge(a_g, 1)
                        nc.scalar.activation(la[:, 0:n], la[:, 0:n], ACT.Ln, bias=eps[:, E_ONE:E_ONE + 1]).then_inc(a_g, 1)
                        evacuate(0, q[:, 0:n], scale=C ** -0.5)
                    if c is not None:
                        for t, (dst, bank) in enumerate(((KT_, Q[2]), (VT[0], Q[3]), (VT[1], Q[0]))):
                            act.wait_ge(s_tr, t + 1)
                            nc.scalar.activation(dst[:, 0:pairs, :], by_pair(bank), ACT.Copy).then_inc(a_tb, 1)
                    if e is not None:
                        evacuate(1, k[:, 0:n])
                    if g is not None:
                        for h in range(2):
                            act.wait_ge(s_ssq, h + 1)
                            nc.scalar.activation(rs[h][:, 0:m], EB[1 - h][:, 0:m], ACT.Ln, scale=1.0 / P,
                                                 bias=eps[:, E_RMS:E_RMS + 1]).then_inc(a_ln, 1)
                        for h in range(2):
                            act.wait_ge(a_ln, h + 1)
                            nc.scalar.activation(rs[h][:, 0:m], rs[h][:, 0:m], ACT.Exp, scale=-0.5).then_inc(a_rs, 1)
                    if e is not None:
                        act.wait_ge(v_cs, 1)
                        nc.scalar.activation(eb[:, 0:n], cs[:, 0:n], ACT.Exp, scale=1.0 / 16).then_inc(a_exp, 1)
                        nc.scalar.activation(enb[:, 0:n], cs[:, 0:n], ACT.Exp, scale=-1.0 / 16).then_inc(a_exp, 1)
                        for h in range(2):
                            evacuate(2 + h, Ve[h][:, 0:n])
                    if step == NB + 1:
                        nc.scalar.activation(B["gnp"][:], par[:, G_NORM:G_NORM + 1], ACT.Copy)
                    if c is not None:
                        for h in range(2):
                            act.wait_ge(s_Y, h + 1)
                            if g is not None:
                                act.wait_ge(v_o, 2 * h + 1)
                            nc.scalar.activation(o[h][:, 0:cn], (Q[3], Q[0])[h][:, 0:cn], ACT.Copy).then_inc(a_y, 1)
                    if e is not None:
                        for h in range(2):
                            evacuate(4 + h, gse[h][:, 0:n], ACT.Silu)

                @block.vector
                def _(dve):
                    if e is not None:
                        dve.wait_ge(s_lora, 1)
                        if step == 0:
                            dve.wait_ge(d_p, 32)
                        nc.vector.tensor_scalar(x[:, 0:n], EB[0][:, 0:n], par[:, G_GB:G_GB + 1], None, ALU.add).then_inc(v_g, 1)
                        dve.wait_ge(v_g, 1)
                        nc.vector.scalar_tensor_tensor(la[:, 0:n], x[:, 0:n], -1.0, x[:, 0:n], ALU.mult, ALU.max).then_inc(v_g, 1)
                    if c is not None:
                        mg = cst("maskGs" if sample_c else "maskG")
                        for h in range(2):
                            dve.wait_ge(s_A, h + 1)
                            nc.vector.tensor_tensor(AT[:, h, 0:pairs, :], by_pair(Q[h]),
                                                    mg.unsqueeze(1).to_broadcast([P, pairs, P]), ALU.mult).then_inc(v_M, 1)
                    if e is not None:
                        dve.wait_ge(a_g, 2)
                        nc.vector.scalar_tensor_tensor(x[:, 0:n], x[:, 0:n], 0.0, la[:, 0:n], ALU.min, ALU.subtract).then_inc(v_g, 1)
                        dve.wait_ge(v_g, 3)
                        rm = cst("resets" if sample_e else "reset")
                        nc.vector.tensor_tensor_scan(cs[:, 0:n], rm, x[:, 0:n], 0.0, ALU.mult, ALU.add).then_inc(v_cs, 1)
                    if c is not None and not sample_c:
                        if c == 0:
                            nc.vector.memset(Sh[:, 0, :], 0.0).then_inc(v_S, 1)
                        else:
                            nc.vector.tensor_copy(Sh[:, 0, :], Sh[:, NC, :]).then_inc(v_S, 1)
                        ec = B["ebC"][c % 2]
                        dve.wait_ge(s_SU, 2)
                        for j in range(NC):
                            dve.wait_ge(v_S, 1 + 2 * j)
                            nc.vector.tensor_tensor(Sh[:, j + 1, :], Q[1 + j % 2][:, (j // 2) * P:(j // 2 + 1) * P], Sh[:, j, :],
                                                    ALU.add).then_inc(v_S, 1)
                            dve.wait_ge(v_S, 2 + 2 * j)
                            nc.vector.tensor_scalar(Sh[:, j + 1, :], Sh[:, j + 1, :], ec[:, j:j + 1], None, ALU.mult).then_inc(v_S, 1)
                    if sample_c:
                        dve.wait_ge(a_tb, 3)
                        for h in range(2):
                            nc.vector.tensor_tensor(VM[:, h, :, :], VT[h][0:64, 0, :].unsqueeze(1).to_broadcast([64, SB, P]),
                                                    cst("seq")[0:64, :].unsqueeze(2).to_broadcast([64, SB, P]),
                                                    ALU.mult).then_inc(v_b, 1)
                        dve.wait_ge(s_SU, 2)
                        dve.wait_ge(s_Y, 2)
                        for i in range(2):
                            nc.vector.tensor_tensor(Sg[:, 4 * i:4 * i + 4, :], Q[1 + i].rearrange("p (s v) -> p s v", v=P),
                                                    Sg[:, 4 * i:4 * i + 4, :], ALU.add).then_inc(v_x1, 1)
                        dve.wait_ge(v_x1, 2)
                        nc.vector.tensor_tensor(Sg[:], Sg[:], B["ebC"][0][:, :].unsqueeze(2).to_broadcast([P, SB, P]),
                                                ALU.mult).then_inc(v_S, 2)
                    if g is not None:
                        for h in range(2):
                            dve.wait_ge(a_rs, h + 1)
                            nc.vector.tensor_tensor(rs[h][:, 0:m], o[h][:, 0:m], rs[h][:, 0:m], ALU.mult).then_inc(v_o, 1)
                            dve.wait_ge(v_o, 2 * h + 1)
                            nc.vector.scalar_tensor_tensor(rs[h][:, 0:m], rs[h][:, 0:m], g_gain,
                                                           B["gs"][g % 3][h][:, 0:m], ALU.mult, ALU.mult).then_inc(v_o, 1)
                    if e is not None:
                        dve.wait_ge(a_exp, 2)
                        dve.wait_ge(a_ev, 2)
                        nc.vector.tensor_tensor(QGe[:, 0:n], q[:, 0:n], eb[:, 0:n], ALU.mult).then_inc(v_zr, 1)
                        nc.vector.tensor_tensor(KGe[:, 0:n], k[:, 0:n], enb[:, 0:n], ALU.mult).then_inc(v_zr, 1)

                @block.gpsimd
                def _(pool):
                    if e is not None:
                        pool.wait_ge(a_exp, 1)
                        last = eb[:, 0:n].rearrange("p (s j) -> p s j", j=SL if sample_e else C)[:, :, -1:].squeeze(2)
                        nc.gpsimd.tensor_copy(B["ebC"][e % 2][:, :], last).then_inc(p_e, 1)
            rounds_end()

        BANKS = [*Q, *PJ]

        def even_out_stage():
            c1 = ExitStack()
            with c1:
                def sb(name, *shape):
                    return c1.enter_context(nc.sbuf_tensor(name, list(shape), F32))

                ob = [sb(f"ob{i}", P, KT, RB) for i in range(3)]
                xr = [sb(f"xr{i}", P, KT, RB) for i in range(3)]
                rs2 = sb("rs2", P, RB)
                WO1 = sb("WO1", P, KT // 2, D)

                def w_rows(k, t):
                    return (WO0, WO1)[k // (KT // 2)][:, k % (KT // 2), t * P:(t + 1) * P]


                def load_o(sp, b, signals):
                    for to, row, rows_ in ((0, 1, RU), (RU, RU + 3, 2 * GU)):
                        sp.dma_start(ob[b % 3][:, to:to + rows_, :],
                                     A["O"][row:row + rows_, :, b * RB:(b + 1) * RB].rearrange("k p n -> p k n")).then_inc(signals[0], 16)
                    sp.dma_start(xr[b % 3][:], A["xT"][:, :, b * RB:(b + 1) * RB]).then_inc(signals[1], 16)

                for step in range(NRB + 1):
                    e = step if step < NRB else None
                    g = step - 1 if step else None
                    with nc.Block() as block:
                        @block.sync
                        def _(sp):
                            if step == 0:
                                load_o(sp, 0, (d_r, d_g))
                                sp.dma_start(WO1[:], A["w_out_even"][:, KT // 2:, :]).then_inc(d_w, 16)
                            if step + 1 < NRB:
                                load_o(sp, step + 1, d_x)
                            if step == NRB:
                                load_tile0(sp)
                            if g is not None:
                                sp.dma_start(A["X2"][:, :, g * RB:(g + 1) * RB], xr[g % 3][:]).then_inc(d_o, 16)
                            if step + 1 < NRB:
                                sp.wait_ge(d_x[0], 32)
                                sp.wait_ge(d_x[1], 16)
                            if g is not None:
                                sp.wait_ge(d_o, 16)
                            if step == NRB:
                                sp.wait_ge(d_w, 16)
                                sp.wait_ge(d_p, 32)

                        def total(pe):
                            pe.wait_ge(v_cl, 1)
                            nc.tensor.matmul(EB[0][:, 0:RB], ones, ob[g % 3][:, 0, :], start=True, stop=True).then_inc(s_ssum, 1)

                        @block.tensor
                        def _(pe):
                            ahead = len(BANKS) if step == 0 else 0
                            if step == 0:
                                pe.wait_ge(d_r, 32)
                                for t in range(ahead):
                                    for k in range(KT // 2):
                                        nc.tensor.matmul(BANKS[t][:, 0:RB], w_rows(k, t), ob[0][:, k, :], start=(k == 0), stop=False)
                                pe.wait_ge(d_w, 16)
                            for t in range(KT if e is not None else 0):
                                if t >= len(BANKS):
                                    pe.wait_ge(v_mix, t - len(BANKS) + 1)
                                for k in range(KT // 2 if t < ahead else 0, KT):
                                    mm = nc.tensor.matmul(BANKS[t % len(BANKS)][:, 0:RB], w_rows(k, t),
                                                          ob[e % 3][:, k, :], start=(k == 0), stop=(k == KT - 1))
                                mm.then_inc(s_proj, 1)
                                if t == 1 and g is not None:
                                    total(pe)
                            if e is None:
                                total(pe)

                        @block.scalar
                        def _(act):
                            if g is not None:
                                nc.scalar.activation(ob[g % 3][:], xr[g % 3][:], ACT.Square).then_inc(a_sq, 1)
                                act.wait_ge(s_ssum, 1)
                                nc.scalar.activation(rs2[:], EB[0][:, 0:RB], ACT.Ln, scale=1.0 / D,
                                                     bias=eps[:, E_RMS:E_RMS + 1]).then_inc(a_ln, 1)
                                act.wait_ge(a_ln, 1)
                                nc.scalar.activation(rs2[:], rs2[:], ACT.Exp, scale=-0.5).then_inc(a_rs, 1)

                        @block.vector
                        def _(dve):
                            def add(t):
                                dve.wait_ge(s_proj, t + 1)
                                nc.vector.tensor_tensor(xr[e % 3][:, t, :], BANKS[t % len(BANKS)][:, 0:RB], xr[e % 3][:, t, :],
                                                        ALU.add).then_inc(v_mix, 1)

                            if g is not None:
                                sum_tiles(dve, ob[g % 3], 1, v_pr, v_cl)
                            if step == 0:
                                dve.wait_ge(d_g, 16)
                            if e is not None:
                                for t in range(2):
                                    add(t)
                            if g is not None:
                                dve.wait_ge(a_rs, 1)
                                for k in range(KT):
                                    nc.vector.scalar_tensor_tensor(H[:, k, g * RB:(g + 1) * RB], xr[g % 3][:, k, :], gno[:, k:k + 1],
                                                                   rs2[:], ALU.mult, ALU.mult)
                            if e is not None:
                                for t in range(2, KT):
                                    add(t)
                    rounds_end()

        LAST_PE_TAPS = 13

        def conv_stage():
            c1 = ExitStack()
            with c1:
                def sb(name, *shape):
                    return c1.enter_context(nc.sbuf_tensor(name, list(shape), F32))

                B = {
                    "W": [oW0, sb("oW1", P, 3, D)], "par": [opar0, sb("opar1", P, 4)], "cw": [cw0, sb("cw1", P, CW)],
                    "U": [sb(f"U{i}", P, HALO + SEQ) for i in range(2)],
                    "Us": [sb(f"Us{i}", P, SB, HALO + SL) for i in range(2)],
                    "acc": [sb(f"acc{i}", P, T) for i in range(2)], "sg": [sb(f"osg{i}", P, RB) for i in range(2)],
                    "va": [sb(f"ova{i}", P, RB) for i in range(2)], "gt": [sb(f"ogt{i}", P, RB) for i in range(2)],
                    "dg": sb("dg", P, LAST_PE_TAPS, P), "pr": sb("prs", P, CW, NS),
                }

                conv_step(B, 0, None, None, 0, True)
                conv_step(B, 1, 0, None, 1, True)
                with nc.Fori(0, (CT - 2) // 2) as j:
                    conv_step(B, j * 2 + 2, j * 2 + 1, j * 2, 0, False)
                    conv_step(B, j * 2 + 3, j * 2 + 2, j * 2 + 1, 1, False)
                conv_step(B, None, CT - 1, CT - 2, 0, True)
                conv_step(B, None, None, CT - 1, 1, True)

        def conv_step(B, e, c, g, i, static):
            W, par, U, Us = B["W"][i], B["par"][i], B["U"][i], B["Us"][i]
            U2, Us2, cw2, par2 = B["U"][1 - i], B["Us"][1 - i], B["cw"][1 - i], B["par"][1 - i]
            acc, accg, sg, va, gt, dg, pr = B["acc"][1 - i], B["acc"][i], B["sg"], B["va"], B["gt"], B["dg"], B["pr"]
            one = (lambda a, t: a[t:t + 1]) if static else (lambda a, t: a[bass.ds(t, 1)])
            accs = acc[:, SEQ:T]
            RING = [*PJ, *EB]
            BLOCKS = [(b * RB, RB) for b in range(NRB)]
            TAIL = SEQ - (NRB - 1) * RB
            NR = len(RING)
            npe = LAST_PE_TAPS if e is None and c is not None else 0
            nv = CW - npe
            last_e = e is not None and static and e == CT - 1
            with nc.Block() as block:
                @block.sync
                def _(sp):
                    if e is not None:
                        sp.dma_start(Us[:, :, 0:HALO], one(A["conv_in"], e).rearrange("c p s j -> p (c s) j")).then_inc(d_s, 16)
                    if e is None and c is not None:
                        load_last(sp)
                        sp.wait_ge(d_r, 32)
                        sp.wait_ge(d_g, 16)
                    if g is not None:
                        sp.dma_start(one(A["Y"], g).rearrange("c p n -> p (c n)"), accg[:]).then_inc(d_o2, 16)
                    if e is not None and not last_e:
                        sp.dma_start(B["W"][1 - i][:], one(A["w_odd"], e + 1).rearrange("c j p n -> p (c j) n")).then_inc(d_w, 16)
                        if c is not None:
                            sp.wait_ge(v_acc, nv)
                            sp.wait_ge(v_smp, 1)
                        sp.dma_start(B["par"][1 - i][:], one(A["odd_par"], e + 1).rearrange("c p n -> p (c n)")).then_inc(d_p, 16)
                        sp.dma_start(B["cw"][1 - i][:], one(A["conv_w"], e + 1).rearrange("c p n -> p (c n)")).then_inc(d_p, 16)
                        sp.wait_ge(d_w, 16)
                        sp.wait_ge(d_p, 32)
                    if g is not None:
                        sp.wait_ge(d_o2, 16)
                    if e is not None:
                        sp.wait_ge(p_u, NRB + 1)
                        sp.dma_start(one(A["conv_p_out"], e).rearrange("c p n -> p (c n)"), U[:, SEQ:SEQ + HALO]).then_inc(d_x[0], 16)
                        sp.dma_start(one(A["conv_s_out"], e).rearrange("c p s j -> p (c s) j"), Us[:, :, SL:SL + HALO]).then_inc(d_x[0], 16)
                        sp.wait_ge(d_x[0], 32)

                @block.tensor
                def _(pe):
                    for b, (c0, n) in enumerate(BLOCKS):
                        if e is not None:
                            for t in range(3):
                                x = 3 * b + t
                                if x >= NR:
                                    pe.wait_ge(a_ev, x - NR + 1)
                                project(RING[x % NR], W, t, c0, n).then_inc(s_proj, 1)
                    for b in range(NB if npe else 0):
                        if b == 0:
                            pe.wait_ge(a_dg, npe)
                        for d in range(npe):
                            mm = nc.tensor.matmul(Q[b][:, :], dg[:, d, :], U2[:, d + b * BLK:d + (b + 1) * BLK],
                                                  start=(d == 0), stop=(d == npe - 1))
                        mm.then_inc(s_tap, 1)

                @block.scalar
                def _(act):
                    if c is not None:
                        for d in range(npe):
                            nc.scalar.activation(dg[:, d, :], ident, ACT.Copy, scale=cw2[:, d:d + 1]).then_inc(a_dg, 1)
                    if e is None:
                        return
                    for b, (c0, n) in enumerate(BLOCKS):
                        for t, (dst, func) in enumerate(((va, ACT.Identity), (sg, ACT.Sigmoid), (gt, ACT.Silu))):
                            x = 3 * b + t
                            act.wait_ge(s_proj, x + 1)
                            if b >= 2:
                                if t < 2:
                                    act.wait_ge(p_u, b - 1)
                                else:
                                    act.wait_ge(d_sg[b % 2], 16 * (b // 2))
                            nc.scalar.activation(dst[b % 2][:, 0:n], RING[x % NR][:, 0:n], func, bias=par[:, t:t + 1]).then_inc(a_ev, 1)
                        act.wait_ge(a_ev, 3 * b + 3)
                        act.dma_start(one(A["SG"], e)[:, :, c0:c0 + n].rearrange("c p n -> p (c n)"),
                                      gt[b % 2][:, 0:n]).then_inc(d_sg[b % 2], 16)
                    for i_ in range(2):
                        act.wait_ge(d_sg[i_], 16 * len(range(i_, NRB, 2)))

                @block.gpsimd
                def _(pool):
                    if c is None and e is not None:
                        nc.gpsimd.memset(ysum[:], 0.0)
                        for x in B["U"]:
                            nc.gpsimd.memset(x[:, 0:HALO], 0.0)
                    if e is not None:
                        for b, (c0, n) in enumerate(BLOCKS):
                            pool.wait_ge(a_ev, 3 * b + 2)
                            m = n if b < NRB - 1 else TAIL
                            nc.gpsimd.tensor_tensor(U[:, HALO + c0:HALO + c0 + m], va[b % 2][:, 0:m], sg[b % 2][:, 0:m],
                                                    ALU.mult).then_inc(p_u, 1)
                        pool.wait_ge(d_s, 16)
                        nc.gpsimd.tensor_tensor(Us[:, :, HALO:HALO + SL], va[b % 2][:, m:n].rearrange("p (s j) -> p s j", j=SL),
                                                sg[b % 2][:, m:n].rearrange("p (s j) -> p s j", j=SL), ALU.mult).then_inc(p_u, 1)
                    if g is not None:
                        nc.gpsimd.tensor_tensor(ysum[:], ysum[:], accg[:], ALU.add).then_inc(p_ys, 1)

                @block.vector
                def _(dve):
                    if c is None:
                        return
                    for j in range(SL):
                        nc.vector.tensor_tensor(pr[:, :, j * SB:(j + 1) * SB], Us2[:, :, j:j + CW].rearrange("p s d -> p d s"),
                                                cw2[:, :].unsqueeze(2).to_broadcast([P, CW, SB]), ALU.mult).then_inc(v_pr, 1)
                    dve.wait_ge(v_pr, SL)
                    nc.vector.tensor_reduce(accs.rearrange("p (s j) -> p j s", j=SL),
                                            pr[:, :, :].rearrange("p d (j s) -> p j s d", s=SB), mybir.AxisListType.X,
                                            ALU.add).then_inc(v_pr, 1)
                    dve.wait_ge(v_pr, SL + 1)
                    nc.vector.tensor_scalar(accs, accs, par2[:, O_CB:O_CB + 1], None, ALU.add).then_inc(v_smp, 1)
                    for d in range(npe, CW):
                        out, src, w = acc[:, 0:SEQ], U2[:, d:d + SEQ], cw2[:, d:d + 1]
                        if d == npe:
                            nc.vector.tensor_scalar(out, src, w, par2[:, O_CB:O_CB + 1], ALU.mult, ALU.add).then_inc(v_acc, 1)
                        else:
                            dve.wait_ge(v_acc, d - npe)
                            nc.vector.scalar_tensor_tensor(out, src, w, out, ALU.mult, ALU.add).then_inc(v_acc, 1)
                    dve.wait_ge(v_acc, nv)
                    for b in range(NB if npe else 0):
                        dve.wait_ge(s_tap, b + 1)
                        out = acc[:, b * BLK:(b + 1) * BLK]
                        nc.vector.tensor_tensor(out, out, Q[b][:, :], ALU.add).then_inc(v_sum, 1)
            rounds_end()

        def final_stage():
            c1 = ExitStack()
            with c1:
                def sb(name, *shape):
                    return c1.enter_context(nc.sbuf_tensor(name, list(shape), F32))

                sq = sb("fsq", P, KT, RB)
                xr = [sb(f"fx{i}", P, KT, RB) for i in range(4)]
                rsl, rsf = sb("rsl", P, RB), sb("rsf", P, RB)
                lw, lb, fn = sb("lw", P, KT), sb("lb", P, KT), sb("fn", P, KT)

                def rows(a, b):
                    return a[:, :, b * RB:(b + 1) * RB]

                def load_y(sp, b):
                    sp.dma_start(yb[b % 3], A["Y"][:, :, b * RB:(b + 1) * RB].rearrange("k p n -> p k n")).then_inc(d_x[0], 16)
                    sp.dma_start(sgb[b % 2], A["SG"][:, :, b * RB:(b + 1) * RB].rearrange("k p n -> p k n")).then_inc(d_g, 16)

                for step in range(NRB + 3):
                    a = step if step < NRB else None
                    e = step - 1 if 1 <= step <= NRB else None
                    g = step - 2 if 2 <= step <= NRB + 1 else None
                    out = step - 3 if step >= 3 else None
                    with nc.Block() as block:
                        @block.sync
                        def _(sp):
                            if step == 0:
                                sp.dma_start(yb[0], A["Y"][:, :, 0:RB].rearrange("k p n -> p k n")).then_inc(d_s, 16)
                                for dst, name in ((lw, "ln_w"), (lb, "ln_b"), (fn, "final_norm")):
                                    sp.dma_start(dst[:], A[name]).then_inc(d_p, 16)
                            if a is not None:
                                sp.dma_start(xr[a % 4][:], rows(A["X2"], a)).then_inc(d_r, 16)
                            if step + 1 < NRB:
                                load_y(sp, step + 1)
                            if out is not None:
                                sp.dma_start(rows(A["yT"], out), xr[out % 4][:]).then_inc(d_o, 16)
                            if a is not None:
                                sp.wait_ge(d_r, 16)
                            if step + 1 < NRB:
                                sp.wait_ge(d_x[0], 16)
                                sp.wait_ge(d_g, 16)
                            if out is not None:
                                sp.wait_ge(d_o, 16)
                            if step == 0:
                                sp.wait_ge(d_p, 48)

                        def final_total(pe):
                            pe.wait_ge(v_cl, 1)
                            nc.tensor.matmul(BANKS[5][:, 0:RB], ones, sq[:, 0, :], start=True, stop=True).then_inc(s_ssum, 1)

                        def centred_total(pe):
                            pe.wait_ge(v_cl, 1 + (g is not None))
                            nc.tensor.matmul(EB[1][:, 0:RB], ones, sq[:, 0, :], start=True, stop=True).then_inc(s_var, 1)

                        @block.tensor
                        def _(pe):
                            if a is not None:
                                nc.tensor.matmul(EB[0][:, 0:RB], ones, ysum[:, a * RB:(a + 1) * RB], start=True, stop=True).then_inc(s_mean, 1)
                            for t in range(KT if e is not None else 0):
                                if t >= 5:
                                    pe.wait_ge(v_mix, t - 4)
                                for k in range(KT):
                                    mm = nc.tensor.matmul(BANKS[t % 5][:, 0:RB], (WO0, WOF)[k // (KT // 2)][:, k % (KT // 2), t * P:(t + 1) * P], yb[e % 3][:, k, :],
                                                          start=(k == 0), stop=(k == KT - 1))
                                mm.then_inc(s_proj, 1)
                                if t == 1 and g is not None:
                                    final_total(pe)
                                if t == 3 and a is not None:
                                    centred_total(pe)
                            if e is None and g is not None:
                                final_total(pe)
                            if e is None and a is not None:
                                centred_total(pe)

                        @block.scalar
                        def _(act):
                            if g is not None:
                                nc.scalar.activation(sq[:], xr[g % 4][:], ACT.Square).then_inc(a_sq, 1)
                                act.wait_ge(s_ssum, 1)
                                nc.scalar.activation(rsf[:], BANKS[5][:, 0:RB], ACT.Ln, scale=1.0 / D,
                                                     bias=eps[:, E_RMS:E_RMS + 1]).then_inc(a_ln, 1)
                                act.wait_ge(a_ln, 1)
                                nc.scalar.activation(rsf[:], rsf[:], ACT.Exp, scale=-0.5).then_inc(a_rs, 1)
                            if a is not None:
                                n0 = 1 if g is not None else 0
                                act.wait_ge(v_yc, KT)
                                nc.scalar.activation(sq[:], yb[a % 3], ACT.Square).then_inc(a_sq, 1)
                                act.wait_ge(s_var, 1)
                                nc.scalar.activation(rsl[:], EB[1][:, 0:RB], ACT.Ln, scale=1.0 / D,
                                                     bias=eps[:, E_LN:E_LN + 1]).then_inc(a_ln, 1)
                                act.wait_ge(a_ln, n0 + 1)
                                nc.scalar.activation(rsl[:], rsl[:], ACT.Exp, scale=-0.5).then_inc(a_rs, 1)
                                if step == 0:
                                    act.wait_ge(d_p, 48)
                                for k in range(KT):
                                    act.wait_ge(v_kn, k + 1)
                                    nc.scalar.activation(yb[a % 3][:, k, :], yb[a % 3][:, k, :], ACT.Silu, scale=lw[:, k:k + 1],
                                                         bias=lb[:, k:k + 1]).then_inc(a_gl, 1)

                        @block.gpsimd
                        def _(pool):
                            if a is not None:
                                for k in range(KT):
                                    pool.wait_ge(a_gl, k + 1)
                                    nc.gpsimd.tensor_tensor(yb[a % 3][:, k, :], yb[a % 3][:, k, :], sgb[a % 2][:, k, :],
                                                            ALU.mult).then_inc(p_u, 1)

                        @block.vector
                        def _(dve):
                            n0 = 1 if g is not None else 0
                            if step == 0:
                                dve.wait_ge(d_s, 16)
                            if a is not None:
                                dve.wait_ge(s_mean, 1)
                                for k in range(KT):
                                    nc.vector.scalar_tensor_tensor(yb[a % 3][:, k, :], EB[0][:, 0:RB], -1.0 / D, yb[a % 3][:, k, :],
                                                                   ALU.mult, ALU.add).then_inc(v_yc, 1)

                            def add(t):
                                dve.wait_ge(s_proj, t + 1)
                                nc.vector.tensor_tensor(xr[e % 4][:, t, :], BANKS[t % 5][:, 0:RB], xr[e % 4][:, t, :],
                                                        ALU.add).then_inc(v_mix, 1)

                            steps = 0
                            if g is not None:
                                steps = sum_tiles(dve, sq, 1, v_pr, v_cl)
                            if e is not None:
                                for t in range(2):
                                    add(t)
                            if g is not None:
                                dve.wait_ge(a_rs, 1)
                                for k in range(KT):
                                    nc.vector.scalar_tensor_tensor(xr[g % 4][:, k, :], xr[g % 4][:, k, :], fn[:, k:k + 1], rsf[:],
                                                                   ALU.mult, ALU.mult).then_inc(v_o, 1)
                            if a is not None:
                                sum_tiles(dve, sq, n0 + 1, v_pr, v_cl, steps)
                            if e is not None:
                                for t in range(2, 4):
                                    add(t)
                            if a is not None:
                                dve.wait_ge(a_rs, n0 + 1)
                                for k in range(KT):
                                    nc.vector.tensor_tensor(yb[a % 3][:, k, :], yb[a % 3][:, k, :], rsl[:], ALU.mult).then_inc(v_kn, 1)
                            if e is not None:
                                for t in range(4, KT):
                                    add(t)
                    rounds_end()

        rwkv_stage()
        WO0 = ctx.enter_context(nc.sbuf_tensor("WO0", [P, KT // 2, D], F32))
        gno = ctx.enter_context(nc.sbuf_tensor("gno", [P, KT], F32))
        gla_stage()
        oW0, opar0, cw0 = (ctx.enter_context(nc.sbuf_tensor(name, [P, *shape], F32))
                           for name, shape in (("oW0", (3, D)), ("opar0", (4,)), ("cw0", (CW,))))

        def load_tile0(sp):
            sp.dma_start(oW0[:], A["w_odd"][0:1].rearrange("c j p n -> p (c j) n")).then_inc(d_w, 16)
            sp.dma_start(opar0[:], A["odd_par"][0]).then_inc(d_p, 16)
            sp.dma_start(cw0[:], A["conv_w"][0]).then_inc(d_p, 16)

        even_out_stage()
        WOF = ctx.enter_context(nc.sbuf_tensor("WOF", [P, KT // 2, D], F32))
        parts_of_H = [H[:, :, i * RB:(i + 1) * RB] for i in range(NRB)]
        yb, sgb = parts_of_H[:3], parts_of_H[3:5]

        def load_last(sp):
            sp.dma_start(WO0[:], A["w_out_odd"][:, 0:KT // 2, :]).then_inc(d_r, 16)
            sp.dma_start(WOF[:], A["w_out_odd"][:, KT // 2:, :]).then_inc(d_r, 16)
            sp.dma_start(sgb[0], A["SG"][:, :, 0:RB].rearrange("k p n -> p k n")).then_inc(d_g, 16)

        conv_stage()
        final_stage()




def constants():
    K = np.zeros((P, NCONST), np.float32)

    def put(name, x):
        a, b = _COLS[name]
        K[:, a:b] = x

    s, t = np.arange(P)[:, None] % C, np.arange(C)[None, :]
    live = (s < NS) & (t < NS) & (s // SL == t // SL)
    put("maskA", np.concatenate([s < t, s <= t], 1))
    put("maskAs", np.concatenate([(s < t) & live, (s <= t) & live], 1))
    lv = [((s >> l) == (t >> l)) & (((s >> (l - 1)) & 1) == 1) & (((t >> (l - 1)) & 1) == 0) for l in range(1, 7)]
    put("lvl", np.concatenate(lv, 1))
    put("lvl1t", ((s >> 1) == (t >> 1)) & (s < t))
    put("ident", np.eye(P))
    put("ident2", s == t)
    r, c = np.arange(P)[:, None], np.arange(P)[None, :]
    put("bones", r // C == c // C)
    put("ones", 1.0)
    put("reset", (np.arange(BLK) % C != 0)[None, :])
    put("resets", (np.arange(NS) % SL != 0)[None, :])
    put("seq", (s < NS) & (s // SL == np.arange(SB)[None, :]))
    put("maskG", (r // C == c // C) & (r <= c))
    put("maskGs", (r < NS) & (c < NS) & (r // SL == c // SL) & (r <= c))
    e = np.zeros((P, 8))
    e[:, E_RMS], e[:, E_GN], e[:, E_LN], e[:, E_UP], e[:, E_ONE] = RMS_EPS, GN_EPS, LN_EPS, 0.5 * LN_UP * math.log(2), 1.0
    put("eps", e)
    return K


def kernel(**inputs):
    import concourse.bacc as bacc
    from concourse.bass_utils import run_bass_kernel_spmd as run

    I = {k: np.asarray(v) for k, v in inputs.items()}

    def tiles(x):
        return x.reshape(KT, P, -1).transpose(1, 0, 2)

    def col(x):
        return x.reshape(-1, P).T

    def pad_row(x):
        return np.concatenate([x, np.zeros_like(x[:1])], 0)

    x = np.concatenate([I["x_prompt"].reshape(SEQ, D), I["x_sample"].reshape(NS, D)], 0)
    w = I["w_in_even"][0]
    G0, S0 = RPROJ, RPROJ + GPROJ
    cols = [(3 * 512, P), (G0 + 1024, 16)]
    for u in range(RU):
        cols += [(u * P, P), (512 + u * P, P), (1024 + u * P, P), (S0 + u * P, P)]
    for g in range(GU):
        cols += [(G0 + g * P, P), (G0 + 256 + g * P, P), (G0 + 512 + 2 * g * P, P), (G0 + 512 + (2 * g + 1) * P, P),
                 (S0 + (4 + 2 * g) * P, P), (S0 + (5 + 2 * g) * P, P)]
    w_even = np.zeros((len(cols), P, KT, P), np.float32)
    for i, (a, n) in enumerate(cols):
        w_even[i, :, :, :n] = tiles(w[:, a:a + n])
    mu = I["rwkv_mu"][0]
    par = [mu[0:512], mu[512:1024], mu[1024:1536], I["rwkv_w0"][0], I["rwkv_a0"][0], I["rwkv_k_k"][0],
           I["rwkv_k_a"][0], I["rwkv_r_k"][0].reshape(-1), I["rwkv_ln_w"][0], I["rwkv_ln_b"][0]]
    shift = I["state_rwkv_shift"][0]
    order = [a + u * P for u in range(RU) for a in (0, 512, 1024)] + [3 * 512]
    wo = I["w_in_odd"][0]
    w_odd = np.stack([np.stack([tiles(wo[:, j * D + c * P:j * D + (c + 1) * P]) for j in range(3)]) for c in range(CT)])
    b3 = I["b_in_odd"][0].reshape(3, CT, P)
    arrays = {
        "const": constants(),
        "xT": x.T.reshape(KT, P, T).transpose(1, 0, 2),
        "norm_even": col(I["norm_even"][0]),
        "w_even": w_even.reshape(len(cols), P, KT * P),
        "mu_lora": mu[1536:1664].reshape(P, 1),
        "rwkv_par": np.stack([p.reshape(RU, P) for p in par], -1),
        "lora_up": np.concatenate([I["rwkv_w_up"][0], I["rwkv_a_up"][0]], 0),
        "shift_in": np.stack([shift[:, a:a + P].T for a in order]),
        "rwkv_in": I["state_rwkv"][0].reshape(SB, RU, 2, C, C).transpose(1, 2, 4, 0, 3).reshape(RU, P, SB * C),
        "gla_in": I["state_gla"][0].reshape(SB, GU, 2, C, P).transpose(1, 2, 3, 0, 4).reshape(GU, P, SB * P),
        "gla_up": I["gla_g_up"][0],
        "gla_par": np.stack([I["gla_g_b"][0].reshape(GU, P), np.broadcast_to(I["gla_norm"][0], (GU, P))], -1),
        "w_out_even": tiles(I["w_out_even"][0]),
        "norm_odd": col(I["norm_odd"][0]),
        "w_odd": pad_row(w_odd.reshape(CT, 3, P, KT * P)),
        "odd_par": pad_row(np.stack([b3[0], b3[1], b3[2], I["conv_b"][0].reshape(CT, P)], -1)),
        "conv_w": pad_row(I["conv_w"][0].reshape(CW, CT, P).transpose(1, 2, 0)),
        "conv_in": I["cache_conv"][0].reshape(SB, HALO, CT, P).transpose(2, 3, 0, 1),
        "ln_w": col(I["conv_ln_w"][0]),
        "ln_b": col(I["conv_ln_b"][0]),
        "w_out_odd": tiles(I["w_out_odd"][0]),
        "final_norm": col(I["final_norm"]),
    }
    outs = {
        "yT": (P, KT, T), "shift_out": (13, P, 1 + SB), "rwkv_p_out": (RU, P, C), "rwkv_s_out": (RU + 1, P, SB * C),
        "gla_p_out": (GU, P, P), "gla_s_out": (GU + 1, P, SB * P), "conv_p_out": (CT, P, HALO),
        "conv_s_out": (CT, P, SB, HALO),
    }
    scratch = {"O": (KT + 3, P, T), "X2": (P, KT, T), "SG": (CT, P, T), "Y": (CT, P, T)}
    nc = bacc.Bacc("TRN2", target_bir_lowering=False, num_devices=1)
    A = {}
    for name, a in arrays.items():
        arrays[name] = a = np.ascontiguousarray(a)
        A[name] = nc.dram_tensor("in_" + name, a.shape, F32, kind="ExternalInput").ap()
    for name, shape in outs.items():
        A[name] = nc.dram_tensor("out_" + name, shape, F32, kind="ExternalOutput").ap()
    for name, shape in scratch.items():
        A[name] = nc.dram_tensor("tmp_" + name, shape, F32, kind="Internal").ap()
    build(nc, A)
    res = run(nc, [{"in_" + k: v for k, v in arrays.items()}], core_ids=[0]).results[0]
    R = {k: np.asarray(res["out_" + k]) for k in outs}
    y = R["yT"].transpose(1, 0, 2).reshape(D, T).T
    sh = np.zeros((1 + SB, RPROJ), np.float32)
    for i, a in enumerate(order):
        sh[:, a:a + P] = R["shift_out"][i].T
    rp = R["rwkv_p_out"].reshape(RU, 2, C, C).transpose(0, 1, 3, 2).reshape(1, 1, 8, C, C)
    rsmp = R["rwkv_s_out"][1:].reshape(RU, 2, C, SB, C).transpose(3, 0, 1, 4, 2).reshape(1, SB, 8, C, C)
    gp = R["gla_p_out"].reshape(1, 1, 4, C, P)
    gsmp = R["gla_s_out"][1:].reshape(GU, 2, C, SB, P).transpose(3, 0, 1, 2, 4).reshape(1, SB, 4, C, P)
    cp = R["conv_p_out"].transpose(2, 0, 1).reshape(1, 1, HALO, D)
    csmp = R["conv_s_out"].transpose(2, 3, 0, 1).reshape(1, SB, HALO, D)
    return (y[:SEQ].reshape(1, SEQ, D).copy(), y[SEQ:].reshape(SB, SL, D).copy(), sh[0:1].reshape(1, 1, RPROJ).copy(),
            sh[1:].reshape(1, SB, RPROJ).copy(), rp.copy(), rsmp.copy(), gp.copy(), gsmp.copy(), cp.copy(), csmp.copy())
```
